# Optimizing a Trainium2 kernel written in Bass

```python
import jax, jax.numpy as jnp
from jax import lax
import numpy as np

D_MODEL = 1024
BATCH = 1
SEQ = 512
DEPTH = 2

HEAD_DIM = 64
N_FOX_HEADS = 8
N_NSA_HEADS = 8
N_NSA_KV = 2
NSA_GROUP = N_NSA_HEADS // N_NSA_KV
CMP_LEN = 32
CMP_STRIDE = 16
SLC_LEN = 64
SLC_TOPK = 16
WINDOW = 512
Q_BLOCK = 128
FORCE_BONUS = 1.0e4
NEG = -1.0e30
ATTN_WIDTH = (N_FOX_HEADS + N_NSA_HEADS) * HEAD_DIM
FOX_QKV = 3 * N_FOX_HEADS * HEAD_DIM
FOX_F = N_FOX_HEADS
NSA_Q = N_NSA_HEADS * HEAD_DIM
NSA_KV = 6 * N_NSA_KV * HEAD_DIM
NSA_GATES = 3 * N_NSA_HEADS
EVEN_IN = FOX_QKV + FOX_F + NSA_Q + NSA_KV + NSA_GATES

D_RNN = 1280
RNN_BLOCKS = 10
RNN_BLOCK_W = D_RNN // RNN_BLOCKS
CONV_W = 4
LRU_C = 8.0

PEER_HEADS = 8
PEER_NKEYS = 128
PEER_NEXP = PEER_NKEYS * PEER_NKEYS
PEER_DKEY = 256
PEER_HALF = PEER_DKEY // 2
PEER_TOPK = 16
TOKEN_BLOCK = 128

RMS_EPS = 1e-6

kernel_name = 'fox_nsa_rglru_peer_hybrid'

def rmsnorm(x, g):
    xf = x.astype(jnp.float32)
    y = xf * lax.rsqrt(jnp.mean(xf * xf, axis=-1, keepdims=True) + RMS_EPS)
    return (y * g.astype(jnp.float32)).astype(x.dtype)

def alibi_slopes(n):
    return jnp.asarray(2.0 ** (-8.0 * np.arange(1, n + 1) / n), jnp.float32)

def masked_softmax(s, mask):
    return jax.nn.softmax(jnp.where(mask, s, NEG), axis=-1)

def fox_attention(q, k, v, logf):
    B, S, H, dh = q.shape
    cT = jnp.cumsum(logf, axis=1).transpose(0, 2, 1)
    qs = q * (dh ** -0.5)
    kpos = jnp.arange(S)

    def block(i):
        t0 = i * Q_BLOCK
        tpos = t0 + jnp.arange(Q_BLOCK)
        qb = lax.dynamic_slice_in_dim(qs, t0, Q_BLOCK, axis=1)
        cb = lax.dynamic_slice_in_dim(cT, t0, Q_BLOCK, axis=2)
        s = jnp.einsum('bthd,bshd->bhts', qb, k) + cb[..., None] - cT[:, :, None, :]
        p = masked_softmax(s, kpos[None, :] <= tpos[:, None])
        return jnp.einsum('bhts,bshd->bthd', p, v)

    out = lax.map(block, jnp.arange(S // Q_BLOCK))
    return out.swapaxes(0, 1).reshape(B, S, H * dh)

def nsa_attention(q, k_cmp, v_cmp, k_slc, v_slc, k_win, v_win, gates, cmp_pos, w_cmp_k, w_cmp_v):
    B, S, H, dh = q.shape
    G, R = N_NSA_KV, NSA_GROUP
    f32 = jnp.float32
    n_cmp = (S - CMP_LEN) // CMP_STRIDE + 1
    n_sel = S // SLC_LEN
    k_sel = min(SLC_TOPK, n_sel)
    slopes = alibi_slopes(H).reshape(G, R)
    cstart = CMP_STRIDE * np.arange(n_cmp)
    cidx = cstart[:, None] + np.arange(CMP_LEN)[None, :]
    kc = jnp.einsum('bnlgd,lde->bnge', k_cmp[:, cidx] + cmp_pos[:, None, :], w_cmp_k)
    vc = jnp.einsum('bnlgd,lde->bnge', v_cmp[:, cidx] + cmp_pos[:, None, :], w_cmp_v)
    cend = jnp.asarray(cstart + CMP_LEN - 1, jnp.int32)
    sstart = SLC_LEN * np.arange(n_sel)
    overlap = jnp.asarray((cstart[:, None] < sstart[None, :] + SLC_LEN)
                          & (cstart[:, None] + CMP_LEN > sstart[None, :]), f32)
    ks = k_slc.reshape(B, n_sel, SLC_LEN, G, dh).transpose(0, 3, 1, 2, 4)
    vs = v_slc.reshape(B, n_sel, SLC_LEN, G, dh).transpose(0, 3, 1, 2, 4)
    kw_pad = jnp.pad(k_win, ((0, 0), (WINDOW, 0), (0, 0), (0, 0)))
    vw_pad = jnp.pad(v_win, ((0, 0), (WINDOW, 0), (0, 0), (0, 0)))
    qg = q.reshape(B, S, G, R, dh) * (dh ** -0.5)
    gg = gates.reshape(B, S, G, R, 3)
    jpos = jnp.arange(n_sel)
    gather_blocks = jax.vmap(jax.vmap(lambda tab, ix: tab[ix]))
    M = k_sel * SLC_LEN

    def block(i):
        t0 = i * Q_BLOCK
        tpos = t0 + jnp.arange(Q_BLOCK)
        qb = lax.dynamic_slice_in_dim(qg, t0, Q_BLOCK, axis=1)
        gb = lax.dynamic_slice_in_dim(gg, t0, Q_BLOCK, axis=1)
        cmask = cend[None, :] <= tpos[:, None]
        s_c = (jnp.einsum('btgrd,bngd->bgrtn', qb, kc)
               - slopes[:, :, None, None] * (tpos[:, None] - cend[None, :]).astype(f32))
        p_c = masked_softmax(s_c, cmask) * jnp.any(cmask, axis=-1)[:, None].astype(f32)
        o_c = jnp.einsum('bgrtn,bngd->btgrd', p_c, vc)
        imp = jnp.einsum('bgrtn,nj->bgtj', p_c, overlap)
        cur = tpos // SLC_LEN
        forced = ((jpos[None, :] == 0) | (jpos[None, :] == cur[:, None])
                  | (jpos[None, :] == cur[:, None] - 1))
        imp = jnp.where(jpos[None, :] <= cur[:, None], imp + FORCE_BONUS * forced.astype(f32), -jnp.inf)
        _, sel = lax.top_k(imp, k_sel)
        gk = gather_blocks(ks, sel).reshape(B, G, Q_BLOCK, M, dh)
        gv = gather_blocks(vs, sel).reshape(B, G, Q_BLOCK, M, dh)
        spos = (sel[..., None] * SLC_LEN + jnp.arange(SLC_LEN)).reshape(B, G, Q_BLOCK, M)
        sdist = (tpos[:, None] - spos).astype(f32)
        s_s = (jnp.einsum('btgrd,bgtmd->bgrtm', qb, gk)
               - slopes[None, :, :, None, None] * sdist[:, :, None])
        p_s = masked_softmax(s_s, (sdist >= 0)[:, :, None])
        o_s = jnp.einsum('bgrtm,bgtmd->btgrd', p_s, gv)
        kw = lax.dynamic_slice_in_dim(kw_pad, t0, Q_BLOCK + WINDOW, axis=1)
        vw = lax.dynamic_slice_in_dim(vw_pad, t0, Q_BLOCK + WINDOW, axis=1)
        wpos = t0 - WINDOW + jnp.arange(Q_BLOCK + WINDOW)
        wdist = tpos[:, None] - wpos[None, :]
        wmask = (wdist >= 0) & (wdist < WINDOW) & (wpos[None, :] >= 0)
        s_w = (jnp.einsum('btgrd,bsgd->bgrts', qb, kw)
               - slopes[:, :, None, None] * wdist.astype(f32))
        o_w = jnp.einsum('bgrts,bsgd->btgrd', masked_softmax(s_w, wmask), vw)
        return gb[..., 0:1] * o_c + gb[..., 1:2] * o_s + gb[..., 2:3] * o_w

    out = lax.map(block, jnp.arange(S // Q_BLOCK))
    return out.swapaxes(0, 1).reshape(B, S, H * dh)

def even_mixer(h, w_in, b_f, cmp_pos, w_cmp_k, w_cmp_v, w_out):
    B, S, _ = h.shape
    z = jnp.einsum('bsd,de->bse', h, w_in).astype(jnp.float32)
    splits = [int(v) for v in np.cumsum([FOX_QKV, FOX_F, NSA_Q, NSA_KV])]
    fox_qkv, fox_f, nsa_q, nsa_kv, nsa_g = jnp.split(z, splits, axis=-1)
    fqkv = fox_qkv.reshape(B, S, 3, N_FOX_HEADS, HEAD_DIM)
    logf = jax.nn.log_sigmoid(fox_f + b_f.astype(jnp.float32))
    o_fox = fox_attention(fqkv[:, :, 0], fqkv[:, :, 1], fqkv[:, :, 2], logf)
    kv = nsa_kv.reshape(B, S, 6, N_NSA_KV, HEAD_DIM)
    gates = jax.nn.sigmoid(nsa_g).reshape(B, S, N_NSA_HEADS, 3)
    o_nsa = nsa_attention(nsa_q.reshape(B, S, N_NSA_HEADS, HEAD_DIM),
                          kv[:, :, 0], kv[:, :, 1], kv[:, :, 2], kv[:, :, 3], kv[:, :, 4], kv[:, :, 5],
                          gates, cmp_pos.astype(jnp.float32), w_cmp_k.astype(jnp.float32),
                          w_cmp_v.astype(jnp.float32))
    o = jnp.concatenate([o_fox, o_nsa], axis=-1)
    return jnp.einsum('bse,ed->bsd', o, w_out.astype(jnp.float32)).astype(h.dtype)

def rg_lru(x, w_ra, b_ra, w_ri, b_ri, lam):
    B, S, C = x.shape
    f32 = jnp.float32
    xf = x.astype(f32)
    xb = xf.reshape(B, S, RNN_BLOCKS, RNN_BLOCK_W)
    r = jax.nn.sigmoid(jnp.einsum('bsnc,nce->bsne', xb, w_ra.astype(f32)).reshape(B, S, C) + b_ra.astype(f32))
    i = jax.nn.sigmoid(jnp.einsum('bsnc,nce->bsne', xb, w_ri.astype(f32)).reshape(B, S, C) + b_ri.astype(f32))
    log_a = -LRU_C * r * jax.nn.softplus(-lam.astype(f32))
    a = jnp.exp(log_a)
    u = jnp.sqrt(-jnp.expm1(2.0 * log_a)) * (i * xf)

    def combine(left, right):
        a1, b1 = left
        a2, b2 = right
        return a1 * a2, a2 * b1 + b2

    _, hs = lax.associative_scan(combine, (a, u), axis=1)
    return hs

def odd_mixer(h, w_in, conv_w, conv_b, w_ra, b_ra, w_ri, b_ri, lam, w_out):
    z = jnp.einsum('bsd,de->bse', h, w_in)
    gate, xr = jnp.split(z, 2, axis=-1)
    xr = lax.conv_general_dilated(xr, conv_w[:, None, :].astype(xr.dtype), window_strides=(1,),
                                  padding=((CONV_W - 1, 0),),
                                  dimension_numbers=('NWC', 'WIO', 'NWC'),
                                  feature_group_count=D_RNN) + conv_b.astype(xr.dtype)
    y = rg_lru(xr, w_ra, b_ra, w_ri, b_ri, lam)
    y = jax.nn.gelu(gate.astype(jnp.float32), approximate=False) * y
    return jnp.einsum('bse,ed->bsd', y, w_out.astype(jnp.float32)).astype(h.dtype)

def peer_ffn(h, w_q, sub_keys, u_tab, v_tab):
    B, S, D = h.shape
    K = PEER_TOPK
    q = jnp.einsum('bsd,de->bse', h, w_q).astype(jnp.float32).reshape(B, S, PEER_HEADS, 2, PEER_HALF)
    s = jnp.einsum('bshcd,hckd->bshck', q, sub_keys.astype(jnp.float32))
    top_s, top_i = lax.top_k(s, K)
    cand = (top_s[..., 0, :, None] + top_s[..., 1, None, :]).reshape(B, S, PEER_HEADS, K * K)
    best_s, best_c = lax.top_k(cand, K)
    i1 = jnp.take_along_axis(top_i[..., 0, :], best_c // K, axis=-1)
    i2 = jnp.take_along_axis(top_i[..., 1, :], best_c % K, axis=-1)
    ids = i1 * PEER_NKEYS + i2
    g = jax.nn.softmax(best_s, axis=-1)
    nb = S // TOKEN_BLOCK

    def to_blocks(a):
        return a.reshape(B, nb, TOKEN_BLOCK, *a.shape[2:]).swapaxes(0, 1)

    def block(args):
        xb, idb, gb = args
        act = jax.nn.gelu(jnp.einsum('btd,bthkd->bthk', xb, u_tab[idb]).astype(jnp.float32),
                          approximate=False)
        w = (gb * act).astype(v_tab.dtype)
        return jnp.einsum('bthk,bthkd->btd', w, v_tab[idb])

    out = lax.map(block, (to_blocks(h), to_blocks(ids), to_blocks(g)))
    return out.swapaxes(0, 1).reshape(B, S, D).astype(h.dtype)

def setup_inputs(seed: int = 0) -> dict:
    key = jax.random.key(seed)
    ks = jax.random.split(key, 32)
    f32 = jnp.float32
    n_even = (DEPTH + 1) // 2
    n_odd = DEPTH // 2

    def nrm(k, shape, scale):
        return scale * jax.random.normal(k, shape, f32)

    def gain(k, shape):
        return 1.0 + 0.02 * jax.random.normal(k, shape, f32)

    a0 = jax.random.uniform(ks[16], (n_odd, D_RNN), f32, 0.9, 0.999)
    return {
        'x': nrm(ks[0], (BATCH, SEQ, D_MODEL), 1.0),
        'even_norm_g': gain(ks[1], (n_even, D_MODEL)),
        'even_w_in': nrm(ks[2], (n_even, D_MODEL, EVEN_IN), D_MODEL ** -0.5),
        'even_b_f': 3.0 + nrm(ks[3], (n_even, N_FOX_HEADS), 0.5),
        'even_cmp_pos': nrm(ks[4], (n_even, CMP_LEN, HEAD_DIM), 0.1),
        'even_w_cmp_k': nrm(ks[5], (n_even, CMP_LEN, HEAD_DIM, HEAD_DIM), (CMP_LEN * HEAD_DIM) ** -0.5),
        'even_w_cmp_v': nrm(ks[6], (n_even, CMP_LEN, HEAD_DIM, HEAD_DIM), (CMP_LEN * HEAD_DIM) ** -0.5),
        'even_w_out': nrm(ks[7], (n_even, ATTN_WIDTH, D_MODEL), ATTN_WIDTH ** -0.5),
        'odd_norm_g': gain(ks[8], (n_odd, D_MODEL)),
        'odd_w_in': nrm(ks[9], (n_odd, D_MODEL, 2 * D_RNN), D_MODEL ** -0.5),
        'odd_conv_w': nrm(ks[10], (n_odd, CONV_W, D_RNN), CONV_W ** -0.5),
        'odd_conv_b': nrm(ks[11], (n_odd, D_RNN), 0.01),
        'odd_w_ra': nrm(ks[12], (n_odd, RNN_BLOCKS, RNN_BLOCK_W, RNN_BLOCK_W), RNN_BLOCK_W ** -0.5),
        'odd_b_ra': nrm(ks[13], (n_odd, D_RNN), 0.01),
        'odd_w_ri': nrm(ks[14], (n_odd, RNN_BLOCKS, RNN_BLOCK_W, RNN_BLOCK_W), RNN_BLOCK_W ** -0.5),
        'odd_b_ri': nrm(ks[15], (n_odd, D_RNN), 0.01),
        'odd_lam': jnp.log(a0) - jnp.log1p(-a0),
        'odd_w_out': nrm(ks[17], (n_odd, D_RNN, D_MODEL), D_RNN ** -0.5),
        'ffn_norm_g': gain(ks[18], (DEPTH, D_MODEL)),
        'peer_w_q': nrm(ks[19], (DEPTH, D_MODEL, PEER_HEADS * PEER_DKEY), D_MODEL ** -0.5),
        'peer_sub_keys': nrm(ks[20], (DEPTH, PEER_HEADS, 2, PEER_NKEYS, PEER_HALF), PEER_HALF ** -0.5),
        'peer_u': nrm(ks[21], (DEPTH, PEER_NEXP, D_MODEL), D_MODEL ** -0.5),
        'peer_v': nrm(ks[22], (DEPTH, PEER_NEXP, D_MODEL), PEER_HEADS ** -0.5),
        'final_g': gain(ks[23], (D_MODEL,)),
    }

def reference(x, even_norm_g, even_w_in, even_b_f, even_cmp_pos, even_w_cmp_k, even_w_cmp_v, even_w_out,
              odd_norm_g, odd_w_in, odd_conv_w, odd_conv_b, odd_w_ra, odd_b_ra, odd_w_ri, odd_b_ri,
              odd_lam, odd_w_out, ffn_norm_g, peer_w_q, peer_sub_keys, peer_u, peer_v, final_g):
    h = x
    for layer in range(DEPTH):
        j = layer // 2
        if layer % 2 == 0:
            h = h + even_mixer(rmsnorm(h, even_norm_g[j]), even_w_in[j], even_b_f[j], even_cmp_pos[j],
                               even_w_cmp_k[j], even_w_cmp_v[j], even_w_out[j])
        else:
            h = h + odd_mixer(rmsnorm(h, odd_norm_g[j]), odd_w_in[j], odd_conv_w[j], odd_conv_b[j],
                              odd_w_ra[j], odd_b_ra[j], odd_w_ri[j], odd_b_ri[j], odd_lam[j], odd_w_out[j])
        h = h + peer_ffn(rmsnorm(h, ffn_norm_g[layer]), peer_w_q[layer], peer_sub_keys[layer],
                         peer_u[layer], peer_v[layer])
    return rmsnorm(h, final_g)


_drawn_inputs = setup_inputs


def setup_inputs(seed=0):
    import zlib

    import numpy as np

    out = dict(_drawn_inputs(seed))
    spreads = {}
    factors = {'odd_norm_g': 2.891,
     'odd_conv_b': 2.761,
     'odd_b_ra': 31.197,
     'odd_b_ri': 23.256,
     'final_g': 8.4}
    for name, (base, spread) in spreads.items():
        noise = np.random.default_rng([zlib.crc32(name.encode()), seed]).standard_normal(out[name].shape)
        drawn = base * np.exp(spread * noise) if base else spread * noise
        out[name] = __import__('jax').numpy.asarray(drawn.astype(out[name].dtype))
    for name, factor in factors.items():
        out[name] = (out[name] * factor).astype(out[name].dtype)
    return out
```

```python
from contextlib import ExitStack

import concourse.bass as bass
from concourse import mybir

ALU = mybir.AluOpType
ACT = mybir.ActivationFunctionType
X = mybir.AxisListType.X
F32 = mybir.dt.float32
F32R = mybir.dt.float32r
F16 = mybir.dt.float16
U32 = mybir.dt.uint32

P = 128
SEQ = 512
TT = SEQ // P
D = 1024
KD = D // P
EPS = 1e-6
NEG = -1.0e30
BIG = 3.0e38

DH = 64
NH = 8
GROUPS = 2
CMP_LEN = 32
CMP_STRIDE = 16
N_CMP = (SEQ - CMP_LEN) // CMP_STRIDE + 1
FOX_QKV = 3 * NH * DH
EVEN_IN = FOX_QKV + NH + NH * DH + 6 * GROUPS * DH + 3 * NH
HALF_ROW = SEQ - P

D_RNN = 1280
NR = D_RNN // P
CONV_W = 4

PH = 8
NK = 128
TOPK = 16
HC = 2 * PH
GSCALE = 2.0 ** 14


def bc(ap, shape):
    return ap.to_broadcast(shape)


class Core:

    def __init__(self, nc, ctx):
        self.nc = nc
        self.sems = []
        self.h = ctx.enter_context(nc.sbuf_tensor("h", [P, TT, D], F32))
        self.ident = ctx.enter_context(nc.sbuf_tensor("ident", [P, P], F32))
        self.ps = [ctx.enter_context(nc.psum_tensor(f"bank{i}", [P, 512], F32)) for i in range(8)]

    def sem(self, name):
        self.sems.append(self.nc.alloc_semaphore(name=name))
        return self.sems[-1]

    def end_layer(self):
        self.nc.clear_and_free_semaphores(self.sems)
        self.nc.all_engine_barrier()
        self.sems = []


def constants(c, x):
    nc = c.nc
    x_loaded, ident_made = c.sem("x_loaded"), c.sem("ident_made")
    with nc.Block() as block:
        @block.sync
        def _(sp):
            sp.dma_start(c.h[:], x[0].rearrange("(t p) d -> p t d", p=P)).then_inc(x_loaded, 16)
            sp.wait_ge(x_loaded, 16)

        @block.gpsimd
        def _(pool):
            pool.memset(c.ident[:], 1.0).then_inc(ident_made, 1)
            pool.wait_ge(ident_made, 1)
            pool.affine_select(out=c.ident[:], in_=c.ident[:], compare_op=ALU.is_equal, fill=0.0, base=0,
                               pattern=[[-1, P]], channel_multiplier=1).then_inc(ident_made, 1)


def norm_block(c, name, gain, hT, split=None):
    nc = c.nc
    gain_loaded, squares, scale, scaled = (c.sem(f"{name}_{s}") for s in ("gain", "squares", "scale", "scaled"))
    turned, out_a, out_v, hi_done = (c.sem(f"{name}_{s}") for s in ("turned", "out_a", "out_v", "hi"))
    with ExitStack() as st:
        gT = st.enter_context(nc.sbuf_tensor(f"{name}_gT", [P, KD], F32))
        hn = st.enter_context(nc.sbuf_tensor(f"{name}_hn", [P, TT, D], F32))
        ss = st.enter_context(nc.sbuf_tensor(f"{name}_ss", [P, TT], F32))
        ms = st.enter_context(nc.sbuf_tensor(f"{name}_ms", [P, TT], F32))
        std = st.enter_context(nc.sbuf_tensor(f"{name}_std", [P, TT], F32))
        r = st.enter_context(nc.sbuf_tensor(f"{name}_r", [P, TT], F32))
        block = st.enter_context(nc.Block())

        @block.sync
        def _(sp):
            sp.dma_start(gT[:], gain.rearrange("(k p) -> p k", p=P),
                         allow_slow_non_contiguous=True).then_inc(gain_loaded, 16)

        @block.scalar
        def _(act):
            for t in range(TT):
                act.activation(hn[:, t, :], c.h[:, t, :], ACT.Square, accum_out=ss[:, t:t + 1]).then_inc(squares, 1)
            act.wait_ge(scale, 1)
            act.activation(std[:], ms[:], ACT.Sqrt).then_inc(squares, 1)
            act.wait_ge(gain_loaded, 16)
            for k in range(1, KD, 2):
                act.wait_ge(turned, k + 1)
                act.activation(hT[:, k, :], c.ps[k][:], ACT.Copy, scale=gT[:, k:k + 1]).then_inc(out_a, 1)
            if split:
                for k in range(KD):
                    if k % 2:
                        act.wait_ge(out_a, k // 2 + 1)
                    else:
                        act.wait_ge(out_v, k // 2 + 1)
                    act.activation(split[0][:, k, :], hT[:, k, :], ACT.Copy).then_inc(hi_done, 1)

        @block.vector
        def _(dve):
            dve.wait_ge(squares, TT)
            dve.tensor_scalar(ms[:], ss[:], 1.0 / D, EPS, ALU.mult, ALU.add).then_inc(scale, 1)
            dve.wait_ge(squares, TT + 1)
            dve.reciprocal(r[:], std[:]).then_inc(scale, 1)
            dve.wait_ge(scale, 2)
            for t in range(TT):
                dve.tensor_scalar(hn[:, t, :], c.h[:, t, :], r[:, t:t + 1], None, ALU.mult).then_inc(scaled, 1)
            dve.wait_ge(gain_loaded, 16)
            for k in range(0, KD, 2):
                dve.wait_ge(turned, k + 1)
                dve.tensor_scalar(hT[:, k, :], c.ps[k][:], gT[:, k:k + 1], None, ALU.mult).then_inc(out_v, 1)
            if split:
                for k in range(KD):
                    dve.wait_ge(hi_done, k + 1)
                    dve.tensor_tensor(split[1][:, k, :], hT[:, k, :], split[0][:, k, :].bitcast(F32), ALU.subtract)

        @block.tensor
        def _(pe):
            pe.wait_ge(scaled, TT)
            for k in range(KD):
                for t in range(TT):
                    last = pe.transpose(c.ps[k][:, t * P:(t + 1) * P], hn[:, t, k * P:(k + 1) * P], c.ident[:])
                last.then_inc(turned, 1)


SERIES = [1 / 15, 1 / 13, 1 / 11, 1 / 9, 1 / 7, 1 / 5, 1 / 3]


def half_log1p(dve, chain, at, e, d, z, q, p):
    dve.tensor_scalar(d, e, 2.0, None, ALU.add).then_inc(chain, 1)
    dve.wait_ge(chain, at + 1)
    dve.reciprocal(q, d).then_inc(chain, 1)
    dve.wait_ge(chain, at + 2)
    dve.tensor_tensor(z, e, q, ALU.mult).then_inc(chain, 1)
    dve.wait_ge(chain, at + 3)
    dve.tensor_tensor(q, z, z, ALU.mult).then_inc(chain, 1)
    dve.wait_ge(chain, at + 4)
    dve.tensor_scalar(p, q, SERIES[0], None, ALU.mult).then_inc(chain, 1)
    n = at + 5
    for coefficient in SERIES[1:]:
        dve.wait_ge(chain, n)
        dve.scalar_tensor_tensor(p, p, coefficient, q, ALU.add, ALU.mult).then_inc(chain, 1)
        n += 1
    dve.wait_ge(chain, n)
    dve.scalar_tensor_tensor(p, p, 1.0, z, ALU.add, ALU.mult).then_inc(chain, 1)
    dve.wait_ge(chain, n + 1)
    return n + 1


def even_project(c, hT, w_in, b_f, R):
    nc = c.nc
    slots = [c.sem(f"proj_w{i}") for i in range(3)]
    bias_in, product, out_a, out_v = (c.sem(f"proj_{s}") for s in ("bias", "product", "out_a", "out_v"))
    GROUPS_W = [(0, 512), (512, 512), (1024, 512), (1536, 8 + 512), (2056, 384), (2440, 384 + 3 * NH)]
    jobs = []
    for m in range(4):
        jobs.append((0, "feature", m * P, (R["Qf"], 2 * m), DH ** -0.5))
    for m in range(4):
        jobs.append((1, "feature", m * P, (R["Kf"], 2 * m), 1.0))
    for t in range(TT):
        jobs.append((2, "fox_v", 0, t, 1.0))
    jobs.append((3, "forget", 0, None, 1.0))
    for m in range(4):
        jobs.append((3, "feature", 8 + m * P, (R["Qn"], 2 * m), DH ** -0.5))
    for m in range(2):
        jobs.append((4, "feature", m * P, (R["Kc"], 2 * m), 1.0))
    jobs.append((4, "feature", 2 * P, (R["Kn"], 0), 1.0))
    jobs.append((5, "feature", P, (R["Kn"], 2), 1.0))
    for t in range(TT):
        jobs.append((5, "nsa_v", 0, t, 1.0))
    group_end = [max(j for j, job in enumerate(jobs) if job[0] == g) + 1 for g in range(6)]
    v_count = [sum(job[1] == "feature" for job in jobs[:j + 1]) for j in range(len(jobs))]
    with ExitStack() as st:
        w = st.enter_context(nc.sbuf_tensor("proj_w", [P, 3, KD, 520], F32))
        bf = st.enter_context(nc.sbuf_tensor("proj_bf", [NH, 1], F32))
        block = st.enter_context(nc.Block())

        @block.sync
        def _(sp):
            sp.dma_start(bf[:], b_f.unsqueeze(1)).then_inc(bias_in, 16)
            for g, (c0, width) in enumerate(GROUPS_W):
                if g >= 3:
                    sp.wait_ge(product, group_end[g - 3])
                sp.dma_start(w[:, g % 3, :, 0:width],
                             w_in[:, c0:c0 + width].rearrange("(k p) n -> p k n", p=P)).then_inc(slots[g % 3], 16)

        @block.tensor
        def _(pe):
            for j, (g, kind, col, where, _) in enumerate(jobs):
                if j == 0 or jobs[j - 1][0] != g:
                    pe.wait_ge(slots[g % 3], 16 * (g // 3 + 1))
                if j >= 8:
                    pe.wait_ge(out_a, j - 7)
                    pe.wait_ge(out_v, v_count[j - 8])
                b = c.ps[j % 8]
                if kind in ("feature", "forget"):
                    m = P if kind == "feature" else NH
                    for k in range(KD):
                        last = pe.matmul(b[0:m, :], w[:, g % 3, k, col:col + m], hT[:, k, :], start=(k == 0),
                                         stop=(k == KD - 1))
                elif kind == "fox_v":
                    for k in range(KD):
                        last = pe.matmul(b[:], hT[:, k, where * P:(where + 1) * P], w[:, g % 3, k, 0:512],
                                         start=(k == 0), stop=(k == KD - 1))
                else:
                    for lo, hi, at in ((0, P, 0), (2 * P, 3 * P + 3 * NH, P)):
                        for k in range(KD):
                            last = pe.matmul(b[:, at:at + hi - lo], hT[:, k, where * P:(where + 1) * P],
                                             w[:, g % 3, k, lo:hi], start=(k == 0), stop=(k == KD - 1))
                last.then_inc(product, 1)

        @block.scalar
        def _(act):
            act.wait_ge(bias_in, 16)
            for j, (g, kind, col, where, scale) in enumerate(jobs):
                act.wait_ge(product, j + 1)
                b = c.ps[j % 8]
                if kind == "feature":
                    last = act.activation(where[0][0:DH, where[1], :], b[0:DH, :], ACT.Copy, scale=scale)
                elif kind == "forget":
                    last = act.activation(R["f"][:], b[0:NH, :], ACT.Identity, bias=bf[:, 0:1])
                elif kind == "fox_v":
                    last = act.activation(R["Vf"][:, where, :], b[:], ACT.Copy)
                else:
                    act.activation(R["Vn"][:, where, :], b[:, 0:2 * P], ACT.Copy)
                    last = act.activation(R["gates"][:, where, :], b[:, 2 * P:2 * P + 3 * NH], ACT.Sigmoid)
                last.then_inc(out_a, 1)

        @block.vector
        def _(dve):
            for j, (g, kind, col, where, scale) in enumerate(jobs):
                if kind == "feature":
                    dve.wait_ge(product, j + 1)
                    dve.tensor_scalar(where[0][0:DH, where[1] + 1, :], c.ps[j % 8][DH:P, :], scale, None,
                                      ALU.mult).then_inc(out_v, 1)

        @block.gpsimd
        def _(pool):
            tables = c.sem("tables")
            pool.iota(R["bias"][:, NH, :], [[-1, SEQ]], base=HALF_ROW, channel_multiplier=1,
                      allow_small_or_imprecise_dtypes=True)
            pool.iota(R["dist_c"][:], [[P, TT], [-CMP_STRIDE, N_CMP]], base=-(CMP_LEN - 1), channel_multiplier=1,
                      allow_small_or_imprecise_dtypes=True).then_inc(tables, 1)
            pool.wait_ge(tables, 1)
            for h in range(NH):
                slope = 2.0 ** (-8.0 * (h + 1) / NH)
                pool.tensor_scalar(R["bias"][:, h, :], R["bias"][:, NH, :], -slope, None, ALU.mult)
                last = pool.tensor_scalar(R["bias_c"][:, h], R["dist_c"][:], -slope, None, ALU.mult)
            last.then_inc(tables, 1)
            pool.wait_ge(tables, 2)
            pool.memset(R["bias"][:, NH, :], 0.0).then_inc(tables, 1)
            pool.wait_ge(tables, 3)
            for h in range(NH + 1):
                pool.affine_select(out=R["bias"][:, h, :], in_=R["bias"][:, h, :], compare_op=ALU.is_ge, fill=NEG,
                                   base=HALF_ROW, pattern=[[-1, SEQ]], channel_multiplier=1)
            for h in range(NH):
                pool.affine_select(out=R["bias_c"][:, h], in_=R["bias_c"][:, h], compare_op=ALU.is_ge, fill=NEG,
                                   base=-(CMP_LEN - 1), pattern=[[P, TT], [-CMP_STRIDE, N_CMP]], channel_multiplier=1)


def even_prepare(c, A, R):
    nc = c.nc
    loaded, rows, padded, summed, product, chain, exps = (
        c.sem(f"prep_{s}") for s in ("loaded", "rows", "padded", "summed", "product", "chain", "exps"))
    with ExitStack() as st:
        def sb(n, shape):
            return st.enter_context(nc.sbuf_tensor(f"prep_{n}", shape, F32))

        wk, wv = sb("wk", [DH, CMP_LEN, DH]), sb("wv", [DH, CMP_LEN, DH])
        pos = sb("pos", [DH, CMP_LEN])
        win = sb("win", [DH, 4, N_CMP, CMP_LEN])
        e, d, z, q, p = (sb(n, [NH, SEQ]) for n in "edzqp")
        low, cum, neg, ones = (sb(n, [NH, SEQ]) for n in ("low", "cum", "neg", "ones"))
        block = st.enter_context(nc.Block())
        f = R["f"]

        @block.sync
        def _(sp):
            sp.dma_start(pos[:], A["even_cmp_pos"][0].rearrange("l d -> d l"),
                         allow_slow_non_contiguous=True).then_inc(loaded, 16)
            sp.dma_start(wk[:], A["even_w_cmp_k"][0].rearrange("l d e -> d l e")).then_inc(loaded, 16)
            sp.dma_start(wv[:], A["even_w_cmp_v"][0].rearrange("l d e -> d l e")).then_inc(loaded, 16)
            sp.wait_ge(padded, 2)
            sp.wait_ge(summed, 1)
            for h in range(NH):
                sp.dma_start(R["Qf"][DH:DH + 1, h, :], cum[h:h + 1, :]).then_inc(rows, 16)
                sp.dma_start(R["Kf"][96:97, h, :], neg[h:h + 1, :]).then_inc(rows, 16)
            sp.wait_ge(rows, 16 * 2 * NH)

        @block.gpsimd
        def _(pool):
            pool.memset(R["Qf"][DH:97, :, :], 0.0)
            pool.memset(R["Kf"][DH:97, :, :], 0.0).then_inc(padded, 1)
            pool.wait_ge(padded, 1)
            pool.memset(R["Qf"][96:97, :, :], 1.0)
            pool.memset(R["Kf"][DH:DH + 1, :, :], 1.0).then_inc(padded, 1)
            pool.wait_ge(padded, 2)
            first = R["gates"][:, 0, :].rearrange("p (h b) -> p h b", b=3)[:, :, 0]
            pool.affine_select(out=first, in_=first, compare_op=ALU.is_ge, fill=0.0, base=-(CMP_LEN - 1),
                               pattern=[[0, NH]], channel_multiplier=1)

        @block.scalar
        def _(act):
            act.activation(e[:], f[:], ACT.Abs).then_inc(exps, 1)
            act.wait_ge(exps, 1)
            act.activation(e[:], e[:], ACT.Exp, scale=-1.0).then_inc(exps, 1)

        @block.vector
        def _(dve):
            dve.memset(ones[:], 1.0)
            dve.tensor_scalar(low[:], f[:], 0.0, None, ALU.min)
            dve.wait_ge(exps, 2)
            n = half_log1p(dve, chain, 0, e[:], d[:], z[:], q[:], p[:])
            dve.scalar_tensor_tensor(low[:], p[:], -2.0, low[:], ALU.mult, ALU.add).then_inc(chain, 1)
            dve.wait_ge(chain, n + 1)
            dve.tensor_tensor_scan(cum[:], ones[:], low[:], 0.0, ALU.mult, ALU.add).then_inc(chain, 1)
            dve.wait_ge(chain, n + 2)
            dve.tensor_scalar(neg[:], cum[:], -1.0, None, ALU.mult).then_inc(summed, 1)
            dve.wait_ge(loaded, 48)
            for s in range(4):
                for half in range(2):
                    a = half * CMP_STRIDE
                    src = R["Kc"][:, s, a:a + N_CMP * CMP_STRIDE].rearrange("p (n b) -> p n b", b=CMP_STRIDE)
                    last = dve.tensor_tensor(win[:, s, :, a:a + CMP_STRIDE], src,
                                             bc(pos[:, a:a + CMP_STRIDE].unsqueeze(1), [DH, N_CMP, CMP_STRIDE]),
                                             ALU.add)
            last.then_inc(summed, 1)
            dve.wait_ge(product, 1)
            dve.tensor_copy(R["kc"][:], c.ps[0][0:DH, 0:GROUPS * N_CMP].rearrange("p (g n) -> p g n", g=GROUPS))
            dve.wait_ge(product, 2)
            dve.tensor_copy(R["vc"][:], c.ps[1][0:N_CMP, 0:GROUPS * DH].rearrange("p (g e) -> p g e", g=GROUPS))

        @block.tensor
        def _(pe):
            pe.wait_ge(summed, 2)
            for m in range(CMP_LEN):
                last = pe.matmul(c.ps[0][0:DH, 0:GROUPS * N_CMP], wk[:, m, :], win[:, 0:2, :, m], start=(m == 0),
                                 stop=(m == CMP_LEN - 1))
            last.then_inc(product, 1)
            for g in range(GROUPS):
                for m in range(CMP_LEN):
                    last = pe.matmul(c.ps[1][0:N_CMP, g * DH:(g + 1) * DH], win[:, 2 + g, :, m], wv[:, m, :],
                                     start=(m == 0), stop=(m == CMP_LEN - 1))
            last.then_inc(product, 1)


def even_attend(c, R, w_out, w_loaded, w_dram):
    nc = c.nc
    names = ("scores", "biased", "exp", "rz", "normed", "turned", "copied", "pv", "out")
    S = {s: c.sem(f"att_{s}") for s in names}
    units = []
    for j in range(2 * NH):
        for i in range(TT):
            width = P * (i + 1)
            cols = slice(i * P, (i + 1) * P)
            if j < NH:
                v = [R["Vf"][:, s, j * DH:(j + 1) * DH] for s in range(i + 1)]
                units.append((j, i, width, R["Qf"][:, j, cols], R["Kf"][:, j, 0:width],
                              R["bias"][:, NH, HALF_ROW - i * P:SEQ], v, None, True, True))
                continue
            h = j - NH
            g = h // (NH // GROUPS)
            q = R["Qn"][:, h, cols]
            units.append((j, i, N_CMP, q, R["kc"][:, g, :], R["bias_c"][:, h, i, :], [R["vc"][:, g, :]],
                          R["gates"][:, i, 3 * h:3 * h + 1], True, False))
            for b in range(2):
                v = [R["Vn"][:, s, b * P + g * DH:b * P + (g + 1) * DH] for s in range(i + 1)]
                units.append((j, i, width, q, R["Kn"][:, 2 * b + g, 0:width], R["bias"][:, h, HALF_ROW - i * P:SEQ], v,
                              R["gates"][:, i, 3 * h + b + 1:3 * h + b + 2], False, b == 1))
    N = len(units)
    head_end = [max(u for u in range(N) if units[u][0] == j) for j in range(2 * NH)]
    LAG_N, LAG_T, LAG_V = 2, 3, 4
    with ExitStack() as st:
        def sb(n, shape):
            return st.enter_context(nc.sbuf_tensor(f"att_{n}", shape, F32))

        sc = sb("sc", [P, 2, SEQ])
        p = sb("p", [P, 4, SEQ])
        pT = sb("pT", [P, 2, SEQ])
        low = sb("low", [P, 4])
        z = sb("z", [P, 4])
        rz = sb("rz", [P, 4])
        block = st.enter_context(nc.Block())

        @block.sync
        def _(sp):
            sp.dma_start(w_out[:], w_dram.rearrange("(k p) n -> p k n", p=P)).then_inc(w_loaded, 16)

        @block.tensor
        def _(pe):
            def scores(u):
                _, _, width, q, k, *_ = units[u]
                if u >= 2:
                    pe.wait_ge(S["biased"], u - 1)
                pe.matmul(c.ps[u % 2][:, 0:width], q, k, start=True, stop=True).then_inc(S["scores"], 1)

            def turn(u):
                width = units[u][2]
                pe.wait_ge(S["normed"], u + 1)
                if u >= 2:
                    pe.wait_ge(S["copied"], u - 1)
                for a in range(0, width, P):
                    m = min(P, width - a)
                    last = pe.transpose(c.ps[2 + u % 2][0:m, a:a + P], p[:, u % 4, a:a + m], c.ident[:])
                last.then_inc(S["turned"], 1)

            def weigh(u):
                j, i, width, *_, values, _, first, final = units[u]
                pe.wait_ge(S["copied"], u + 1)
                if u == 0 or units[u - 1][0] != j:
                    if j >= 2:
                        pe.wait_ge(S["out"], j - 1)
                for s, v in enumerate(values):
                    m = min(P, width - s * P)
                    last = pe.matmul(c.ps[4 + j % 2][0:DH, i * P:(i + 1) * P], v, pT[0:m, u % 2, s * P:(s + 1) * P],
                                     start=(first and s == 0), stop=(final and s == len(values) - 1))
                last.then_inc(S["pv"], 1)

            for u in range(N + LAG_V):
                if u < N:
                    scores(u)
                if LAG_T <= u < N + LAG_T:
                    turn(u - LAG_T)
                if u >= LAG_V:
                    weigh(u - LAG_V)

        @block.vector
        def _(dve):
            for u in range(N + LAG_N):
                m = u - LAG_N
                if m >= 0:
                    dve.wait_ge(S["exp"], m + 1)
                    dve.reciprocal(rz[:, m % 4:m % 4 + 1], z[:, m % 4:m % 4 + 1]).then_inc(S["rz"], 1)
                if u < N:
                    width, bias = units[u][2], units[u][5]
                    dve.wait_ge(S["scores"], u + 1)
                    if u >= 2:
                        dve.wait_ge(S["exp"], u - 1)
                    dve.tensor_tensor_reduce(sc[:, u % 2, 0:width], c.ps[u % 2][:, 0:width], bias, -1.0, BIG, ALU.add,
                                             ALU.min, low[:, u % 4:u % 4 + 1]).then_inc(S["biased"], 1)
                if m >= 0:
                    width, gate = units[m][2], units[m][7]
                    dve.wait_ge(S["rz"], m + 1)
                    o = p[:, m % 4, 0:width]
                    dve.tensor_scalar(o, o, rz[:, m % 4:m % 4 + 1], gate, ALU.mult,
                                      ALU.bypass if gate is None else ALU.mult).then_inc(S["normed"], 1)

        @block.scalar
        def _(act):
            done = 0
            for u in range(N + LAG_V + 1):
                if u < N:
                    width = units[u][2]
                    act.wait_ge(S["biased"], u + 1)
                    if u >= 4:
                        act.wait_ge(S["turned"], u - 3)
                    act.activation(p[:, u % 4, 0:width], sc[:, u % 2, 0:width], ACT.Exp, bias=low[:, u % 4:u % 4 + 1],
                                   scale=-1.0, accum_out=z[:, u % 4:u % 4 + 1]).then_inc(S["exp"], 1)
                m = u - LAG_T
                if 0 <= m < N:
                    width = units[m][2]
                    act.wait_ge(S["turned"], m + 1)
                    if m >= 2:
                        act.wait_ge(S["pv"], m - 1)
                    rows = min(P, width)
                    act.activation(pT[0:rows, m % 2, 0:max(width, P)], c.ps[2 + m % 2][0:rows, 0:max(width, P)],
                                   ACT.Copy).then_inc(S["copied"], 1)
                if done < 2 * NH and u - LAG_V - 1 == head_end[done]:
                    act.wait_ge(S["pv"], head_end[done] + 1)
                    r0 = done % 2 * DH
                    act.activation(R["hT"][r0:r0 + DH, done // 2, :], c.ps[4 + done % 2][0:DH, :],
                                   ACT.Copy).then_inc(S["out"], 1)
                    done += 1


def project_out(c, name, oT, n_k, w, w_loaded, w_count):
    nc = c.nc
    product = c.sem(f"{name}_product")
    with nc.Block() as block:
        @block.tensor
        def _(pe):
            pe.wait_ge(w_loaded, w_count)
            for n in range(2 * TT):
                t, half = n // 2, n % 2
                for k in range(n_k):
                    last = pe.matmul(c.ps[n][:], oT[:, k, t * P:(t + 1) * P], w[:, k, half * 512:(half + 1) * 512],
                                     start=(k == 0), stop=(k == n_k - 1))
                last.then_inc(product, 1)

        @block.vector
        def _(dve):
            for n in range(2 * TT):
                t, half = n // 2, n % 2
                dve.wait_ge(product, n + 1)
                o = c.h[:, t, half * 512:(half + 1) * 512]
                dve.tensor_tensor(o, c.ps[n][:], o, ALU.add)


def even_layer(c, A):
    nc = c.nc
    with ExitStack() as st:
        def sb(n, shape):
            return st.enter_context(nc.sbuf_tensor(f"even_{n}", shape, F32))

        R = {"hT": sb("hT", [P, KD, SEQ])}
        norm_block(c, "even_norm", A["even_norm_g"][0], R["hT"])
        R.update(
            Qf=sb("Qf", [97, NH, SEQ]), Kf=sb("Kf", [97, NH, SEQ]), Vf=sb("Vf", [P, TT, NH * DH]),
            Qn=sb("Qn", [DH, NH, SEQ]), Kn=sb("Kn", [DH, 2 * GROUPS, SEQ]), Kc=sb("Kc", [DH, 2 * GROUPS, SEQ]),
            Vn=sb("Vn", [P, TT, 2 * P]), gates=sb("gates", [P, TT, 3 * NH]), f=sb("f", [NH, SEQ]),
            kc=sb("kc", [DH, GROUPS, N_CMP]), vc=sb("vc", [N_CMP, GROUPS, DH]),
            bias=sb("bias", [P, NH + 1, SEQ]), bias_c=sb("bias_c", [P, NH, TT, N_CMP]),
            dist_c=sb("dist_c", [P, TT, N_CMP]))
        even_project(c, R["hT"], A["even_w_in"][0], A["even_b_f"][0], R)
        even_prepare(c, A, R)
        w_loaded = c.sem("even_w_out_loaded")
        w_out = sb("w_out", [P, KD, D])
        even_attend(c, R, w_out, w_loaded, A["even_w_out"][0])
        project_out(c, "even_out", R["hT"], KD, w_out, w_loaded, 16)


def odd_project(c, hT, w_in, gate, xr):
    nc = c.nc
    slots = [c.sem(f"odd_proj_w{i}") for i in range(3)]
    product, read_a, read_v = (c.sem(f"odd_proj_{s}") for s in ("product", "read_a", "read_v"))
    with ExitStack() as st:
        w = st.enter_context(nc.sbuf_tensor("odd_proj_w", [P, 3, KD, 512], F32))
        block = st.enter_context(nc.Block())

        @block.sync
        def _(sp):
            for g in range(5):
                if g >= 3:
                    sp.wait_ge(product, 4 * (g - 2))
                sp.dma_start(w[:, g % 3], w_in[:, g * 512:(g + 1) * 512].rearrange("(k p) n -> p k n", p=P)) \
                    .then_inc(slots[g % 3], 16)

        @block.tensor
        def _(pe):
            for n in range(2 * NR):
                g = n // 4
                if n % 4 == 0:
                    pe.wait_ge(slots[g % 3], 16 * (g // 3 + 1))
                if n >= 8:
                    pe.wait_ge(read_a, min(n - 7, NR))
                    if n - 8 >= NR:
                        pe.wait_ge(read_v, n - 7 - NR)
                for k in range(KD):
                    last = pe.matmul(c.ps[n % 8][:], w[:, g % 3, k, n % 4 * P:(n % 4 + 1) * P], hT[:, k, :],
                                     start=(k == 0), stop=(k == KD - 1))
                last.then_inc(product, 1)

        @block.scalar
        def _(act):
            for n in range(NR):
                act.wait_ge(product, n + 1)
                act.activation(gate[:, n, :], c.ps[n % 8][:], ACT.Gelu).then_inc(read_a, 1)

        @block.vector
        def _(dve):
            dve.memset(xr[:, :, 0:CONV_W - 1], 0.0)
            for n in range(NR):
                dve.wait_ge(product, NR + n + 1)
                dve.tensor_copy(xr[:, n, CONV_W - 1:], c.ps[(NR + n) % 8][:]).then_inc(read_v, 1)


def odd_recur(c, A, gate, xr, w_out, w_loaded):
    nc = c.nc
    S = {s: c.sem(f"lru_{s}") for s in ("loaded", "w", "chain", "exps", "soft", "conv", "y", "product", "ri", "tanh",
                                        "ix", "root", "step", "decay", "rix", "u", "scan")}
    with ExitStack() as st:
        def sb(n, shape):
            return st.enter_context(nc.sbuf_tensor(f"lru_{n}", shape, F32))

        cw = sb("cw", [P, CONV_W, NR])
        cb, ba, bi, lam = sb("cb", [P, NR]), sb("ba", [P, NR]), sb("bi", [P, NR]), sb("lam", [P, NR])
        wa, wi = sb("wa", [P, NR, P]), sb("wi", [P, NR, P])
        e, d, z, q, pp, soft = (sb(n, [P, NR]) for n in ("e", "d", "z", "q", "p", "soft"))
        y = sb("y", [P, 2, SEQ])
        r, i_ = sb("r", [P, 2, SEQ]), sb("i", [P, 2, SEQ])
        s_ = sb("s", [P, NR, SEQ])
        ix = sb("ix", [P, NR, SEQ])
        den, inv, a, root = sb("den", [P, SEQ]), sb("inv", [P, 2, SEQ]), sb("a", [P, SEQ]), sb("root", [P, 2, SEQ])
        u, hs = sb("u", [P, SEQ]), sb("hs", [P, SEQ])
        block = st.enter_context(nc.Block())

        @block.sync
        def _(sp):
            small = dict(allow_slow_non_contiguous=True)
            sp.dma_start(cb[:], A["odd_conv_b"][0].rearrange("(n p) -> p n", p=P), **small).then_inc(S["loaded"], 16)
            for j in range(CONV_W):
                sp.dma_start(cw[:, j, :], A["odd_conv_w"][0, j].rearrange("(n p) -> p n", p=P), **small) \
                    .then_inc(S["loaded"], 16)
            sp.dma_start(ba[:], A["odd_b_ra"][0].rearrange("(n p) -> p n", p=P), **small).then_inc(S["loaded"], 16)
            sp.dma_start(bi[:], A["odd_b_ri"][0].rearrange("(n p) -> p n", p=P), **small).then_inc(S["loaded"], 16)
            sp.dma_start(lam[:], A["odd_lam"][0].rearrange("(n p) -> p n", p=P), **small).then_inc(S["loaded"], 16)
            sp.dma_start(wa[:], A["odd_w_ra"][0].rearrange("n c e -> c n e")).then_inc(S["w"], 16)
            sp.dma_start(wi[:], A["odd_w_ri"][0].rearrange("n c e -> c n e")).then_inc(S["w"], 16)
            sp.dma_start(w_out[:], A["odd_w_out"][0].rearrange("(k p) n -> p k n", p=P)).then_inc(w_loaded, 16)
        LOADED = 16 * (CONV_W + 4)

        @block.tensor
        def _(pe):
            pe.wait_ge(S["w"], 32)
            for n in range(NR):
                pe.wait_ge(S["y"], n + 1)
                if n >= 2:
                    pe.wait_ge(S["ri"], 2 * n - 2)
                pe.matmul(c.ps[2 * (n % 2)][:], wa[:, n, :], y[:, n % 2, :], start=True, stop=True) \
                    .then_inc(S["product"], 1)
                pe.matmul(c.ps[2 * (n % 2) + 1][:], wi[:, n, :], y[:, n % 2, :], start=True, stop=True) \
                    .then_inc(S["product"], 1)

        @block.scalar
        def _(act):
            act.wait_ge(S["loaded"], LOADED)
            act.activation(e[:], lam[:], ACT.Abs).then_inc(S["exps"], 1)
            act.wait_ge(S["exps"], 1)
            act.activation(e[:], e[:], ACT.Exp, scale=-1.0).then_inc(S["exps"], 1)
            act.wait_ge(S["soft"], 1)
            for n in range(NR):
                act.wait_ge(S["product"], 2 * n + 1)
                act.activation(r[:, n % 2, :], c.ps[2 * (n % 2)][:], ACT.Sigmoid, bias=ba[:, n:n + 1]) \
                    .then_inc(S["ri"], 1)
                act.wait_ge(S["product"], 2 * n + 2)
                if n >= 2:
                    act.wait_ge(S["ix"], n - 1)
                act.activation(i_[:, n % 2, :], c.ps[2 * (n % 2) + 1][:], ACT.Sigmoid, bias=bi[:, n:n + 1]) \
                    .then_inc(S["ri"], 1)
                act.wait_ge(S["ri"], 2 * n + 1)
                act.activation(s_[:, n, :], r[:, n % 2, :], ACT.Tanh, scale=soft[:, n:n + 1]).then_inc(S["tanh"], 1)
            for n in range(NR):
                act.wait_ge(S["tanh"], n + 1)
                if n >= 2:
                    act.wait_ge(S["u"], n - 1)
                act.activation(root[:, n % 2, :], s_[:, n, :], ACT.Sqrt, scale=4.0).then_inc(S["root"], 1)

        @block.gpsimd
        def _(pool):
            for n in range(NR):
                pool.wait_ge(S["ri"], 2 * n + 2)
                pool.tensor_tensor(ix[:, n, :], i_[:, n % 2, :], y[:, n % 2, :], ALU.mult).then_inc(S["ix"], 1)
            for n in range(NR):
                pool.wait_ge(S["decay"], 2 * n + 1)
                pool.tensor_tensor(ix[:, n, :], ix[:, n, :], inv[:, n % 2, :], ALU.mult).then_inc(S["rix"], 1)

        @block.vector
        def _(dve):
            dve.wait_ge(S["loaded"], LOADED)
            dve.wait_ge(S["exps"], 2)
            at = half_log1p(dve, S["chain"], 0, e[:], d[:], z[:], q[:], pp[:])
            dve.tensor_scalar(d[:], lam[:], -4.0, 0.0, ALU.mult, ALU.max).then_inc(S["chain"], 1)
            dve.wait_ge(S["chain"], at + 1)
            dve.scalar_tensor_tensor(soft[:], pp[:], 8.0, d[:], ALU.mult, ALU.add).then_inc(S["soft"], 1)
            for n in range(NR):
                yn = y[:, n % 2, :]
                if n >= 2:
                    dve.wait_ge(S["ix"], n - 1)
                    dve.wait_ge(S["product"], 2 * n - 2)
                dve.tensor_scalar(yn, xr[:, n, 0:SEQ], cw[:, 0, n:n + 1], cb[:, n:n + 1], ALU.mult,
                                  ALU.add).then_inc(S["conv"], 1)
                for j in range(1, CONV_W):
                    dve.wait_ge(S["conv"], (CONV_W - 1) * n + j)
                    last = dve.scalar_tensor_tensor(yn, xr[:, n, j:j + SEQ], cw[:, j, n:n + 1], yn, ALU.mult, ALU.add)
                    last.then_inc(S["conv"] if j < CONV_W - 1 else S["y"], 1)
            for n in range(NR):
                dve.wait_ge(S["tanh"], n + 1)
                dve.tensor_scalar(den[:], s_[:, n, :], 1.0, None, ALU.add).then_inc(S["step"], 1)
                dve.wait_ge(S["step"], n + 1)
                if n >= 2:
                    dve.wait_ge(S["rix"], n - 1)
                dve.reciprocal(inv[:, n % 2, :], den[:]).then_inc(S["decay"], 1)
                dve.wait_ge(S["decay"], 2 * n + 1)
                dve.tensor_scalar(a[:], inv[:, n % 2, :], 2.0, -1.0, ALU.mult, ALU.add).then_inc(S["decay"], 1)
                dve.wait_ge(S["rix"], n + 1)
                dve.wait_ge(S["root"], n + 1)
                dve.tensor_tensor(u[:], ix[:, n, :], root[:, n % 2, :], ALU.mult).then_inc(S["u"], 1)
                dve.wait_ge(S["u"], n + 1)
                dve.wait_ge(S["decay"], 2 * n + 2)
                dve.tensor_tensor_scan(hs[:], a[:], u[:], 0.0, ALU.mult, ALU.add).then_inc(S["scan"], 1)
                dve.wait_ge(S["scan"], 2 * n + 1)
                dve.tensor_tensor(gate[:, n, :], gate[:, n, :], hs[:], ALU.mult).then_inc(S["scan"], 1)
                if n < NR - 1:
                    dve.wait_ge(S["scan"], 2 * n + 2)


def odd_layer(c, A):
    nc = c.nc
    with ExitStack() as st:
        def sb(n, shape):
            return st.enter_context(nc.sbuf_tensor(f"odd_{n}", shape, F32))

        gate = sb("gate", [P, NR, SEQ])
        xr = sb("xr", [P, NR, CONV_W - 1 + SEQ])
        with nc.sbuf_tensor("odd_hT", [P, KD, SEQ], F32) as hT:
            norm_block(c, "odd_norm", A["odd_norm_g"][0], hT)
            odd_project(c, hT, A["odd_w_in"][0], gate, xr)
        w_loaded = c.sem("odd_w_out_loaded")
        w_out = sb("w_out", [P, NR, D])
        odd_recur(c, A, gate, xr, w_out, w_loaded)
        project_out(c, "odd_out", gate, NR, w_out, w_loaded, 16)


def peer_pick(c, name, hT, w_q, sub_keys, picks, gates):
    nc = c.nc
    S = {s: c.sem(f"{name}_{s}") for s in (
        "w0", "w1", "keys", "keysT", "keysT_out", "q", "q_out", "sc", "sc_out", "chain", "place", "onehot", "exp",
        "turn")}

    steps = []
    for n in range(HC):
        steps += [(s, n) for s in ("max", "strike", "max2", "index2", "float")]
        if n % 2:
            steps += [(s, n // 2) for s in ("cand", "bmax", "bstrike", "bmax2", "bindex2", "split", "split_float", "eq")]
            if n > 1:
                steps.append(("gather", n // 2 - 1))
    steps += [("gather", PH - 1), ("sub", 0), ("sum", 0), ("recip", 0), ("weigh", 0)]
    done = {s: i + 1 for i, s in enumerate(steps)}
    with ExitStack() as st:
        def sb(n, shape, dt=F32):
            return st.enter_context(nc.sbuf_tensor(f"{name}_{n}", shape, dt))

        w = sb("w", [P, 2, KD, 512])
        keys = sb("keys", [P, HC, P])
        keysT = sb("keysT", [P, HC, P])
        qT = sb("qT", [P, 2, SEQ])
        sc = sb("sc", [P, TT, 4, P])
        left = sb("left", [P, TT, P])
        top_v = sb("top_v", [P, HC, TT, TOPK])
        top_i = sb("top_i", [P, HC, TT, TOPK], U32)
        top_f = sb("top_f", [P, 2, 2, TT, TOPK])
        cand = sb("cand", [P, TT, TOPK * TOPK])
        rest = sb("rest", [P, TT, TOPK * TOPK])
        best = sb("best", [P, TT, PH, TOPK])
        best_i = sb("best_i", [P, TT, PH, TOPK], U32)
        ab = sb("ab", [P, 2, TT, TOPK], U32)
        abf = sb("abf", [P, 2, 2, TT, TOPK])
        eq = sb("eq", [P, 2, 2, TT, TOPK, TOPK])
        iota16 = sb("iota16", [P, TOPK])
        i12 = sb("i12", [P, 2, TT, PH, TOPK])
        e = sb("e", [P, TT, PH, TOPK])
        z = sb("z", [P, TT, PH])
        rz = sb("rz", [P, TT, PH])
        g16 = sb("g16", [P, SEQ], F16)
        gT = sb("gT", [P, SEQ])
        block = st.enter_context(nc.Block())

        @block.sync
        def _(sp):
            sp.dma_start(keys[:], sub_keys.rearrange("h c k d -> k (h c) d")).then_inc(S["keys"], 16)
            for g in range(4):
                if g >= 2:
                    sp.wait_ge(S["q"], 4 * (g - 1))
                sp.dma_start(w[:, g % 2], w_q[:, g * 512:(g + 1) * 512].rearrange("(k p) n -> p k n", p=P)) \
                    .then_inc(S[f"w{g % 2}"], 16)

        @block.tensor
        def _(pe):
            pe.wait_ge(S["keys"], 16)
            for g in range(4):
                for j in range(4):
                    last = pe.transpose(c.ps[g][:, j * P:(j + 1) * P], keys[:, 4 * g + j, :], c.ident[:])
                last.then_inc(S["keysT"], 1)

            def scores(n):
                pe.wait_ge(S["q_out"], n + 1)
                if n == 0:
                    pe.wait_ge(S["keysT_out"], 4)
                if n >= 2:
                    pe.wait_ge(S["sc_out"], n - 1)
                for t in range(TT):
                    last = pe.matmul(c.ps[6 + n % 2][:, t * P:(t + 1) * P], qT[:, n % 2, t * P:(t + 1) * P],
                                     keysT[:, n, :], start=True, stop=True)
                last.then_inc(S["sc"], 1)

            for n in range(HC):
                if n % 4 == 0:
                    pe.wait_ge(S[f"w{n // 4 % 2}"], 16 * (n // 8 + 1))
                if n >= 2:
                    pe.wait_ge(S["q_out"], n - 1)
                for k in range(KD):
                    last = pe.matmul(c.ps[4 + n % 2][:], w[:, n // 4 % 2, k, n % 4 * P:(n % 4 + 1) * P], hT[:, k, :],
                                     start=(k == 0), stop=(k == KD - 1))
                last.then_inc(S["q"], 1)
                if n >= 1:
                    scores(n - 1)
            scores(HC - 1)
            pe.wait_ge(S["chain"], done["weigh", 0])
            for s, src in enumerate((i12[:, 0], i12[:, 1], e)):
                for t in range(TT):
                    last = pe.transpose(c.ps[s][:, t * P:(t + 1) * P], src[:, t].rearrange("p h k -> p (h k)"),
                                        c.ident[:])
                last.then_inc(S["turn"], 1)

        @block.scalar
        def _(act):
            for g in range(4):
                act.wait_ge(S["keysT"], g + 1)
                act.activation(keysT[:, 4 * g:4 * g + 4, :], c.ps[g][:].rearrange("p (j k) -> p j k", j=4),
                               ACT.Copy).then_inc(S["keysT_out"], 1)
            for n in range(HC + 1):
                if n < HC:
                    act.wait_ge(S["q"], n + 1)
                    if n >= 2:
                        act.wait_ge(S["sc"], n - 1)
                    act.activation(qT[:, n % 2, :], c.ps[4 + n % 2][:], ACT.Copy).then_inc(S["q_out"], 1)
                if n >= 1:
                    m = n - 1
                    act.wait_ge(S["sc"], m + 1)
                    if m >= 4:
                        act.wait_ge(S["chain"], done["max2", m - 4])
                    act.activation(sc[:, :, m % 4, :], c.ps[6 + m % 2][:].rearrange("p (t k) -> p t k", t=TT),
                                   ACT.Copy).then_inc(S["sc_out"], 1)
            act.wait_ge(S["chain"], done["sub", 0])
            act.activation(e[:], e[:], ACT.Exp).then_inc(S["exp"], 1)

        @block.gpsimd
        def _(pool):
            pool.iota(iota16[:], [[1, TOPK]], base=0, channel_multiplier=0,
                      allow_small_or_imprecise_dtypes=True).then_inc(S["place"], 1)
            for h in range(PH):
                pool.wait_ge(S["chain"], done["eq", h])
                for s in range(2):
                    pool.tensor_tensor(eq[:, h % 2, s], eq[:, h % 2, s],
                                       bc(top_f[:, h % 2, s].unsqueeze(2), [P, TT, TOPK, TOPK]),
                                       ALU.mult).then_inc(S["onehot"], 1)

        @block.vector
        def _(dve):
            chain = S["chain"]
            dve.wait_ge(S["place"], 1)

            def gather(h):
                dve.wait_ge(S["onehot"], 2 * h + 2)
                dve.tensor_reduce(i12[:, 0, :, h, :], eq[:, h % 2, 0], X, ALU.add)
                dve.tensor_reduce(i12[:, 1, :, h, :], eq[:, h % 2, 1], X, ALU.add).then_inc(chain, 1)

            for n in range(HC):
                s = sc[:, :, n % 4, :]
                dve.wait_ge(S["sc_out"], n + 1)
                for t in range(TT):
                    last = dve.max(top_v[:, n, t, 0:8], s[:, t, :])
                last.then_inc(chain, 1)
                dve.wait_ge(chain, done["max", n])
                for t in range(TT):
                    last = dve.match_replace(left[:, t, :], top_v[:, n, t, 0:8], s[:, t, :], -BIG)
                last.then_inc(chain, 1)
                dve.wait_ge(chain, done["strike", n])
                for t in range(TT):
                    dve.max(top_v[:, n, t, 8:16], left[:, t, :])
                    last = dve.max_index(top_i[:, n, t, 0:8], top_v[:, n, t, 0:8], s[:, t, :])
                last.then_inc(chain, 1)
                dve.wait_ge(chain, done["max2", n])
                for t in range(TT):
                    last = dve.max_index(top_i[:, n, t, 8:16], top_v[:, n, t, 8:16], left[:, t, :])
                last.then_inc(chain, 1)
                dve.wait_ge(chain, done["index2", n])
                dve.tensor_copy(top_f[:, n // 2 % 2, n % 2], top_i[:, n]).then_inc(chain, 1)
                if n % 2 == 0:
                    continue
                h = n // 2
                dve.tensor_tensor(cand[:].rearrange("p t (a b) -> p t a b", a=TOPK),
                                  bc(top_v[:, n - 1].unsqueeze(3), [P, TT, TOPK, TOPK]),
                                  bc(top_v[:, n].unsqueeze(2), [P, TT, TOPK, TOPK]), ALU.add).then_inc(chain, 1)
                dve.wait_ge(chain, done["cand", h])
                for t in range(TT):
                    last = dve.max(best[:, t, h, 0:8], cand[:, t, :])
                last.then_inc(chain, 1)
                dve.wait_ge(chain, done["bmax", h])
                for t in range(TT):
                    last = dve.match_replace(rest[:, t, :], best[:, t, h, 0:8], cand[:, t, :], -BIG)
                last.then_inc(chain, 1)
                dve.wait_ge(chain, done["bstrike", h])
                for t in range(TT):
                    dve.max(best[:, t, h, 8:16], rest[:, t, :])
                    last = dve.max_index(best_i[:, t, h, 0:8], best[:, t, h, 0:8], cand[:, t, :])
                last.then_inc(chain, 1)
                dve.wait_ge(chain, done["bmax2", h])
                for t in range(TT):
                    last = dve.max_index(best_i[:, t, h, 8:16], best[:, t, h, 8:16], rest[:, t, :])
                last.then_inc(chain, 1)
                dve.wait_ge(chain, done["bindex2", h])
                dve.tensor_scalar(ab[:, 0], best_i[:, :, h, :], 4, None, ALU.logical_shift_right)
                dve.tensor_scalar(ab[:, 1], best_i[:, :, h, :], TOPK - 1, None, ALU.bitwise_and).then_inc(chain, 1)
                dve.wait_ge(chain, done["split", h])
                dve.tensor_copy(abf[:, h % 2], ab[:]).then_inc(chain, 1)
                dve.wait_ge(chain, done["split_float", h])
                for s in range(2):
                    last = dve.tensor_tensor(eq[:, h % 2, s], bc(abf[:, h % 2, s].unsqueeze(3), [P, TT, TOPK, TOPK]),
                                             bc(iota16[:].unsqueeze(1).unsqueeze(1), [P, TT, TOPK, TOPK]),
                                             ALU.is_equal)
                last.then_inc(chain, 1)
                if h >= 1:
                    gather(h - 1)
            gather(PH - 1)
            b3, e3 = best[:].rearrange("p t h k -> p (t h) k"), e[:].rearrange("p t h k -> p (t h) k")
            z2, rz2 = z[:].rearrange("p t h -> p (t h)"), rz[:].rearrange("p t h -> p (t h)")
            dve.tensor_tensor(e3, b3, bc(b3[:, :, 0:1], [P, TT * PH, TOPK]), ALU.subtract).then_inc(chain, 1)
            dve.wait_ge(S["exp"], 1)
            dve.tensor_reduce(z2, e3, X, ALU.add).then_inc(chain, 1)
            dve.wait_ge(chain, done["sum", 0])
            dve.reciprocal(rz2, z2).then_inc(chain, 1)
            dve.wait_ge(chain, done["recip", 0])
            dve.scalar_tensor_tensor(e3, e3, GSCALE, bc(rz2.unsqueeze(2), [P, TT * PH, TOPK]), ALU.mult,
                                     ALU.mult).then_inc(chain, 1)
            for s in range(2):
                dve.wait_ge(S["turn"], s + 1)
                dve.tensor_copy(picks[s][:], c.ps[s][:])
            dve.wait_ge(S["turn"], 3)
            dve.tensor_copy(gT[:], c.ps[2][:]).then_inc(chain, 1)
            dve.wait_ge(chain, len(steps) + 1)
            dve.tensor_copy(g16[:], gT[:]).then_inc(chain, 1)
            dve.wait_ge(chain, len(steps) + 2)
            dve.tensor_copy(gates[0][:], g16[:]).then_inc(chain, 1)
            dve.wait_ge(chain, len(steps) + 3)
            dve.tensor_tensor(gates[1][:], gT[:], gates[0][:], ALU.subtract).then_inc(chain, 1)


BATCH = 8
STAGE = 128


def peer_gates(c, name, picks, gates, G):
    nc = c.nc
    made, summed, staged = (c.sem(f"{name}_{s}") for s in ("made", "summed", "staged"))
    iota_made = c.sem(f"{name}_iota_made")
    stored = [c.sem(f"{name}_stored{i}") for i in range(2)]
    PER = 4
    with ExitStack() as st:
        def sb(n, shape, dt=F32):
            return st.enter_context(nc.sbuf_tensor(f"{name}_{n}", shape, dt))

        iota = sb("iota", [P, NK], F16)
        A = sb("A", [P, 2, BATCH, NK], F16)
        B1 = sb("B1", [P, 2, BATCH, NK], F16)
        B2 = sb("B2", [P, 2, BATCH, NK], F16)
        stage = sb("stage", [P, 2, NK, STAGE])
        block = st.enter_context(nc.Block())
        SB = STAGE // BATCH
        QB = BATCH // PER

        @block.gpsimd
        def _(pool):
            pool.iota(iota[:], [[1, NK]], base=0, channel_multiplier=0,
                      allow_small_or_imprecise_dtypes=True).then_inc(iota_made, 1)

        @block.vector
        def _(dve):
            dve.wait_ge(iota_made, 1)

            def batch(b, half, wait):
                if wait:
                    dve.wait_ge(summed, (b - 1) * QB)
                for j in range(BATCH):
                    t = bass.ds(b * BATCH + j, 1)
                    dve.tensor_scalar(A[:, half, j, :], iota[:], picks[0][:, t], 1.0 / GSCALE, ALU.is_equal,
                                      ALU.mult)
                    dve.tensor_scalar(B1[:, half, j, :], iota[:], picks[1][:, t], gates[0][:, t], ALU.is_equal,
                                      ALU.mult)
                    last = dve.tensor_scalar(B2[:, half, j, :], iota[:], picks[1][:, t], gates[1][:, t],
                                             ALU.is_equal, ALU.mult)
                last.then_inc(made, 1)

            batch(0, 0, False)
            batch(1, 1, False)
            with dve.Fori(1, SEQ // BATCH // 2) as i:
                for half in range(2):
                    batch(2 * i + half, half, True)

        @block.tensor
        def _(pe):
            def batch(b, half, banks, wait):
                pe.wait_ge(made, b + 1)
                for q in range(QB):
                    if wait:
                        pe.wait_ge(staged, b * QB + q - 7)
                    for j in range(PER):
                        o = c.ps[banks + q][:, j * NK:(j + 1) * NK]
                        a = A[:, half, q * PER + j, :]
                        pe.matmul(o, a, B1[:, half, q * PER + j, :], start=True, stop=False)
                        last = pe.matmul(o, a, B2[:, half, q * PER + j, :], start=False, stop=True)
                    last.then_inc(summed, 1)

            def batches(first, wait):
                for r in range(8 // QB):
                    batch(first + r, r % 2, r * QB, wait)

            batches(0, False)
            with pe.Fori(1, SEQ // BATCH // (8 // QB)) as i:
                batches(i * (8 // QB), True)

        @block.scalar
        def _(act):
            for s in range(SEQ // STAGE):
                if s >= 2:
                    act.wait_ge(stored[s % 2], 16 * (s // 2))
                with act.Fori(0, STAGE // PER // 8) as i:
                    for q in range(8):
                        act.wait_ge(summed, s * (STAGE // PER) + 8 * i + q + 1)
                        act.activation(stage[:, s % 2, :, bass.ds((8 * i + q) * PER, PER)],
                                       c.ps[q][:].rearrange("p (t k) -> p k t", t=PER), ACT.Copy).then_inc(staged, 1)

        @block.sync
        def _(sp):
            for s in range(SEQ // STAGE):
                sp.wait_ge(staged, (s + 1) * (STAGE // PER))
                sp.dma_start(G[:, :, s * STAGE:(s + 1) * STAGE], stage[:, s % 2]).then_inc(stored[s % 2], 16)
            for s in range(2):
                sp.wait_ge(stored[s], 16 * (SEQ // STAGE // 2))


def peer_dense(c, name, hi, lo, G, u_tab, v_tab):
    nc = c.nc
    S = {s: c.sem(f"{name}_{s}") for s in (
        "u0", "u1", "v0", "v1", "g0", "g1", "turned", "u_hi", "u_lo", "act", "gelu", "w", "w_hi", "w_lo", "v_hi",
        "v_lo", "out", "added")}
    GRP = 4
    NS = NK
    TURN, ACTB, OUTB = 0, 2, 4
    with ExitStack() as st:
        def sb(n, shape, dt=F32):
            return st.enter_context(nc.sbuf_tensor(f"{name}_{n}", shape, dt))

        u = sb("u", [P, 2, 2, D])
        v = sb("v", [P, 2, GRP, 512])
        g = sb("g", [P, 2, 2, SEQ])
        u_hi, u_lo = sb("u_hi", [P, 2, KD, P], F32R), sb("u_lo", [P, 2, KD, P], F32R)
        v_hi, v_lo = sb("v_hi", [P, 2, GRP, 512], F32R), sb("v_lo", [P, 2, GRP, 512], F32R)
        w_hi, w_lo = sb("w_hi", [P, 2, GRP, SEQ], F32R), sb("w_lo", [P, 2, GRP, SEQ], F32R)
        a = sb("a", [P, 2, SEQ])
        w = sb("w", [P, 2, SEQ])
        block = st.enter_context(nc.Block())
        uv = u_tab.rearrange("(i j) d -> i j d", i=P)
        vv = v_tab.rearrange("(i j) d -> i j d", i=P)

        LOOPS = NS // 8

        def before(i, r, n):
            return isinstance(i, int) and 8 * i + r < n

        def after(i, r, by=1):
            return (i, r + by) if r + by < 8 else (i + 1, r + by - 8)

        @block.sync
        def _(sp):
            def loads(i, r, free):
                s = 2 * i + r
                if free:
                    sp.wait_ge(S["turned"], 4 * s - 4)
                sp.dma_start(u[:, r], uv[:, bass.ds(s * 2, 2), :]).then_inc(S[f"u{r}"], 16)
                if free:
                    sp.wait_ge(S["w"], 2 * s - 2)
                sp.dma_start(g[:, r], G[:, bass.ds(s * 2, 2), :]).then_inc(S[f"g{r}"], 16)
                if free:
                    sp.wait_ge(S["v_hi"], 2 * s - 2)
                    sp.wait_ge(S["v_lo"], 2 * s - 2)
                sp.dma_start(v[:, r], vv[:, bass.ds(i * GRP, GRP), r * 512:(r + 1) * 512]) \
                    .then_inc(S[f"v{r}"], 16)

            loads(0, 0, False)
            loads(0, 1, False)
            with sp.Fori(1, NS // GRP) as i:
                for r in range(2):
                    loads(i, r, True)

        @block.tensor
        def _(pe):
            def turn(i, r):
                if r % 2 == 0:
                    pe.wait_ge(S[f"u{r // 2 % 2}"], 16 * (2 * i + r // 4 + 1))
                for b in range(2):
                    for k in range(4):
                        last = pe.transpose(c.ps[TURN + b][:, k * P:(k + 1) * P],
                                            u[:, r // 2 % 2, r % 2, (4 * b + k) * P:(4 * b + k + 1) * P], c.ident[:])
                    last.then_inc(S["turned"], 1)

            def activations(i, r):
                if not before(i, r, 2):
                    pe.wait_ge(S["gelu"], 8 * i + r - 1)
                o = c.ps[ACTB + r % 2]
                for k in range(KD):
                    uh, ul = u_hi[:, r % 2, k, :], u_lo[:, r % 2, k, :]
                    pe.matmul(o[:], uh, hi[:, k, :], start=(k == 0), stop=False)
                    pe.matmul(o[:], uh, lo[:, k, :], start=False, stop=False)
                    last = pe.matmul(o[:], ul, hi[:, k, :], start=False, stop=(k == KD - 1))
                last.then_inc(S["act"], 1)

            def outputs(i, r):
                n = 8 * i + r
                q2, grp2 = r // 2 % 2, (r // 4 + 1) % 2
                if r % 4 == 0:
                    pe.wait_ge(S["w_hi"], n)
                    pe.wait_ge(S["w_lo"], n)
                if r % 2 == 0:
                    pe.wait_ge(S["v_hi"], n - 2)
                    pe.wait_ge(S["v_lo"], n - 2)
                for m in range(2):
                    t = 2 * (r % 2) + m
                    b = c.ps[OUTB + t]
                    if not before(i, r, GRP + 2):
                        pe.wait_ge(S["added"], 2 * n + m - 2 * GRP - 3)
                    for j in range(GRP):
                        wh, wl = w_hi[:, grp2, j, t * P:(t + 1) * P], w_lo[:, grp2, j, t * P:(t + 1) * P]
                        pe.matmul(b[:], wh, v_hi[:, q2, j, :], start=(j == 0), stop=False)
                        pe.matmul(b[:], wh, v_lo[:, q2, j, :], start=False, stop=False)
                        last = pe.matmul(b[:], wl, v_hi[:, q2, j, :], start=False, stop=(j == GRP - 1))
                    last.then_inc(S["out"], 1)

            def step(i, r, turn_next=True):
                pe.wait_ge(S["u_hi"], 2 * (8 * i + r) + 2)
                pe.wait_ge(S["u_lo"], 2 * (8 * i + r) + 2)
                if turn_next:
                    turn(*after(i, r))
                activations(i, r)
                if not before(i, r, GRP):
                    outputs(i, r)

            turn(0, 0)
            for r in range(8):
                step(0, r)
            with pe.Fori(1, LOOPS - 1) as i:
                for r in range(8):
                    step(i, r)
            for r in range(8):
                step(LOOPS - 1, r, turn_next=(r < 7))
            for r in range(GRP):
                outputs(LOOPS, r)

        @block.scalar
        def _(act):
            def split_u(i, r):
                n = 8 * i + r
                if not before(i, r, 2):
                    act.wait_ge(S["act"], n - 1)
                for b in range(2):
                    act.wait_ge(S["turned"], 2 * n + b + 1)
                    act.activation(u_hi[:, r % 2, 4 * b:4 * b + 4, :].rearrange("p k i -> p (k i)"),
                                   c.ps[TURN + b][:], ACT.Copy).then_inc(S["u_hi"], 1)

            def split_v(i, r):
                s2 = r // 2 % 2
                if r % 2 == 0:
                    act.wait_ge(S[f"v{s2}"], 16 * (2 * i + r // 4 + 1))
                    if not before(i, r, 4):
                        act.wait_ge(S["out"], 2 * (8 * i + r) - 4)
                j = 2 * (r % 2)
                act.activation(v_hi[:, s2, j:j + 2, :], v[:, s2, j:j + 2, :], ACT.Copy).then_inc(S["v_hi"], 1)

            def step(i, r, split_next=True):
                n = 8 * i + r
                if split_next:
                    split_u(*after(i, r))
                if not before(i, r, 2):
                    split_v(i, r - 2) if r >= 2 else split_v(i - 1, r + 6)
                act.wait_ge(S["act"], n + 1)
                if not before(i, r, 2):
                    act.wait_ge(S["w"], n - 1)
                act.activation(a[:, r % 2, :], c.ps[ACTB + r % 2][:], ACT.Gelu).then_inc(S["gelu"], 1)
                act.wait_ge(S["w"], n + 1)
                if r % 4 == 0 and not before(i, r, 8):
                    act.wait_ge(S["out"], 2 * n - 8)
                act.activation(w_hi[:, r // 4, r % 4, :], w[:, r % 2, :], ACT.Copy).then_inc(S["w_hi"], 1)

            split_u(0, 0)
            for r in range(8):
                step(0, r)
            with act.Fori(1, LOOPS - 1) as i:
                for r in range(8):
                    step(i, r)
            for r in range(8):
                step(LOOPS - 1, r, split_next=(r < 7))
            for r in range(6, 8):
                split_v(LOOPS - 1, r)

        @block.gpsimd
        def _(pool):
            with pool.Fori(0, LOOPS) as i:
                for r in range(8):
                    s2, j = r // 2 % 2, 2 * (r % 2)
                    pool.wait_ge(S["v_hi"], 8 * i + r + 1)
                    pool.tensor_tensor(v_lo[:, s2, j:j + 2, :], v[:, s2, j:j + 2, :],
                                       v_hi[:, s2, j:j + 2, :].bitcast(F32), ALU.subtract).then_inc(S["v_lo"], 1)

        @block.vector
        def _(dve):
            def split_u(i, r):
                for b in range(2):
                    dve.wait_ge(S["u_hi"], 2 * (8 * i + r) + b + 1)
                    part = slice(4 * b, 4 * b + 4)
                    dve.tensor_tensor(u_lo[:, r % 2, part, :].rearrange("p k i -> p (k i)"), c.ps[TURN + b][:],
                                      u_hi[:, r % 2, part, :].rearrange("p k i -> p (k i)").bitcast(F32),
                                      ALU.subtract).then_inc(S["u_lo"], 1)

            def weigh(i, r):
                n = 8 * i + r
                dve.wait_ge(S["gelu"], n + 1)
                if r % 2 == 0:
                    dve.wait_ge(S[f"g{r // 2 % 2}"], 16 * (2 * i + r // 4 + 1))
                if not before(i, r, 2):
                    dve.wait_ge(S["w_lo"], n - 1)
                dve.tensor_tensor(w[:, r % 2, :], a[:, r % 2, :], g[:, r // 2 % 2, r % 2, :],
                                  ALU.mult).then_inc(S["w"], 1)
                dve.wait_ge(S["w_hi"], n + 1)
                dve.tensor_tensor(w_lo[:, r // 4, r % 4, :], w[:, r % 2, :],
                                  w_hi[:, r // 4, r % 4, :].bitcast(F32), ALU.subtract).then_inc(S["w_lo"], 1)

            def add_out(i, r):
                n = 8 * i + r
                for m in range(2):
                    t = 2 * (r % 2) + m
                    dve.wait_ge(S["out"], 2 * n + m - 2 * GRP + 1)
                    if not before(i, r, 2 * GRP):
                        dve.wait_ge(S["added"], 2 * n + m - 2 * GRP - 7)
                    o = c.h[:, t, r // 2 % 2 * 512:(r // 2 % 2 + 1) * 512]
                    dve.tensor_tensor(o, c.ps[OUTB + t][:], o, ALU.add).then_inc(S["added"], 1)

            def step(i, r, split_next=True):
                if split_next:
                    split_u(*after(i, r))
                weigh(i, r)
                if not before(i, r, GRP):
                    add_out(i, r)

            split_u(0, 0)
            for r in range(8):
                step(0, r)
            with dve.Fori(1, LOOPS - 1) as i:
                for r in range(8):
                    step(i, r)
            for r in range(8):
                step(LOOPS - 1, r, split_next=(r < 7))
            for r in range(GRP):
                add_out(LOOPS, r)


def final_norm(c, gain, out):
    nc = c.nc
    gain_loaded, squares, scale, normed, stored = (
        c.sem(f"final_{s}") for s in ("gain", "squares", "scale", "normed", "stored"))
    with ExitStack() as st:
        g = st.enter_context(nc.sbuf_tensor("final_gain", [P, D], F32))
        o = st.enter_context(nc.sbuf_tensor("final_o", [P, TT, D], F32))
        ss = st.enter_context(nc.sbuf_tensor("final_ss", [P, TT], F32))
        ms = st.enter_context(nc.sbuf_tensor("final_ms", [P, TT], F32))
        std = st.enter_context(nc.sbuf_tensor("final_std", [P, TT], F32))
        r = st.enter_context(nc.sbuf_tensor("final_r", [P, TT], F32))
        block = st.enter_context(nc.Block())

        @block.sync
        def _(sp):
            sp.dma_start(g[:], gain.partition_broadcast(P)).then_inc(gain_loaded, 16)
            for t in range(TT):
                sp.wait_ge(normed, t + 1)
                sp.dma_start(out[0, t * P:(t + 1) * P, :], o[:, t, :]).then_inc(stored, 16)
            sp.wait_ge(stored, 16 * TT)

        @block.scalar
        def _(act):
            for t in range(TT):
                act.activation(o[:, t, :], c.h[:, t, :], ACT.Square, accum_out=ss[:, t:t + 1]).then_inc(squares, 1)
            act.wait_ge(scale, 1)
            act.activation(std[:], ms[:], ACT.Sqrt).then_inc(squares, 1)

        @block.vector
        def _(dve):
            dve.wait_ge(squares, TT)
            dve.tensor_scalar(ms[:], ss[:], 1.0 / D, EPS, ALU.mult, ALU.add).then_inc(scale, 1)
            dve.wait_ge(squares, TT + 1)
            dve.reciprocal(r[:], std[:]).then_inc(scale, 1)
            dve.wait_ge(scale, 2)
            dve.wait_ge(gain_loaded, 16)
            for t in range(TT):
                dve.scalar_tensor_tensor(o[:, t, :], c.h[:, t, :], r[:, t:t + 1], g[:], ALU.mult,
                                         ALU.mult).then_inc(normed, 1)


def peer(c, name, gain, w_q, sub_keys, u_tab, v_tab, G):
    nc = c.nc
    with ExitStack() as st:
        def sb(n, shape, dt=F32):
            return st.enter_context(nc.sbuf_tensor(f"{name}_{n}", shape, dt))
        hi, lo = sb("hn_hi", [P, KD, SEQ], F32R), sb("hn_lo", [P, KD, SEQ], F32R)
        with ExitStack() as st2:
            picks = [st2.enter_context(nc.sbuf_tensor(f"{name}_picks{i}", [P, SEQ], F32)) for i in range(2)]
            gates = [st2.enter_context(nc.sbuf_tensor(f"{name}_gates{i}", [P, SEQ], F32)) for i in range(2)]
            with nc.sbuf_tensor(f"{name}_hT", [P, KD, SEQ], F32) as hT:
                norm_block(c, f"{name}_norm", gain, hT, (hi, lo))
                peer_pick(c, f"{name}_pick", hT, w_q, sub_keys, picks, gates)
            peer_gates(c, f"{name}_gate", picks, gates, G)
        peer_dense(c, f"{name}_dense", hi, lo, G, u_tab, v_tab)


def trunk(nc, A, out, stages=("even", "peer0", "odd", "peer1", "final")):
    ctx = ExitStack()
    with ctx:
        c = Core(nc, ctx)
        G = nc.dram_tensor("gate_matrix", (P, NK, SEQ), F32).ap()
        constants(c, A["x"])
        for s in stages:
            if s == "even":
                even_layer(c, A)
            if s == "odd":
                odd_layer(c, A)
            if s[:4] == "peer":
                i = int(s[4])
                peer(c, s, A["ffn_norm_g"][i], A["peer_w_q"][i], A["peer_sub_keys"][i], A["peer_u"][i],
                     A["peer_v"][i], G)
            if s == "final":
                final_norm(c, A["final_g"], out)
            c.end_layer()


_INS = ["x", "even_norm_g", "even_w_in", "even_b_f", "even_cmp_pos", "even_w_cmp_k", "even_w_cmp_v", "even_w_out",
        "odd_norm_g", "odd_w_in", "odd_conv_w", "odd_conv_b", "odd_w_ra", "odd_b_ra", "odd_w_ri", "odd_b_ri",
        "odd_lam", "odd_w_out", "ffn_norm_g", "peer_w_q", "peer_sub_keys", "peer_u", "peer_v", "final_g"]


def kernel(**inputs):
    import numpy as _np
    import concourse.bacc as _bacc
    from concourse import mybir as _mybir
    from concourse.bass_utils import run_bass_kernel_spmd as _run

    nc = _bacc.Bacc("TRN2", target_bir_lowering=False, num_devices=1)
    arrays, args = {}, {}
    for name in _INS:
        a = _np.ascontiguousarray(inputs[name])
        arrays[f"in_{name}_dram"] = a
        args[name] = nc.dram_tensor(f"in_{name}_dram", a.shape, _mybir.dt.from_np(a.dtype), kind="ExternalInput").ap()
    out = nc.dram_tensor("out_0_dram", (1, SEQ, D), F32, kind="ExternalOutput").ap()
    trunk(nc, args, out)
    r = _run(nc, [arrays], core_ids=[0])
    return r.results[0]["out_0_dram"]
```

```python
from contextlib import ExitStack

import concourse.bass as bass
from concourse import mybir

ALU = mybir.AluOpType
ACT = mybir.ActivationFunctionType
X = mybir.AxisListType.X
F32 = mybir.dt.float32
F32R = mybir.dt.float32r
F16 = mybir.dt.float16
U32 = mybir.dt.uint32

P = 128
SEQ = 512
TT = SEQ // P
D = 1024
KD = D // P
EPS = 1e-6
NEG = -1.0e30
BIG = 3.0e38

DH = 64
NH = 8
GROUPS = 2
CMP_LEN = 32
CMP_STRIDE = 16
N_CMP = (SEQ - CMP_LEN) // CMP_STRIDE + 1
FOX_QKV = 3 * NH * DH
EVEN_IN = FOX_QKV + NH + NH * DH + 6 * GROUPS * DH + 3 * NH
HALF_ROW = SEQ - P

D_RNN = 1280
NR = D_RNN // P
CONV_W = 4

PH = 8
NK = 128
TOPK = 16
HC = 2 * PH
GSCALE = 2.0 ** 14


def bc(ap, shape):
    return ap.to_broadcast(shape)


class Core:

    def __init__(self, nc, ctx):
        self.nc = nc
        self.sems = []
        self.h = ctx.enter_context(nc.sbuf_tensor("h", [P, TT, D], F32))
        self.ident = ctx.enter_context(nc.sbuf_tensor("ident", [P, P], F32))
        self.ps = [ctx.enter_context(nc.psum_tensor(f"bank{i}", [P, 512], F32)) for i in range(8)]

    def sem(self, name):
        self.sems.append(self.nc.alloc_semaphore(name=name))
        return self.sems[-1]

    def end_layer(self):
        self.nc.clear_and_free_semaphores(self.sems)
        self.nc.all_engine_barrier()
        self.sems = []


def constants(c, x):
    nc = c.nc
    x_loaded, ident_made = c.sem("x_loaded"), c.sem("ident_made")
    with nc.Block() as block:
        @block.sync
        def _(sp):
            sp.dma_start(c.h[:], x[0].rearrange("(t p) d -> p t d", p=P)).then_inc(x_loaded, 16)
            sp.wait_ge(x_loaded, 16)

        @block.gpsimd
        def _(pool):
            pool.memset(c.ident[:], 1.0).then_inc(ident_made, 1)
            pool.wait_ge(ident_made, 1)
            pool.affine_select(out=c.ident[:], in_=c.ident[:], compare_op=ALU.is_equal, fill=0.0, base=0,
                               pattern=[[-1, P]], channel_multiplier=1).then_inc(ident_made, 1)


def norm_block(c, name, gain, hi, lo):
    nc = c.nc
    S = {s: c.sem(f"{name}_{s}") for s in ("gain", "sq_a", "sq_v", "scale", "root", "scaled_a", "scaled_v", "turned",
                                           "hi")}
    with ExitStack() as st:
        gT = st.enter_context(nc.sbuf_tensor(f"{name}_gT", [P, KD], F32))
        hn = st.enter_context(nc.sbuf_tensor(f"{name}_hn", [P, TT, D], F32))
        ss, ms, std, r, r2 = (st.enter_context(nc.sbuf_tensor(f"{name}_{n}", [P, TT], F32))
                              for n in ("ss", "ms", "std", "r", "r2"))
        block = st.enter_context(nc.Block())

        @block.sync
        def _(sp):
            sp.dma_start(gT[:], gain.rearrange("(k p) -> p k", p=P),
                         allow_slow_non_contiguous=True).then_inc(S["gain"], 16)

        NEWTON = 6

        @block.scalar
        def _(act):
            for t in (0, 2):
                act.activation(hn[:, t, :], c.h[:, t, :], ACT.Square, accum_out=ss[:, t:t + 1]).then_inc(S["sq_a"], 1)
            act.wait_ge(S["scale"], 1)
            act.activation(std[:], ms[:], ACT.Sqrt).then_inc(S["root"], 1)
            act.wait_ge(S["scale"], NEWTON)
            for t in (0, 2):
                act.activation(hn[:, t, :], c.h[:, t, :], ACT.Copy, scale=r[:, t:t + 1]).then_inc(S["scaled_a"], 1)
            act.wait_ge(S["gain"], 16)
            for k in range(KD):
                act.wait_ge(S["turned"], k + 1)
                act.activation(hi[:, k, :], c.ps[k][:], ACT.Copy, scale=gT[:, k:k + 1]).then_inc(S["hi"], 1)

        @block.vector
        def _(dve):
            for t in (1, 3):
                dve.tensor_tensor_reduce(hn[:, t, :], c.h[:, t, :], c.h[:, t, :], 1.0, 0.0, ALU.mult, ALU.add,
                                         ss[:, t:t + 1]).then_inc(S["sq_v"], 1)
            dve.wait_ge(S["sq_a"], 2)
            dve.wait_ge(S["sq_v"], 2)
            dve.tensor_scalar(ms[:], ss[:], 1.0 / D, EPS, ALU.mult, ALU.add).then_inc(S["scale"], 1)
            dve.wait_ge(S["root"], 1)
            dve.reciprocal(r[:], std[:]).then_inc(S["scale"], 1)
            dve.wait_ge(S["scale"], 2)
            dve.tensor_tensor(r2[:], r[:], r[:], ALU.mult).then_inc(S["scale"], 1)
            dve.wait_ge(S["scale"], 3)
            dve.scalar_tensor_tensor(r2[:], r2[:], -0.5, ms[:], ALU.mult, ALU.mult).then_inc(S["scale"], 1)
            dve.wait_ge(S["scale"], 4)
            dve.scalar_tensor_tensor(r2[:], r2[:], 1.5, r[:], ALU.add, ALU.mult).then_inc(S["scale"], 1)
            dve.wait_ge(S["scale"], 5)
            dve.tensor_copy(r[:], r2[:]).then_inc(S["scale"], 1)
            dve.wait_ge(S["scale"], NEWTON)
            for t in (1, 3):
                dve.tensor_scalar(hn[:, t, :], c.h[:, t, :], r[:, t:t + 1], None, ALU.mult).then_inc(S["scaled_v"], 1)
            for k in range(KD):
                dve.wait_ge(S["hi"], k + 1)
                dve.scalar_tensor_tensor(lo[:, k, :], c.ps[k][:], gT[:, k:k + 1], hi[:, k, :].bitcast(F32), ALU.mult,
                                         ALU.subtract)

        @block.tensor
        def _(pe):
            pe.wait_ge(S["scaled_a"], 2)
            pe.wait_ge(S["scaled_v"], 2)
            for k in range(KD):
                for t in range(TT):
                    last = pe.transpose(c.ps[k][:, t * P:(t + 1) * P], hn[:, t, k * P:(k + 1) * P], c.ident[:])
                last.then_inc(S["turned"], 1)


def norm_plain(c, name, gain, hT, split=None):
    nc = c.nc
    gain_loaded, squares, scale, scaled = (c.sem(f"{name}_{s}") for s in ("gain", "squares", "scale", "scaled"))
    turned, out_a, out_v, hi_done = (c.sem(f"{name}_{s}") for s in ("turned", "out_a", "out_v", "hi"))
    with ExitStack() as st:
        gT = st.enter_context(nc.sbuf_tensor(f"{name}_gT", [P, KD], F32))
        hn = st.enter_context(nc.sbuf_tensor(f"{name}_hn", [P, TT, D], F32))
        ss = st.enter_context(nc.sbuf_tensor(f"{name}_ss", [P, TT], F32))
        ms = st.enter_context(nc.sbuf_tensor(f"{name}_ms", [P, TT], F32))
        std = st.enter_context(nc.sbuf_tensor(f"{name}_std", [P, TT], F32))
        r = st.enter_context(nc.sbuf_tensor(f"{name}_r", [P, TT], F32))
        block = st.enter_context(nc.Block())

        @block.sync
        def _(sp):
            sp.dma_start(gT[:], gain.rearrange("(k p) -> p k", p=P),
                         allow_slow_non_contiguous=True).then_inc(gain_loaded, 16)

        @block.scalar
        def _(act):
            for t in range(TT):
                act.activation(hn[:, t, :], c.h[:, t, :], ACT.Square, accum_out=ss[:, t:t + 1]).then_inc(squares, 1)
            act.wait_ge(scale, 1)
            act.activation(std[:], ms[:], ACT.Sqrt).then_inc(squares, 1)
            act.wait_ge(gain_loaded, 16)
            for k in range(1, KD, 2):
                act.wait_ge(turned, k + 1)
                act.activation(hT[:, k, :], c.ps[k][:], ACT.Copy, scale=gT[:, k:k + 1]).then_inc(out_a, 1)
            if split:
                for k in range(KD):
                    if k % 2:
                        act.wait_ge(out_a, k // 2 + 1)
                    else:
                        act.wait_ge(out_v, k // 2 + 1)
                    act.activation(split[0][:, k, :], hT[:, k, :], ACT.Copy).then_inc(hi_done, 1)

        @block.vector
        def _(dve):
            dve.wait_ge(squares, TT)
            dve.tensor_scalar(ms[:], ss[:], 1.0 / D, EPS, ALU.mult, ALU.add).then_inc(scale, 1)
            dve.wait_ge(squares, TT + 1)
            dve.reciprocal(r[:], std[:]).then_inc(scale, 1)
            dve.wait_ge(scale, 2)
            for t in range(TT):
                dve.tensor_scalar(hn[:, t, :], c.h[:, t, :], r[:, t:t + 1], None, ALU.mult).then_inc(scaled, 1)
            dve.wait_ge(gain_loaded, 16)
            for k in range(0, KD, 2):
                dve.wait_ge(turned, k + 1)
                dve.tensor_scalar(hT[:, k, :], c.ps[k][:], gT[:, k:k + 1], None, ALU.mult).then_inc(out_v, 1)
            if split:
                for k in range(KD):
                    dve.wait_ge(hi_done, k + 1)
                    dve.tensor_tensor(split[1][:, k, :], hT[:, k, :], split[0][:, k, :].bitcast(F32), ALU.subtract)

        @block.tensor
        def _(pe):
            pe.wait_ge(scaled, TT)
            for k in range(KD):
                for t in range(TT):
                    last = pe.transpose(c.ps[k][:, t * P:(t + 1) * P], hn[:, t, k * P:(k + 1) * P], c.ident[:])
                last.then_inc(turned, 1)


SERIES = [1 / 15, 1 / 13, 1 / 11, 1 / 9, 1 / 7, 1 / 5, 1 / 3]


def half_log1p(dve, chain, at, e, d, z, q, p):
    dve.tensor_scalar(d, e, 2.0, None, ALU.add).then_inc(chain, 1)
    dve.wait_ge(chain, at + 1)
    dve.reciprocal(q, d).then_inc(chain, 1)
    dve.wait_ge(chain, at + 2)
    dve.tensor_tensor(z, e, q, ALU.mult).then_inc(chain, 1)
    dve.wait_ge(chain, at + 3)
    dve.tensor_tensor(q, z, z, ALU.mult).then_inc(chain, 1)
    dve.wait_ge(chain, at + 4)
    dve.tensor_scalar(p, q, SERIES[0], None, ALU.mult).then_inc(chain, 1)
    n = at + 5
    for coefficient in SERIES[1:]:
        dve.wait_ge(chain, n)
        dve.scalar_tensor_tensor(p, p, coefficient, q, ALU.add, ALU.mult).then_inc(chain, 1)
        n += 1
    dve.wait_ge(chain, n)
    dve.scalar_tensor_tensor(p, p, 1.0, z, ALU.add, ALU.mult).then_inc(chain, 1)
    dve.wait_ge(chain, n + 1)
    return n + 1


def even_project(c, hT, w_in, b_f, R):
    nc = c.nc
    slots = [c.sem(f"proj_w{i}") for i in range(3)]
    bias_in, product, out_a, out_v = (c.sem(f"proj_{s}") for s in ("bias", "product", "out_a", "out_v"))
    GROUPS_W = [(0, 512), (512, 512), (1024, 512), (1536, 8 + 512), (2056, 384), (2440, 384 + 3 * NH)]
    jobs = []
    for m in range(4):
        jobs.append((0, "feature", m * P, (R["Qf"], 2 * m), DH ** -0.5))
    for m in range(4):
        jobs.append((1, "feature", m * P, (R["Kf"], 2 * m), 1.0))
    for t in range(TT):
        jobs.append((2, "fox_v", 0, t, 1.0))
    jobs.append((3, "forget", 0, None, 1.0))
    for m in range(4):
        jobs.append((3, "feature", 8 + m * P, (R["Qn"], 2 * m), DH ** -0.5))
    for m in range(2):
        jobs.append((4, "feature", m * P, (R["Kc"], 2 * m), 1.0))
    jobs.append((4, "feature", 2 * P, (R["Kn"], 0), 1.0))
    jobs.append((5, "feature", P, (R["Kn"], 2), 1.0))
    for t in range(TT):
        jobs.append((5, "nsa_v", 0, t, 1.0))
    group_end = [max(j for j, job in enumerate(jobs) if job[0] == g) + 1 for g in range(6)]
    v_count = [sum(job[1] == "feature" for job in jobs[:j + 1]) for j in range(len(jobs))]
    with ExitStack() as st:
        w = st.enter_context(nc.sbuf_tensor("proj_w", [P, 3, KD, 520], F32))
        bf = st.enter_context(nc.sbuf_tensor("proj_bf", [NH, 1], F32))
        block = st.enter_context(nc.Block())

        @block.sync
        def _(sp):
            sp.dma_start(bf[:], b_f.unsqueeze(1)).then_inc(bias_in, 16)
            for g, (c0, width) in enumerate(GROUPS_W):
                if g >= 3:
                    sp.wait_ge(product, group_end[g - 3])
                sp.dma_start(w[:, g % 3, :, 0:width],
                             w_in[:, c0:c0 + width].rearrange("(k p) n -> p k n", p=P)).then_inc(slots[g % 3], 16)

        @block.tensor
        def _(pe):
            for j, (g, kind, col, where, _) in enumerate(jobs):
                if j == 0 or jobs[j - 1][0] != g:
                    pe.wait_ge(slots[g % 3], 16 * (g // 3 + 1))
                if j >= 8:
                    pe.wait_ge(out_a, j - 7)
                    pe.wait_ge(out_v, v_count[j - 8])
                b = c.ps[j % 8]
                if kind in ("feature", "forget"):
                    m = P if kind == "feature" else NH
                    for k in range(KD):
                        last = pe.matmul(b[0:m, :], w[:, g % 3, k, col:col + m], hT[:, k, :], start=(k == 0),
                                         stop=(k == KD - 1))
                elif kind == "fox_v":
                    for k in range(KD):
                        last = pe.matmul(b[:], hT[:, k, where * P:(where + 1) * P], w[:, g % 3, k, 0:512],
                                         start=(k == 0), stop=(k == KD - 1))
                else:
                    for lo, hi, at in ((0, P, 0), (2 * P, 3 * P + 3 * NH, P)):
                        for k in range(KD):
                            last = pe.matmul(b[:, at:at + hi - lo], hT[:, k, where * P:(where + 1) * P],
                                             w[:, g % 3, k, lo:hi], start=(k == 0), stop=(k == KD - 1))
                last.then_inc(product, 1)

        @block.scalar
        def _(act):
            act.wait_ge(bias_in, 16)
            for j, (g, kind, col, where, scale) in enumerate(jobs):
                act.wait_ge(product, j + 1)
                b = c.ps[j % 8]
                if kind == "feature":
                    last = act.activation(where[0][0:DH, where[1], :], b[0:DH, :], ACT.Copy, scale=scale)
                elif kind == "forget":
                    last = act.activation(R["f"][:], b[0:NH, :], ACT.Identity, bias=bf[:, 0:1])
                elif kind == "fox_v":
                    last = act.activation(R["Vf"][:, where, :], b[:], ACT.Copy)
                else:
                    act.activation(R["Vn"][:, where, :], b[:, 0:2 * P], ACT.Copy)
                    last = act.activation(R["gates"][:, where, :], b[:, 2 * P:2 * P + 3 * NH], ACT.Sigmoid)
                last.then_inc(out_a, 1)

        @block.vector
        def _(dve):
            for j, (g, kind, col, where, scale) in enumerate(jobs):
                if kind == "feature":
                    dve.wait_ge(product, j + 1)
                    dve.tensor_scalar(where[0][0:DH, where[1] + 1, :], c.ps[j % 8][DH:P, :], scale, None,
                                      ALU.mult).then_inc(out_v, 1)

        @block.gpsimd
        def _(pool):
            tables = c.sem("tables")
            pool.iota(R["bias"][:, NH, :], [[-1, SEQ]], base=HALF_ROW, channel_multiplier=1,
                      allow_small_or_imprecise_dtypes=True)
            pool.iota(R["dist_c"][:], [[P, TT], [-CMP_STRIDE, N_CMP]], base=-(CMP_LEN - 1), channel_multiplier=1,
                      allow_small_or_imprecise_dtypes=True).then_inc(tables, 1)
            pool.wait_ge(tables, 1)
            for h in range(NH):
                slope = 2.0 ** (-8.0 * (h + 1) / NH)
                pool.tensor_scalar(R["bias"][:, h, :], R["bias"][:, NH, :], -slope, None, ALU.mult)
                last = pool.tensor_scalar(R["bias_c"][:, h], R["dist_c"][:], -slope, None, ALU.mult)
            last.then_inc(tables, 1)
            pool.wait_ge(tables, 2)
            pool.memset(R["bias"][:, NH, :], 0.0).then_inc(tables, 1)
            pool.wait_ge(tables, 3)
            for h in range(NH + 1):
                pool.affine_select(out=R["bias"][:, h, :], in_=R["bias"][:, h, :], compare_op=ALU.is_ge, fill=NEG,
                                   base=HALF_ROW, pattern=[[-1, SEQ]], channel_multiplier=1)
            for h in range(NH):
                pool.affine_select(out=R["bias_c"][:, h], in_=R["bias_c"][:, h], compare_op=ALU.is_ge, fill=NEG,
                                   base=-(CMP_LEN - 1), pattern=[[P, TT], [-CMP_STRIDE, N_CMP]], channel_multiplier=1)


def even_prepare(c, A, R):
    nc = c.nc
    loaded, rows, padded, summed, product, chain, exps = (
        c.sem(f"prep_{s}") for s in ("loaded", "rows", "padded", "summed", "product", "chain", "exps"))
    with ExitStack() as st:
        def sb(n, shape):
            return st.enter_context(nc.sbuf_tensor(f"prep_{n}", shape, F32))

        wk, wv = sb("wk", [DH, CMP_LEN, DH]), sb("wv", [DH, CMP_LEN, DH])
        pos = sb("pos", [DH, CMP_LEN])
        win = sb("win", [DH, 4, N_CMP, CMP_LEN])
        e, d, z, q, p = (sb(n, [NH, SEQ]) for n in "edzqp")
        low, cum, neg, ones = (sb(n, [NH, SEQ]) for n in ("low", "cum", "neg", "ones"))
        block = st.enter_context(nc.Block())
        f = R["f"]

        @block.sync
        def _(sp):
            sp.dma_start(pos[:], A["even_cmp_pos"][0].rearrange("l d -> d l"),
                         allow_slow_non_contiguous=True).then_inc(loaded, 16)
            sp.dma_start(wk[:], A["even_w_cmp_k"][0].rearrange("l d e -> d l e")).then_inc(loaded, 16)
            sp.dma_start(wv[:], A["even_w_cmp_v"][0].rearrange("l d e -> d l e")).then_inc(loaded, 16)
            sp.wait_ge(padded, 2)
            sp.wait_ge(summed, 1)
            for h in range(NH):
                sp.dma_start(R["Qf"][DH:DH + 1, h, :], cum[h:h + 1, :]).then_inc(rows, 16)
                sp.dma_start(R["Kf"][96:97, h, :], neg[h:h + 1, :]).then_inc(rows, 16)
            sp.wait_ge(rows, 16 * 2 * NH)

        @block.gpsimd
        def _(pool):
            pool.memset(R["Qf"][DH:97, :, :], 0.0)
            pool.memset(R["Kf"][DH:97, :, :], 0.0).then_inc(padded, 1)
            pool.wait_ge(padded, 1)
            pool.memset(R["Qf"][96:97, :, :], 1.0)
            pool.memset(R["Kf"][DH:DH + 1, :, :], 1.0).then_inc(padded, 1)
            pool.wait_ge(padded, 2)
            first = R["gates"][:, 0, :].rearrange("p (h b) -> p h b", b=3)[:, :, 0]
            pool.affine_select(out=first, in_=first, compare_op=ALU.is_ge, fill=0.0, base=-(CMP_LEN - 1),
                               pattern=[[0, NH]], channel_multiplier=1)

        @block.scalar
        def _(act):
            act.activation(e[:], f[:], ACT.Abs).then_inc(exps, 1)
            act.wait_ge(exps, 1)
            act.activation(e[:], e[:], ACT.Exp, scale=-1.0).then_inc(exps, 1)

        @block.vector
        def _(dve):
            dve.memset(ones[:], 1.0)
            dve.tensor_scalar(low[:], f[:], 0.0, None, ALU.min)
            dve.wait_ge(exps, 2)
            n = half_log1p(dve, chain, 0, e[:], d[:], z[:], q[:], p[:])
            dve.scalar_tensor_tensor(low[:], p[:], -2.0, low[:], ALU.mult, ALU.add).then_inc(chain, 1)
            dve.wait_ge(chain, n + 1)
            dve.tensor_tensor_scan(cum[:], ones[:], low[:], 0.0, ALU.mult, ALU.add).then_inc(chain, 1)
            dve.wait_ge(chain, n + 2)
            dve.tensor_scalar(neg[:], cum[:], -1.0, None, ALU.mult).then_inc(summed, 1)
            dve.wait_ge(loaded, 48)
            for s in range(4):
                for half in range(2):
                    a = half * CMP_STRIDE
                    src = R["Kc"][:, s, a:a + N_CMP * CMP_STRIDE].rearrange("p (n b) -> p n b", b=CMP_STRIDE)
                    last = dve.tensor_tensor(win[:, s, :, a:a + CMP_STRIDE], src,
                                             bc(pos[:, a:a + CMP_STRIDE].unsqueeze(1), [DH, N_CMP, CMP_STRIDE]),
                                             ALU.add)
            last.then_inc(summed, 1)
            dve.wait_ge(product, 1)
            dve.tensor_copy(R["kc"][:], c.ps[0][0:DH, 0:GROUPS * N_CMP].rearrange("p (g n) -> p g n", g=GROUPS))
            dve.wait_ge(product, 2)
            dve.tensor_copy(R["vc"][:], c.ps[1][0:N_CMP, 0:GROUPS * DH].rearrange("p (g e) -> p g e", g=GROUPS))

        @block.tensor
        def _(pe):
            pe.wait_ge(summed, 2)
            for m in range(CMP_LEN):
                last = pe.matmul(c.ps[0][0:DH, 0:GROUPS * N_CMP], wk[:, m, :], win[:, 0:2, :, m], start=(m == 0),
                                 stop=(m == CMP_LEN - 1))
            last.then_inc(product, 1)
            for g in range(GROUPS):
                for m in range(CMP_LEN):
                    last = pe.matmul(c.ps[1][0:N_CMP, g * DH:(g + 1) * DH], win[:, 2 + g, :, m], wv[:, m, :],
                                     start=(m == 0), stop=(m == CMP_LEN - 1))
            last.then_inc(product, 1)


def even_attend(c, R, w_out, w_loaded, w_dram):
    nc = c.nc
    names = ("scores", "biased", "exp", "rz", "normed", "turned", "copied", "pv", "out")
    S = {s: c.sem(f"att_{s}") for s in names}
    units = []
    for j in range(2 * NH):
        for i in range(TT):
            width = P * (i + 1)
            cols = slice(i * P, (i + 1) * P)
            if j < NH:
                v = [R["Vf"][:, s, j * DH:(j + 1) * DH] for s in range(i + 1)]
                units.append((j, i, width, R["Qf"][:, j, cols], R["Kf"][:, j, 0:width],
                              R["bias"][:, NH, HALF_ROW - i * P:SEQ], v, None, True, True))
                continue
            h = j - NH
            g = h // (NH // GROUPS)
            q = R["Qn"][:, h, cols]
            units.append((j, i, N_CMP, q, R["kc"][:, g, :], R["bias_c"][:, h, i, :], [R["vc"][:, g, :]],
                          R["gates"][:, i, 3 * h:3 * h + 1], True, False))
            for b in range(2):
                v = [R["Vn"][:, s, b * P + g * DH:b * P + (g + 1) * DH] for s in range(i + 1)]
                units.append((j, i, width, q, R["Kn"][:, 2 * b + g, 0:width], R["bias"][:, h, HALF_ROW - i * P:SEQ], v,
                              R["gates"][:, i, 3 * h + b + 1:3 * h + b + 2], False, b == 1))
    N = len(units)
    head_end = [max(u for u in range(N) if units[u][0] == j) for j in range(2 * NH)]
    LAG_N, LAG_T, LAG_V = 2, 3, 4
    with ExitStack() as st:
        def sb(n, shape):
            return st.enter_context(nc.sbuf_tensor(f"att_{n}", shape, F32))

        sc = sb("sc", [P, 2, SEQ])
        p = sb("p", [P, 4, SEQ])
        pT = sb("pT", [P, 2, SEQ])
        low = sb("low", [P, 4])
        z = sb("z", [P, 4])
        rz = sb("rz", [P, 4])
        block = st.enter_context(nc.Block())

        @block.sync
        def _(sp):
            sp.dma_start(w_out[:], w_dram.rearrange("(k p) n -> p k n", p=P)).then_inc(w_loaded, 16)

        @block.tensor
        def _(pe):
            def scores(u):
                _, _, width, q, k, *_ = units[u]
                if u >= 2:
                    pe.wait_ge(S["biased"], u - 1)
                pe.matmul(c.ps[u % 2][:, 0:width], q, k, start=True, stop=True).then_inc(S["scores"], 1)

            def turn(u):
                width = units[u][2]
                pe.wait_ge(S["normed"], u + 1)
                if u >= 2:
                    pe.wait_ge(S["copied"], u - 1)
                for a in range(0, width, P):
                    m = min(P, width - a)
                    last = pe.transpose(c.ps[2 + u % 2][0:m, a:a + P], p[:, u % 4, a:a + m], c.ident[:])
                last.then_inc(S["turned"], 1)

            def weigh(u):
                j, i, width, *_, values, _, first, final = units[u]
                pe.wait_ge(S["copied"], u + 1)
                if u == 0 or units[u - 1][0] != j:
                    if j >= 2:
                        pe.wait_ge(S["out"], j - 1)
                for s, v in enumerate(values):
                    m = min(P, width - s * P)
                    last = pe.matmul(c.ps[4 + j % 2][0:DH, i * P:(i + 1) * P], v, pT[0:m, u % 2, s * P:(s + 1) * P],
                                     start=(first and s == 0), stop=(final and s == len(values) - 1))
                last.then_inc(S["pv"], 1)

            for u in range(N + LAG_V):
                if u < N:
                    scores(u)
                if LAG_T <= u < N + LAG_T:
                    turn(u - LAG_T)
                if u >= LAG_V:
                    weigh(u - LAG_V)

        @block.vector
        def _(dve):
            for u in range(N + LAG_N):
                m = u - LAG_N
                if m >= 0:
                    dve.wait_ge(S["exp"], m + 1)
                    dve.reciprocal(rz[:, m % 4:m % 4 + 1], z[:, m % 4:m % 4 + 1]).then_inc(S["rz"], 1)
                if u < N:
                    width, bias = units[u][2], units[u][5]
                    dve.wait_ge(S["scores"], u + 1)
                    if u >= 2:
                        dve.wait_ge(S["exp"], u - 1)
                    dve.tensor_tensor_reduce(sc[:, u % 2, 0:width], c.ps[u % 2][:, 0:width], bias, -1.0, BIG, ALU.add,
                                             ALU.min, low[:, u % 4:u % 4 + 1]).then_inc(S["biased"], 1)
                if m >= 0:
                    width, gate = units[m][2], units[m][7]
                    dve.wait_ge(S["rz"], m + 1)
                    o = p[:, m % 4, 0:width]
                    dve.tensor_scalar(o, o, rz[:, m % 4:m % 4 + 1], gate, ALU.mult,
                                      ALU.bypass if gate is None else ALU.mult).then_inc(S["normed"], 1)

        @block.scalar
        def _(act):
            done = 0
            for u in range(N + LAG_V + 1):
                if u < N:
                    width = units[u][2]
                    act.wait_ge(S["biased"], u + 1)
                    if u >= 4:
                        act.wait_ge(S["turned"], u - 3)
                    act.activation(p[:, u % 4, 0:width], sc[:, u % 2, 0:width], ACT.Exp, bias=low[:, u % 4:u % 4 + 1],
                                   scale=-1.0, accum_out=z[:, u % 4:u % 4 + 1]).then_inc(S["exp"], 1)
                m = u - LAG_T
                if 0 <= m < N:
                    width = units[m][2]
                    act.wait_ge(S["turned"], m + 1)
                    if m >= 2:
                        act.wait_ge(S["pv"], m - 1)
                    rows = min(P, width)
                    act.activation(pT[0:rows, m % 2, 0:max(width, P)], c.ps[2 + m % 2][0:rows, 0:max(width, P)],
                                   ACT.Copy).then_inc(S["copied"], 1)
                if done < 2 * NH and u - LAG_V - 1 == head_end[done]:
                    act.wait_ge(S["pv"], head_end[done] + 1)
                    r0 = done % 2 * DH
                    act.activation(R["hT"][r0:r0 + DH, done // 2, :], c.ps[4 + done % 2][0:DH, :],
                                   ACT.Copy).then_inc(S["out"], 1)
                    done += 1


def project_out(c, name, oT, n_k, w, w_loaded, w_count):
    nc = c.nc
    product = c.sem(f"{name}_product")
    with nc.Block() as block:
        @block.tensor
        def _(pe):
            pe.wait_ge(w_loaded, w_count)
            for n in range(2 * TT):
                t, half = n // 2, n % 2
                for k in range(n_k):
                    last = pe.matmul(c.ps[n][:], oT[:, k, t * P:(t + 1) * P], w[:, k, half * 512:(half + 1) * 512],
                                     start=(k == 0), stop=(k == n_k - 1))
                last.then_inc(product, 1)

        @block.vector
        def _(dve):
            for n in range(2 * TT):
                t, half = n // 2, n % 2
                dve.wait_ge(product, n + 1)
                o = c.h[:, t, half * 512:(half + 1) * 512]
                dve.tensor_tensor(o, c.ps[n][:], o, ALU.add)


def even_layer(c, A):
    nc = c.nc
    with ExitStack() as st:
        def sb(n, shape):
            return st.enter_context(nc.sbuf_tensor(f"even_{n}", shape, F32))

        R = {"hT": sb("hT", [P, KD, SEQ])}
        norm_plain(c, "even_norm", A["even_norm_g"][0], R["hT"])
        R.update(
            Qf=sb("Qf", [97, NH, SEQ]), Kf=sb("Kf", [97, NH, SEQ]), Vf=sb("Vf", [P, TT, NH * DH]),
            Qn=sb("Qn", [DH, NH, SEQ]), Kn=sb("Kn", [DH, 2 * GROUPS, SEQ]), Kc=sb("Kc", [DH, 2 * GROUPS, SEQ]),
            Vn=sb("Vn", [P, TT, 2 * P]), gates=sb("gates", [P, TT, 3 * NH]), f=sb("f", [NH, SEQ]),
            kc=sb("kc", [DH, GROUPS, N_CMP]), vc=sb("vc", [N_CMP, GROUPS, DH]),
            bias=sb("bias", [P, NH + 1, SEQ]), bias_c=sb("bias_c", [P, NH, TT, N_CMP]),
            dist_c=sb("dist_c", [P, TT, N_CMP]))
        even_project(c, R["hT"], A["even_w_in"][0], A["even_b_f"][0], R)
        even_prepare(c, A, R)
        w_loaded = c.sem("even_w_out_loaded")
        w_out = sb("w_out", [P, KD, D])
        even_attend(c, R, w_out, w_loaded, A["even_w_out"][0])
        project_out(c, "even_out", R["hT"], KD, w_out, w_loaded, 16)


def odd_project(c, hT, w_in, gate, xr):
    nc = c.nc
    slots = [c.sem(f"odd_proj_w{i}") for i in range(3)]
    product, read_a, read_v = (c.sem(f"odd_proj_{s}") for s in ("product", "read_a", "read_v"))
    with ExitStack() as st:
        w = st.enter_context(nc.sbuf_tensor("odd_proj_w", [P, 3, KD, 512], F32))
        block = st.enter_context(nc.Block())

        @block.sync
        def _(sp):
            for g in range(5):
                if g >= 3:
                    sp.wait_ge(product, 4 * (g - 2))
                sp.dma_start(w[:, g % 3], w_in[:, g * 512:(g + 1) * 512].rearrange("(k p) n -> p k n", p=P)) \
                    .then_inc(slots[g % 3], 16)

        @block.tensor
        def _(pe):
            for n in range(2 * NR):
                g = n // 4
                if n % 4 == 0:
                    pe.wait_ge(slots[g % 3], 16 * (g // 3 + 1))
                if n >= 8:
                    pe.wait_ge(read_a, min(n - 7, NR))
                    if n - 8 >= NR:
                        pe.wait_ge(read_v, n - 7 - NR)
                for k in range(KD):
                    last = pe.matmul(c.ps[n % 8][:], w[:, g % 3, k, n % 4 * P:(n % 4 + 1) * P], hT[:, k, :],
                                     start=(k == 0), stop=(k == KD - 1))
                last.then_inc(product, 1)

        @block.scalar
        def _(act):
            for n in range(NR):
                act.wait_ge(product, n + 1)
                act.activation(gate[:, n, :], c.ps[n % 8][:], ACT.Gelu).then_inc(read_a, 1)

        @block.vector
        def _(dve):
            dve.memset(xr[:, :, 0:CONV_W - 1], 0.0)
            for n in range(NR):
                dve.wait_ge(product, NR + n + 1)
                dve.tensor_copy(xr[:, n, CONV_W - 1:], c.ps[(NR + n) % 8][:]).then_inc(read_v, 1)


def odd_recur(c, A, gate, xr, w_out, w_loaded):
    nc = c.nc
    S = {s: c.sem(f"lru_{s}") for s in ("loaded", "w", "chain", "exps", "soft", "conv", "y", "product", "ri", "tanh",
                                        "ix", "root", "step", "decay", "rix", "u", "scan")}
    with ExitStack() as st:
        def sb(n, shape):
            return st.enter_context(nc.sbuf_tensor(f"lru_{n}", shape, F32))

        cw = sb("cw", [P, CONV_W, NR])
        cb, ba, bi, lam = sb("cb", [P, NR]), sb("ba", [P, NR]), sb("bi", [P, NR]), sb("lam", [P, NR])
        wa, wi = sb("wa", [P, NR, P]), sb("wi", [P, NR, P])
        e, d, z, q, pp, soft = (sb(n, [P, NR]) for n in ("e", "d", "z", "q", "p", "soft"))
        y = sb("y", [P, 2, SEQ])
        r, i_ = sb("r", [P, 2, SEQ]), sb("i", [P, 2, SEQ])
        s_ = sb("s", [P, NR, SEQ])
        ix = sb("ix", [P, NR, SEQ])
        den, inv, a, root = sb("den", [P, SEQ]), sb("inv", [P, 2, SEQ]), sb("a", [P, SEQ]), sb("root", [P, 2, SEQ])
        u, hs = sb("u", [P, SEQ]), sb("hs", [P, SEQ])
        block = st.enter_context(nc.Block())

        @block.sync
        def _(sp):
            small = dict(allow_slow_non_contiguous=True)
            sp.dma_start(cb[:], A["odd_conv_b"][0].rearrange("(n p) -> p n", p=P), **small).then_inc(S["loaded"], 16)
            for j in range(CONV_W):
                sp.dma_start(cw[:, j, :], A["odd_conv_w"][0, j].rearrange("(n p) -> p n", p=P), **small) \
                    .then_inc(S["loaded"], 16)
            sp.dma_start(ba[:], A["odd_b_ra"][0].rearrange("(n p) -> p n", p=P), **small).then_inc(S["loaded"], 16)
            sp.dma_start(bi[:], A["odd_b_ri"][0].rearrange("(n p) -> p n", p=P), **small).then_inc(S["loaded"], 16)
            sp.dma_start(lam[:], A["odd_lam"][0].rearrange("(n p) -> p n", p=P), **small).then_inc(S["loaded"], 16)
            sp.dma_start(wa[:], A["odd_w_ra"][0].rearrange("n c e -> c n e")).then_inc(S["w"], 16)
            sp.dma_start(wi[:], A["odd_w_ri"][0].rearrange("n c e -> c n e")).then_inc(S["w"], 16)
            sp.dma_start(w_out[:], A["odd_w_out"][0].rearrange("(k p) n -> p k n", p=P)).then_inc(w_loaded, 16)
        LOADED = 16 * (CONV_W + 4)

        @block.tensor
        def _(pe):
            pe.wait_ge(S["w"], 32)
            for n in range(NR):
                pe.wait_ge(S["y"], n + 1)
                if n >= 2:
                    pe.wait_ge(S["ri"], 2 * n - 2)
                pe.matmul(c.ps[2 * (n % 2)][:], wa[:, n, :], y[:, n % 2, :], start=True, stop=True) \
                    .then_inc(S["product"], 1)
                pe.matmul(c.ps[2 * (n % 2) + 1][:], wi[:, n, :], y[:, n % 2, :], start=True, stop=True) \
                    .then_inc(S["product"], 1)

        @block.scalar
        def _(act):
            act.wait_ge(S["loaded"], LOADED)
            act.activation(e[:], lam[:], ACT.Abs).then_inc(S["exps"], 1)
            act.wait_ge(S["exps"], 1)
            act.activation(e[:], e[:], ACT.Exp, scale=-1.0).then_inc(S["exps"], 1)
            act.wait_ge(S["soft"], 1)
            for n in range(NR):
                act.wait_ge(S["product"], 2 * n + 1)
                act.activation(r[:, n % 2, :], c.ps[2 * (n % 2)][:], ACT.Sigmoid, bias=ba[:, n:n + 1]) \
                    .then_inc(S["ri"], 1)
                act.wait_ge(S["product"], 2 * n + 2)
                if n >= 2:
                    act.wait_ge(S["ix"], n - 1)
                act.activation(i_[:, n % 2, :], c.ps[2 * (n % 2) + 1][:], ACT.Sigmoid, bias=bi[:, n:n + 1]) \
                    .then_inc(S["ri"], 1)
                act.wait_ge(S["ri"], 2 * n + 1)
                act.activation(s_[:, n, :], r[:, n % 2, :], ACT.Tanh, scale=soft[:, n:n + 1]).then_inc(S["tanh"], 1)
            for n in range(NR):
                act.wait_ge(S["tanh"], n + 1)
                if n >= 2:
                    act.wait_ge(S["u"], n - 1)
                act.activation(root[:, n % 2, :], s_[:, n, :], ACT.Sqrt, scale=4.0).then_inc(S["root"], 1)

        @block.gpsimd
        def _(pool):
            for n in range(NR):
                pool.wait_ge(S["ri"], 2 * n + 2)
                pool.tensor_tensor(ix[:, n, :], i_[:, n % 2, :], y[:, n % 2, :], ALU.mult).then_inc(S["ix"], 1)
            for n in range(NR):
                pool.wait_ge(S["decay"], 2 * n + 1)
                pool.tensor_tensor(ix[:, n, :], ix[:, n, :], inv[:, n % 2, :], ALU.mult).then_inc(S["rix"], 1)

        @block.vector
        def _(dve):
            dve.wait_ge(S["loaded"], LOADED)
            dve.wait_ge(S["exps"], 2)
            at = half_log1p(dve, S["chain"], 0, e[:], d[:], z[:], q[:], pp[:])
            dve.tensor_scalar(d[:], lam[:], -4.0, 0.0, ALU.mult, ALU.max).then_inc(S["chain"], 1)
            dve.wait_ge(S["chain"], at + 1)
            dve.scalar_tensor_tensor(soft[:], pp[:], 8.0, d[:], ALU.mult, ALU.add).then_inc(S["soft"], 1)
            for n in range(NR):
                yn = y[:, n % 2, :]
                if n >= 2:
                    dve.wait_ge(S["ix"], n - 1)
                    dve.wait_ge(S["product"], 2 * n - 2)
                dve.tensor_scalar(yn, xr[:, n, 0:SEQ], cw[:, 0, n:n + 1], cb[:, n:n + 1], ALU.mult,
                                  ALU.add).then_inc(S["conv"], 1)
                for j in range(1, CONV_W):
                    dve.wait_ge(S["conv"], (CONV_W - 1) * n + j)
                    last = dve.scalar_tensor_tensor(yn, xr[:, n, j:j + SEQ], cw[:, j, n:n + 1], yn, ALU.mult, ALU.add)
                    last.then_inc(S["conv"] if j < CONV_W - 1 else S["y"], 1)
            for n in range(NR):
                dve.wait_ge(S["tanh"], n + 1)
                dve.tensor_scalar(den[:], s_[:, n, :], 1.0, None, ALU.add).then_inc(S["step"], 1)
                dve.wait_ge(S["step"], n + 1)
                if n >= 2:
                    dve.wait_ge(S["rix"], n - 1)
                dve.reciprocal(inv[:, n % 2, :], den[:]).then_inc(S["decay"], 1)
                dve.wait_ge(S["decay"], 2 * n + 1)
                dve.tensor_scalar(a[:], inv[:, n % 2, :], 2.0, -1.0, ALU.mult, ALU.add).then_inc(S["decay"], 1)
                dve.wait_ge(S["rix"], n + 1)
                dve.wait_ge(S["root"], n + 1)
                dve.tensor_tensor(u[:], ix[:, n, :], root[:, n % 2, :], ALU.mult).then_inc(S["u"], 1)
                dve.wait_ge(S["u"], n + 1)
                dve.wait_ge(S["decay"], 2 * n + 2)
                dve.tensor_tensor_scan(hs[:], a[:], u[:], 0.0, ALU.mult, ALU.add).then_inc(S["scan"], 1)
                dve.wait_ge(S["scan"], 2 * n + 1)
                dve.tensor_tensor(gate[:, n, :], gate[:, n, :], hs[:], ALU.mult).then_inc(S["scan"], 1)
                if n < NR - 1:
                    dve.wait_ge(S["scan"], 2 * n + 2)


def odd_layer(c, A):
    nc = c.nc
    with ExitStack() as st:
        def sb(n, shape):
            return st.enter_context(nc.sbuf_tensor(f"odd_{n}", shape, F32))

        gate = sb("gate", [P, NR, SEQ])
        xr = sb("xr", [P, NR, CONV_W - 1 + SEQ])
        with nc.sbuf_tensor("odd_hT", [P, KD, SEQ], F32) as hT:
            norm_plain(c, "odd_norm", A["odd_norm_g"][0], hT)
            odd_project(c, hT, A["odd_w_in"][0], gate, xr)
        w_loaded = c.sem("odd_w_out_loaded")
        w_out = sb("w_out", [P, NR, D])
        odd_recur(c, A, gate, xr, w_out, w_loaded)
        project_out(c, "odd_out", gate, NR, w_out, w_loaded, 16)


WIDE = 4
NARROW = 4
CAND = WIDE * TOPK + (TOPK - WIDE) * NARROW


def peer_pick(c, name, hi, lo, w_q, sub_keys, picks, gates, gate_low):
    nc = c.nc
    S = {s: c.sem(f"{name}_{s}") for s in (
        "w0", "w1", "w_hi", "w_lo", "keys", "keysT", "keysT_out", "q", "q_out", "sc", "sc_out", "chain", "place",
        "float", "onehot", "exp", "turn")}
    WS = 3

    steps = []
    for n in range(HC):
        steps += [(s, n) for s in ("max", "strike", "max2", "index2")]
        if n % 2:
            steps += [(s, n // 2) for s in ("cand", "bmax", "bstrike", "bmax2", "bindex2", "shift", "wide", "row",
                                            "column", "eq")]
            if n > 1:
                steps.append(("gather", n // 2 - 1))
    steps += [("gather", PH - 1), ("sub", 0), ("sum", 0), ("recip", 0), ("weigh", 0)]
    done = {s: i + 1 for i, s in enumerate(steps)}

    with ExitStack() as st:
        def sb(n, shape, dt=F32):
            return st.enter_context(nc.sbuf_tensor(f"{name}_{n}", shape, dt))

        w = sb("w", [P, 2, KD, 512])
        w_hi, w_lo = sb("w_hi", [P, WS, KD, P], F32R), sb("w_lo", [P, WS, KD, P], F32R)
        keys = sb("keys", [P, HC, P])
        keysT = sb("keysT", [P, HC, P])
        qT = sb("qT", [P, 2, SEQ])
        sc = sb("sc", [P, TT, 4, P])
        left = sb("left", [P, TT, P])
        top_v = sb("top_v", [P, HC, TT, TOPK])
        top_i = sb("top_i", [P, HC, TT, TOPK], U32)
        top_f = sb("top_f", [P, 2, 2, TT, TOPK])
        cand = sb("cand", [P, TT, CAND])
        rest = sb("rest", [P, TT, CAND])
        best = sb("best", [P, TT, PH, TOPK])
        best_i = sb("best_i", [P, TT, PH, TOPK], U32)
        sh = sb("sh", [P, 2, TT, TOPK], U32)
        shf = sb("shf", [P, 3, TT, TOPK])
        ab = sb("ab", [P, 2, TT, TOPK])
        eq = sb("eq", [P, 2, 2, TT, TOPK, TOPK])
        iota16 = sb("iota16", [P, TOPK])
        i12 = sb("i12", [P, 2, TT, PH, TOPK])
        e = sb("e", [P, TT, PH, TOPK])
        z = sb("z", [P, TT, PH])
        rz = sb("rz", [P, TT, PH])
        gT = sb("gT", [P, SEQ])
        block = st.enter_context(nc.Block())

        @block.sync
        def _(sp):
            for g in range(4):
                if g >= 2:
                    sp.wait_ge(S["w_hi"], 4 * (g - 1))
                    sp.wait_ge(S["w_lo"], 4 * (g - 1))
                sp.dma_start(w[:, g % 2], w_q[:, g * 512:(g + 1) * 512].rearrange("(k p) n -> p k n", p=P)) \
                    .then_inc(S[f"w{g % 2}"], 16)
                if g == 0:
                    sp.dma_start(keys[:], sub_keys.rearrange("h c k d -> k (h c) d")).then_inc(S["keys"], 16)

        @block.tensor
        def _(pe):
            def turn_keys(g):
                pe.wait_ge(S["keys"], 16)
                for j in range(4):
                    last = pe.transpose(c.ps[g][:, j * P:(j + 1) * P], keys[:, 4 * g + j, :], c.ident[:])
                last.then_inc(S["keysT"], 1)

            def scores(n):
                pe.wait_ge(S["q_out"], n + 1)
                pe.wait_ge(S["keysT_out"], n // 4 + 1)
                if n >= 2:
                    pe.wait_ge(S["sc_out"], n - 1)
                for t in range(TT):
                    last = pe.matmul(c.ps[6 + n % 2][:, t * P:(t + 1) * P], qT[:, n % 2, t * P:(t + 1) * P],
                                     keysT[:, n, :], start=True, stop=True)
                last.then_inc(S["sc"], 1)

            for n in range(HC):
                pe.wait_ge(S["w_hi"], n + 1)
                pe.wait_ge(S["w_lo"], n + 1)
                if n >= 2:
                    pe.wait_ge(S["q_out"], n - 1)
                b = c.ps[4 + n % 2]
                for k in range(KD):
                    wh, wl = w_hi[:, n % WS, k, :], w_lo[:, n % WS, k, :]
                    pe.matmul(b[:], wh, hi[:, k, :], start=(k == 0), stop=False)
                    pe.matmul(b[:], wh, lo[:, k, :], start=False, stop=False)
                    last = pe.matmul(b[:], wl, hi[:, k, :], start=False, stop=(k == KD - 1))
                last.then_inc(S["q"], 1)
                if n < 4:
                    turn_keys(n)
                if n >= 1:
                    scores(n - 1)
            scores(HC - 1)
            for s, src in enumerate((i12[:, 0], i12[:, 1], e)):
                if s == 0:
                    pe.wait_ge(S["chain"], done["gather", PH - 1])
                if s == 2:
                    pe.wait_ge(S["chain"], done["weigh", 0])
                for t in range(TT):
                    last = pe.transpose(c.ps[s][:, t * P:(t + 1) * P], src[:, t].rearrange("p h k -> p (h k)"),
                                        c.ident[:])
                last.then_inc(S["turn"], 1)

        @block.scalar
        def _(act):
            def split(n):
                if n % 4 == 0:
                    act.wait_ge(S[f"w{n // 4 % 2}"], 16 * (n // 8 + 1))
                if n >= WS:
                    act.wait_ge(S["q"], n - WS + 1)
                act.activation(w_hi[:, n % WS], w[:, n // 4 % 2, :, n % 4 * P:(n % 4 + 1) * P],
                               ACT.Copy).then_inc(S["w_hi"], 1)

            def floats(n):
                act.wait_ge(S["chain"], done["index2", n])
                if n >= 4:
                    act.wait_ge(S["onehot"], 2 * (n // 2) - 2)
                act.activation(top_f[:, n // 2 % 2, n % 2], top_i[:, n], ACT.Copy).then_inc(S["float"], 1)

            split(0)
            split(1)
            for n in range(HC + 2):
                if n + 2 < HC:
                    split(n + 2)
                if n < HC:
                    act.wait_ge(S["q"], n + 1)
                    if n >= 2:
                        act.wait_ge(S["sc"], n - 1)
                    act.activation(qT[:, n % 2, :], c.ps[4 + n % 2][:], ACT.Copy).then_inc(S["q_out"], 1)
                if n < 4:
                    act.wait_ge(S["keysT"], n + 1)
                    act.activation(keysT[:, 4 * n:4 * n + 4, :], c.ps[n][:].rearrange("p (j k) -> p j k", j=4),
                                   ACT.Copy).then_inc(S["keysT_out"], 1)
                if 1 <= n <= HC:
                    m = n - 1
                    act.wait_ge(S["sc"], m + 1)
                    if m >= 4:
                        act.wait_ge(S["chain"], done["max2", m - 4])
                    act.activation(sc[:, :, m % 4, :], c.ps[6 + m % 2][:].rearrange("p (t k) -> p t k", t=TT),
                                   ACT.Copy).then_inc(S["sc_out"], 1)
                if n >= 2:
                    floats(n - 2)
            act.wait_ge(S["chain"], done["sub", 0])
            act.activation(e[:], e[:], ACT.Exp).then_inc(S["exp"], 1)

        @block.gpsimd
        def _(pool):
            pool.iota(iota16[:], [[1, TOPK]], base=0, channel_multiplier=0,
                      allow_small_or_imprecise_dtypes=True).then_inc(S["place"], 1)

            def split(n):
                pool.wait_ge(S["w_hi"], n + 1)
                pool.tensor_tensor(w_lo[:, n % WS], w[:, n // 4 % 2, :, n % 4 * P:(n % 4 + 1) * P],
                                   w_hi[:, n % WS].bitcast(F32), ALU.subtract).then_inc(S["w_lo"], 1)

            def index(h):
                pool.wait_ge(S["chain"], done["eq", h])
                pool.wait_ge(S["float"], 2 * h + 2)
                for s in range(2):
                    pool.tensor_tensor(eq[:, h % 2, s], eq[:, h % 2, s],
                                       bc(top_f[:, h % 2, s].unsqueeze(2), [P, TT, TOPK, TOPK]),
                                       ALU.mult).then_inc(S["onehot"], 1)

            for n in range(HC):
                split(n)
                if n % 2 == 0 and n >= 6:
                    index(n // 2 - 3)
            for h in range(PH - 3, PH):
                index(h)

        @block.vector
        def _(dve):
            chain = S["chain"]
            dve.wait_ge(S["place"], 1)

            def gather(h):
                dve.wait_ge(S["onehot"], 2 * h + 2)
                dve.tensor_reduce(i12[:, 0, :, h, :], eq[:, h % 2, 0], X, ALU.add)
                dve.tensor_reduce(i12[:, 1, :, h, :], eq[:, h % 2, 1], X, ALU.add).then_inc(chain, 1)

            for n in range(HC):
                s = sc[:, :, n % 4, :]
                dve.wait_ge(S["sc_out"], n + 1)
                for t in range(TT):
                    last = dve.max(top_v[:, n, t, 0:8], s[:, t, :])
                last.then_inc(chain, 1)
                dve.wait_ge(chain, done["max", n])
                for t in range(TT):
                    last = dve.match_replace(left[:, t, :], top_v[:, n, t, 0:8], s[:, t, :], -BIG)
                last.then_inc(chain, 1)
                dve.wait_ge(chain, done["strike", n])
                for t in range(TT):
                    dve.max(top_v[:, n, t, 8:16], left[:, t, :])
                    last = dve.max_index(top_i[:, n, t, 0:8], top_v[:, n, t, 0:8], s[:, t, :])
                last.then_inc(chain, 1)
                dve.wait_ge(chain, done["max2", n])
                for t in range(TT):
                    last = dve.max_index(top_i[:, n, t, 8:16], top_v[:, n, t, 8:16], left[:, t, :])
                last.then_inc(chain, 1)
                if n % 2 == 0:
                    continue
                h = n // 2
                v0, v1 = top_v[:, n - 1], top_v[:, n]
                split_at = WIDE * TOPK
                dve.tensor_tensor(cand[:, :, 0:split_at].rearrange("p t (a b) -> p t a b", a=WIDE),
                                  bc(v0[:, :, 0:WIDE].unsqueeze(3), [P, TT, WIDE, TOPK]),
                                  bc(v1.unsqueeze(2), [P, TT, WIDE, TOPK]), ALU.add)
                dve.tensor_tensor(cand[:, :, split_at:CAND].rearrange("p t (a b) -> p t a b", b=NARROW),
                                  bc(v0[:, :, WIDE:TOPK].unsqueeze(3), [P, TT, TOPK - WIDE, NARROW]),
                                  bc(v1[:, :, 0:NARROW].unsqueeze(2), [P, TT, TOPK - WIDE, NARROW]),
                                  ALU.add).then_inc(chain, 1)
                dve.wait_ge(chain, done["cand", h])
                for t in range(TT):
                    last = dve.max(best[:, t, h, 0:8], cand[:, t, :])
                last.then_inc(chain, 1)
                dve.wait_ge(chain, done["bmax", h])
                for t in range(TT):
                    last = dve.match_replace(rest[:, t, :], best[:, t, h, 0:8], cand[:, t, :], -BIG)
                last.then_inc(chain, 1)
                dve.wait_ge(chain, done["bstrike", h])
                for t in range(TT):
                    dve.max(best[:, t, h, 8:16], rest[:, t, :])
                    last = dve.max_index(best_i[:, t, h, 0:8], best[:, t, h, 0:8], cand[:, t, :])
                last.then_inc(chain, 1)
                dve.wait_ge(chain, done["bmax2", h])
                for t in range(TT):
                    last = dve.max_index(best_i[:, t, h, 8:16], best[:, t, h, 8:16], rest[:, t, :])
                last.then_inc(chain, 1)
                dve.wait_ge(chain, done["bindex2", h])
                place = best_i[:, :, h, :]
                dve.tensor_scalar(sh[:, 0], place, 4, None, ALU.logical_shift_right)
                dve.tensor_scalar(sh[:, 1], place, 2, None, ALU.logical_shift_right).then_inc(chain, 1)
                dve.wait_ge(chain, done["shift", h])
                dve.tensor_scalar(shf[:, 0], sh[:, 0], float(WIDE), None, ALU.min)
                dve.tensor_scalar(shf[:, 1], sh[:, 1], float(WIDE * TOPK // NARROW), 0.0, ALU.subtract,
                                  ALU.max).then_inc(chain, 1)
                dve.wait_ge(chain, done["wide", h])
                dve.tensor_tensor(ab[:, 0], shf[:, 0], shf[:, 1], ALU.add)
                dve.scalar_tensor_tensor(shf[:, 2], shf[:, 0], float(TOPK // NARROW), shf[:, 1], ALU.mult,
                                         ALU.add).then_inc(chain, 1)
                dve.wait_ge(chain, done["row", h])
                dve.scalar_tensor_tensor(ab[:, 1], shf[:, 2], -float(NARROW), place, ALU.mult,
                                         ALU.add).then_inc(chain, 1)
                dve.wait_ge(chain, done["column", h])
                for s in range(2):
                    last = dve.tensor_tensor(eq[:, h % 2, s], bc(ab[:, s].unsqueeze(3), [P, TT, TOPK, TOPK]),
                                             bc(iota16[:].unsqueeze(1).unsqueeze(1), [P, TT, TOPK, TOPK]),
                                             ALU.is_equal)
                last.then_inc(chain, 1)
                if h >= 1:
                    gather(h - 1)
            gather(PH - 1)
            b3, e3 = best[:].rearrange("p t h k -> p (t h) k"), e[:].rearrange("p t h k -> p (t h) k")
            z2, rz2 = z[:].rearrange("p t h -> p (t h)"), rz[:].rearrange("p t h -> p (t h)")
            dve.tensor_tensor(e3, b3, bc(b3[:, :, 0:1], [P, TT * PH, TOPK]), ALU.subtract).then_inc(chain, 1)
            dve.wait_ge(S["exp"], 1)
            dve.tensor_reduce(z2, e3, X, ALU.add).then_inc(chain, 1)
            dve.wait_ge(chain, done["sum", 0])
            dve.reciprocal(rz2, z2).then_inc(chain, 1)
            dve.wait_ge(chain, done["recip", 0])
            dve.scalar_tensor_tensor(e3, e3, GSCALE, bc(rz2.unsqueeze(2), [P, TT * PH, TOPK]), ALU.mult,
                                     ALU.mult).then_inc(chain, 1)
            for s in range(2):
                dve.wait_ge(S["turn"], s + 1)
                dve.tensor_copy(picks[s][:], c.ps[s][:])
            dve.wait_ge(S["turn"], 3)
            dve.tensor_copy(gT[:], c.ps[2][:]).then_inc(chain, 1)
            dve.wait_ge(chain, len(steps) + 1)
            dve.tensor_copy(gates[0][:], gT[:]).then_inc(chain, 1)
            dve.wait_ge(chain, len(steps) + 2)
            dve.tensor_tensor(gate_low[:], gT[:], gates[0][:], ALU.subtract).then_inc(chain, 1)
            dve.wait_ge(chain, len(steps) + 3)
            dve.tensor_copy(gates[1][:], gate_low[:])


BATCH = 8
STAGE = 64
STAGES = SEQ // STAGE
GRP = 4


def expert_rows(tab):
    return tab.rearrange("(i j) d -> i j d", i=P)


class Tables:

    def __init__(self, c, name, st, u_tab, v_tab):
        self.uv, self.vv = expert_rows(u_tab), expert_rows(v_tab)
        self.u = st.enter_context(c.nc.sbuf_tensor(f"{name}_u", [P, 2, 2, D], F32))
        self.v = st.enter_context(c.nc.sbuf_tensor(f"{name}_v", [P, 2, GRP, 512], F32))
        self.u_loaded = [c.sem(f"{name}_u{r}") for r in range(2)]
        self.v_loaded = [c.sem(f"{name}_v{r}") for r in range(2)]

    def load_u(self, sp, s, r):
        sp.dma_start(self.u[:, r], self.uv[:, bass.ds(s * 2, 2), :]).then_inc(self.u_loaded[r], 16)

    def load_v(self, sp, i, r):
        sp.dma_start(self.v[:, r], self.vv[:, bass.ds(i * GRP, GRP), r * 512:(r + 1) * 512]) \
            .then_inc(self.v_loaded[r], 16)


def peer_gates(c, name, picks, gates, gate_low, G, tables, stored):
    nc = c.nc
    S = {s: c.sem(f"{name}_{s}") for s in ("iota", "picked", "made", "low", "low_a", "summed", "staged")}
    PER = 4
    QB = BATCH // PER
    TURNS = 8 // QB
    LOOPS = SEQ // BATCH // TURNS
    with ExitStack() as st:
        def sb(n, shape, dt=F32):
            return st.enter_context(nc.sbuf_tensor(f"{name}_{n}", shape, dt))

        stage = sb("stage", [P, 2, NK, STAGE])
        row = sb("row", [P, NK], F16)
        iota = sb("iota", [P, NK, BATCH], F16)
        A = sb("A", [P, TURNS, NK, BATCH], F16)
        E = sb("E", [P, TURNS, NK, BATCH], F16)
        B1 = sb("B1", [P, TURNS, NK, BATCH], F16)
        B2 = sb("B2", [P, TURNS, NK, BATCH], F16)
        block = st.enter_context(nc.Block())
        shape = [P, NK, BATCH]

        def columns(x, b):
            return bc(x[:, bass.ds(b * BATCH, BATCH)].unsqueeze(1), shape)

        @block.vector
        def _(dve):
            dve.wait_ge(S["iota"], 1)
            dve.tensor_copy(iota[:], bc(row[:].unsqueeze(2), shape)).then_inc(S["picked"], 1)
            dve.wait_ge(S["picked"], 1)

            def batch(i, r, again):
                b = TURNS * i + r
                if again:
                    dve.wait_ge(S["summed"], (b - TURNS + 1) * QB)
                dve.tensor_tensor(E[:, r], iota[:], columns(picks[1], b), ALU.is_equal).then_inc(S["picked"], 1)
                dve.tensor_tensor(A[:, r], iota[:], columns(picks[0], b), ALU.is_equal)
                dve.wait_ge(S["picked"], b + 2)
                dve.tensor_tensor(B1[:, r], E[:, r], columns(gates[0], b), ALU.mult).then_inc(S["made"], 1)

            for r in range(TURNS):
                batch(0, r, False)
            with dve.Fori(1, LOOPS) as i:
                for r in range(TURNS):
                    batch(i, r, True)

        @block.gpsimd
        def _(pool):
            pool.iota(row[:], [[1, NK]], base=0, channel_multiplier=0,
                      allow_small_or_imprecise_dtypes=True).then_inc(S["iota"], 1)
            with pool.Fori(0, LOOPS) as i:
                for r in range(1, TURNS):
                    b = TURNS * i + r
                    pool.wait_ge(S["picked"], b + 2)
                    pool.tensor_tensor(B2[:, r], E[:, r], columns(gates[1], b), ALU.mult).then_inc(S["low"], 1)

        @block.tensor
        def _(pe):
            def batch(i, r, again):
                b = TURNS * i + r
                pe.wait_ge(S["made"], b + 1)
                if r == 0:
                    pe.wait_ge(S["low_a"], i + 1)
                else:
                    pe.wait_ge(S["low"], (TURNS - 1) * i + r)
                for q in range(QB):
                    if again:
                        pe.wait_ge(S["staged"], b * QB + q - 7)
                    for j in range(PER):
                        t = q * PER + j
                        o = c.ps[r * QB + q][:, j * NK:(j + 1) * NK]
                        pe.matmul(o, A[:, r, :, t], B1[:, r, :, t], start=True, stop=False)
                        last = pe.matmul(o, A[:, r, :, t], B2[:, r, :, t], start=False, stop=True)
                    last.then_inc(S["summed"], 1)

            for r in range(TURNS):
                batch(0, r, False)
            with pe.Fori(1, LOOPS) as i:
                for r in range(TURNS):
                    batch(i, r, True)

        @block.scalar
        def _(act):
            def low(i):
                act.wait_ge(S["picked"], TURNS * i + 2)
                for t in range(BATCH):
                    last = act.activation(B2[:, 0, :, t], E[:, 0, :, t], ACT.Copy,
                                          scale=gate_low[:, bass.ds(i * (TURNS * BATCH) + t, 1)])
                last.then_inc(S["low_a"], 1)

            low(0)
            for s in range(STAGES):
                if s >= 2:
                    act.wait_ge(stored[s % 2], 16 * (s // 2))
                for i in range(STAGE // PER // 8):
                    for q in range(8):
                        if q == 2 and not (s == STAGES - 1 and i == STAGE // PER // 8 - 1):
                            low(s * (STAGE // PER // 8) + i + 1)
                        act.wait_ge(S["summed"], s * (STAGE // PER) + 8 * i + q + 1)
                        act.activation(stage[:, s % 2, :, (8 * i + q) * PER:(8 * i + q + 1) * PER],
                                       c.ps[q][:].rearrange("p (t k) -> p k t", t=PER), ACT.Copy,
                                       scale=1.0 / GSCALE).then_inc(S["staged"], 1)

        @block.sync
        def _(sp):
            for r in range(2):
                tables.load_u(sp, r, r)
                tables.load_v(sp, 0, r)
            for s in range(STAGES):
                sp.wait_ge(S["staged"], (s + 1) * (STAGE // PER))
                sp.dma_start(G[:, s], stage[:, s % 2]).then_inc(stored[s % 2], 16)
            sp.wait_ge(stored[0], 16 * (STAGES // 2))


def peer_dense(c, name, hi, lo, G, tables, stored):
    nc = c.nc
    S = {s: c.sem(f"{name}_{s}") for s in (
        "g0", "g1", "turned", "u_hi", "u_lo", "act", "gelu", "w", "w_hi", "w_lo", "v_hi",
        "v_lo", "out", "added")}
    NS = NK
    TURN, ACTB, OUTB = 0, 2, 4
    with ExitStack() as st:
        def sb(n, shape, dt=F32):
            return st.enter_context(nc.sbuf_tensor(f"{name}_{n}", shape, dt))

        u, v = tables.u, tables.v
        g = sb("g", [P, 2, STAGES, 2, STAGE])
        a = sb("a", [P, 2, SEQ])
        w = sb("w", [P, 2, SEQ])
        u_hi, u_lo = sb("u_hi", [P, 2, KD, P], F32R), sb("u_lo", [P, 2, KD, P], F32R)
        w_hi, w_lo = sb("w_hi", [P, 2, GRP, SEQ], F32R), sb("w_lo", [P, 2, GRP, SEQ], F32R)
        v_hi, v_lo = sb("v_hi", [P, 2, GRP, 512], F32R), sb("v_lo", [P, 2, GRP, 512], F32R)
        block = st.enter_context(nc.Block())

        LOOPS = NS // 8

        def before(i, r, n):
            return isinstance(i, int) and 8 * i + r < n

        def after(i, r, by=1):
            return (i, r + by) if r + by < 8 else (i + 1, r + by - 8)

        @block.sync
        def _(sp):
            def loads(i, r, free):
                s = 2 * i + r
                if free:
                    sp.wait_ge(S["turned"], 4 * s - 4)
                    tables.load_u(sp, s, r)
                    sp.wait_ge(S["w"], 2 * s - 2)
                sp.dma_start(g[:, r], G[:, :, bass.ds(s * 2, 2), :]).then_inc(S[f"g{r}"], 16)
                if free:
                    sp.wait_ge(S["v_hi"], 2 * s - 2)
                    sp.wait_ge(S["v_lo"], 2 * s - 2)
                    tables.load_v(sp, i, r)

            sp.wait_ge(stored[1], 16 * (STAGES // 2))
            loads(0, 0, False)
            loads(0, 1, False)
            with sp.Fori(1, NS // GRP) as i:
                for r in range(2):
                    loads(i, r, True)

        @block.tensor
        def _(pe):
            def turn(i, r):
                if r % 2 == 0:
                    pe.wait_ge(tables.u_loaded[r // 2 % 2], 16 * (2 * i + r // 4 + 1))
                for b in range(2):
                    for k in range(4):
                        last = pe.transpose(c.ps[TURN + b][:, k * P:(k + 1) * P],
                                            u[:, r // 2 % 2, r % 2, (4 * b + k) * P:(4 * b + k + 1) * P], c.ident[:])
                    last.then_inc(S["turned"], 1)

            def activations(i, r):
                if not before(i, r, 2):
                    pe.wait_ge(S["gelu"], 8 * i + r - 1)
                o = c.ps[ACTB + r % 2]
                for k in range(KD):
                    uh, ul = u_hi[:, r % 2, k, :], u_lo[:, r % 2, k, :]
                    pe.matmul(o[:], uh, hi[:, k, :], start=(k == 0), stop=False)
                    pe.matmul(o[:], uh, lo[:, k, :], start=False, stop=False)
                    last = pe.matmul(o[:], ul, hi[:, k, :], start=False, stop=(k == KD - 1))
                last.then_inc(S["act"], 1)

            def outputs(i, r):
                n = 8 * i + r
                q2, grp2 = r // 2 % 2, (r // 4 + 1) % 2
                if r % 4 == 0:
                    pe.wait_ge(S["w_hi"], n)
                    pe.wait_ge(S["w_lo"], n)
                if r % 2 == 0:
                    pe.wait_ge(S["v_hi"], n - 2)
                    pe.wait_ge(S["v_lo"], n - 2)
                for m in range(2):
                    t = 2 * (r % 2) + m
                    b = c.ps[OUTB + t]
                    if not before(i, r, GRP + 2):
                        pe.wait_ge(S["added"], 2 * n + m - 2 * GRP - 3)
                    for j in range(GRP):
                        wh, wl = w_hi[:, grp2, j, t * P:(t + 1) * P], w_lo[:, grp2, j, t * P:(t + 1) * P]
                        pe.matmul(b[:], wh, v_hi[:, q2, j, :], start=(j == 0), stop=False)
                        pe.matmul(b[:], wh, v_lo[:, q2, j, :], start=False, stop=False)
                        last = pe.matmul(b[:], wl, v_hi[:, q2, j, :], start=False, stop=(j == GRP - 1))
                    last.then_inc(S["out"], 1)

            def step(i, r, turn_next=True):
                pe.wait_ge(S["u_hi"], 2 * (8 * i + r) + 2)
                pe.wait_ge(S["u_lo"], 2 * (8 * i + r) + 2)
                if turn_next:
                    turn(*after(i, r))
                activations(i, r)
                if not before(i, r, GRP):
                    outputs(i, r)

            turn(0, 0)
            for r in range(8):
                step(0, r)
            with pe.Fori(1, LOOPS - 1) as i:
                for r in range(8):
                    step(i, r)
            for r in range(8):
                step(LOOPS - 1, r, turn_next=(r < 7))
            for r in range(GRP):
                outputs(LOOPS, r)

        @block.scalar
        def _(act):
            def split_u(i, r):
                n = 8 * i + r
                if not before(i, r, 2):
                    act.wait_ge(S["act"], n - 1)
                for b in range(2):
                    act.wait_ge(S["turned"], 2 * n + b + 1)
                    act.activation(u_hi[:, r % 2, 4 * b:4 * b + 4, :].rearrange("p k i -> p (k i)"),
                                   c.ps[TURN + b][:], ACT.Copy).then_inc(S["u_hi"], 1)

            def split_v(i, r):
                s2 = r // 2 % 2
                if r % 2 == 0:
                    act.wait_ge(tables.v_loaded[s2], 16 * (2 * i + r // 4 + 1))
                    if not before(i, r, 4):
                        act.wait_ge(S["out"], 2 * (8 * i + r) - 4)
                j = 2 * (r % 2)
                act.activation(v_hi[:, s2, j:j + 2, :], v[:, s2, j:j + 2, :], ACT.Copy).then_inc(S["v_hi"], 1)

            def step(i, r, split_next=True):
                n = 8 * i + r
                if split_next:
                    split_u(*after(i, r))
                if not before(i, r, 2):
                    split_v(i, r - 2) if r >= 2 else split_v(i - 1, r + 6)
                act.wait_ge(S["act"], n + 1)
                if not before(i, r, 2):
                    act.wait_ge(S["w"], n - 1)
                act.activation(a[:, r % 2, :], c.ps[ACTB + r % 2][:], ACT.Gelu).then_inc(S["gelu"], 1)
                act.wait_ge(S["w"], n + 1)
                if r % 4 == 0 and not before(i, r, 8):
                    act.wait_ge(S["out"], 2 * n - 8)
                act.activation(w_hi[:, r // 4, r % 4, :], w[:, r % 2, :], ACT.Copy).then_inc(S["w_hi"], 1)

            split_u(0, 0)
            for r in range(8):
                step(0, r)
            with act.Fori(1, LOOPS - 1) as i:
                for r in range(8):
                    step(i, r)
            for r in range(8):
                step(LOOPS - 1, r, split_next=(r < 7))
            for r in range(6, 8):
                split_v(LOOPS - 1, r)

        @block.gpsimd
        def _(pool):
            with pool.Fori(0, LOOPS) as i:
                for r in range(8):
                    s2, j = r // 2 % 2, 2 * (r % 2)
                    pool.wait_ge(S["v_hi"], 8 * i + r + 1)
                    pool.tensor_tensor(v_lo[:, s2, j:j + 2, :], v[:, s2, j:j + 2, :],
                                       v_hi[:, s2, j:j + 2, :].bitcast(F32), ALU.subtract).then_inc(S["v_lo"], 1)

        @block.vector
        def _(dve):
            def split_u(i, r):
                for b in range(2):
                    dve.wait_ge(S["u_hi"], 2 * (8 * i + r) + b + 1)
                    part = slice(4 * b, 4 * b + 4)
                    dve.tensor_tensor(u_lo[:, r % 2, part, :].rearrange("p k i -> p (k i)"), c.ps[TURN + b][:],
                                      u_hi[:, r % 2, part, :].rearrange("p k i -> p (k i)").bitcast(F32),
                                      ALU.subtract).then_inc(S["u_lo"], 1)

            def weigh(i, r):
                n = 8 * i + r
                dve.wait_ge(S["gelu"], n + 1)
                if r % 2 == 0:
                    dve.wait_ge(S[f"g{r // 2 % 2}"], 16 * (2 * i + r // 4 + 1))
                if not before(i, r, 2):
                    dve.wait_ge(S["w_lo"], n - 1)
                dve.tensor_tensor(w[:, r % 2, :].rearrange("p (s t) -> p s t", s=STAGES),
                                  a[:, r % 2, :].rearrange("p (s t) -> p s t", s=STAGES),
                                  g[:, r // 2 % 2, :, r % 2, :], ALU.mult).then_inc(S["w"], 1)
                dve.wait_ge(S["w_hi"], n + 1)
                dve.tensor_tensor(w_lo[:, r // 4, r % 4, :], w[:, r % 2, :],
                                  w_hi[:, r // 4, r % 4, :].bitcast(F32), ALU.subtract).then_inc(S["w_lo"], 1)

            def add_out(i, r):
                n = 8 * i + r
                for m in range(2):
                    t = 2 * (r % 2) + m
                    dve.wait_ge(S["out"], 2 * n + m - 2 * GRP + 1)
                    if not before(i, r, 2 * GRP):
                        dve.wait_ge(S["added"], 2 * n + m - 2 * GRP - 7)
                    o = c.h[:, t, r // 2 % 2 * 512:(r // 2 % 2 + 1) * 512]
                    dve.tensor_tensor(o, c.ps[OUTB + t][:], o, ALU.add).then_inc(S["added"], 1)

            def step(i, r, split_next=True):
                if split_next:
                    split_u(*after(i, r))
                weigh(i, r)
                if not before(i, r, GRP):
                    add_out(i, r)

            split_u(0, 0)
            for r in range(8):
                step(0, r)
            with dve.Fori(1, LOOPS - 1) as i:
                for r in range(8):
                    step(i, r)
            for r in range(8):
                step(LOOPS - 1, r, split_next=(r < 7))
            for r in range(GRP):
                add_out(LOOPS, r)


def final_norm(c, gain, out):
    nc = c.nc
    gain_loaded, squares, scale, normed, stored = (
        c.sem(f"final_{s}") for s in ("gain", "squares", "scale", "normed", "stored"))
    with ExitStack() as st:
        g = st.enter_context(nc.sbuf_tensor("final_gain", [P, D], F32))
        o = st.enter_context(nc.sbuf_tensor("final_o", [P, TT, D], F32))
        ss = st.enter_context(nc.sbuf_tensor("final_ss", [P, TT], F32))
        ms = st.enter_context(nc.sbuf_tensor("final_ms", [P, TT], F32))
        std = st.enter_context(nc.sbuf_tensor("final_std", [P, TT], F32))
        r = st.enter_context(nc.sbuf_tensor("final_r", [P, TT], F32))
        block = st.enter_context(nc.Block())

        @block.sync
        def _(sp):
            sp.dma_start(g[:], gain.partition_broadcast(P)).then_inc(gain_loaded, 16)
            for t in range(TT):
                sp.wait_ge(normed, t + 1)
                sp.dma_start(out[0, t * P:(t + 1) * P, :], o[:, t, :]).then_inc(stored, 16)
            sp.wait_ge(stored, 16 * TT)

        @block.scalar
        def _(act):
            for t in range(TT):
                act.activation(o[:, t, :], c.h[:, t, :], ACT.Square, accum_out=ss[:, t:t + 1]).then_inc(squares, 1)
            act.wait_ge(scale, 1)
            act.activation(std[:], ms[:], ACT.Sqrt).then_inc(squares, 1)

        @block.vector
        def _(dve):
            dve.wait_ge(squares, TT)
            dve.tensor_scalar(ms[:], ss[:], 1.0 / D, EPS, ALU.mult, ALU.add).then_inc(scale, 1)
            dve.wait_ge(squares, TT + 1)
            dve.reciprocal(r[:], std[:]).then_inc(scale, 1)
            dve.wait_ge(scale, 2)
            dve.wait_ge(gain_loaded, 16)
            for t in range(TT):
                dve.scalar_tensor_tensor(o[:, t, :], c.h[:, t, :], r[:, t:t + 1], g[:], ALU.mult,
                                         ALU.mult).then_inc(normed, 1)


def peer(c, name, gain, w_q, sub_keys, u_tab, v_tab, G):
    nc = c.nc
    with ExitStack() as st:
        def sb(n, shape, dt=F32):
            return st.enter_context(nc.sbuf_tensor(f"{name}_{n}", shape, dt))
        hi, lo = sb("hn_hi", [P, KD, SEQ], F32R), sb("hn_lo", [P, KD, SEQ], F32R)
        with ExitStack() as st2:
            picks = [st2.enter_context(nc.sbuf_tensor(f"{name}_picks{i}", [P, SEQ], F16)) for i in range(2)]
            gates = [st2.enter_context(nc.sbuf_tensor(f"{name}_gates{i}", [P, SEQ], F16)) for i in range(2)]
            gate_low = st2.enter_context(nc.sbuf_tensor(f"{name}_gate_low", [P, SEQ], F32))
            norm_block(c, f"{name}_norm", gain, hi, lo)
            peer_pick(c, f"{name}_pick", hi, lo, w_q, sub_keys, picks, gates, gate_low)
            tables = Tables(c, name, st2, u_tab, v_tab)
            stored = [c.sem(f"{name}_stored{i}") for i in range(2)]
            peer_gates(c, f"{name}_gate", picks, gates, gate_low, G, tables, stored)
            peer_dense(c, f"{name}_dense", hi, lo, G, tables, stored)


def trunk(nc, A, out, stages=("even", "peer0", "odd", "peer1", "final")):
    ctx = ExitStack()
    with ctx:
        c = Core(nc, ctx)
        G = nc.dram_tensor("gate_matrix", (P, STAGES, NK, STAGE), F32).ap()
        constants(c, A["x"])
        for s in stages:
            if s == "even":
                even_layer(c, A)
            if s == "odd":
                odd_layer(c, A)
            if s[:4] == "peer":
                i = int(s[4])
                peer(c, s, A["ffn_norm_g"][i], A["peer_w_q"][i], A["peer_sub_keys"][i], A["peer_u"][i],
                     A["peer_v"][i], G)
            if s == "final":
                final_norm(c, A["final_g"], out)
            c.end_layer()


_INS = ["x", "even_norm_g", "even_w_in", "even_b_f", "even_cmp_pos", "even_w_cmp_k", "even_w_cmp_v", "even_w_out",
        "odd_norm_g", "odd_w_in", "odd_conv_w", "odd_conv_b", "odd_w_ra", "odd_b_ra", "odd_w_ri", "odd_b_ri",
        "odd_lam", "odd_w_out", "ffn_norm_g", "peer_w_q", "peer_sub_keys", "peer_u", "peer_v", "final_g"]


def kernel(**inputs):
    import numpy as _np
    import concourse.bacc as _bacc
    from concourse import mybir as _mybir
    from concourse.bass_utils import run_bass_kernel_spmd as _run

    nc = _bacc.Bacc("TRN2", target_bir_lowering=False, num_devices=1)
    arrays, args = {}, {}
    for name in _INS:
        a = _np.ascontiguousarray(inputs[name])
        arrays[f"in_{name}_dram"] = a
        args[name] = nc.dram_tensor(f"in_{name}_dram", a.shape, _mybir.dt.from_np(a.dtype), kind="ExternalInput").ap()
    out = nc.dram_tensor("out_0_dram", (1, SEQ, D), F32, kind="ExternalOutput").ap()
    trunk(nc, args, out)
    r = _run(nc, [arrays], core_ids=[0])
    return r.results[0]["out_0_dram"]
```

```python
from contextlib import ExitStack

import concourse.bass as bass
from concourse import mybir

ALU = mybir.AluOpType
ACT = mybir.ActivationFunctionType
X = mybir.AxisListType.X
F32 = mybir.dt.float32
F32R = mybir.dt.float32r
F16 = mybir.dt.float16
U32 = mybir.dt.uint32

P = 128
SEQ = 512
TT = SEQ // P
D = 1024
KD = D // P
EPS = 1e-6
NEG = -1.0e30
BIG = 3.0e38

DH = 64
NH = 8
GROUPS = 2
CMP_LEN = 32
CMP_STRIDE = 16
N_CMP = (SEQ - CMP_LEN) // CMP_STRIDE + 1
FOX_QKV = 3 * NH * DH
HALF_ROW = SEQ - P

D_RNN = 1280
NR = D_RNN // P
CONV_W = 4

PH = 8
NK = 128
TOPK = 16
HC = 2 * PH
GSCALE = 2.0 ** 14
GRP = 4
AHEAD = 2 * GRP
BATCH = 8


def bc(ap, shape):
    return ap.to_broadcast(shape)


class Core:

    def __init__(self, nc, ctx):
        self.nc = nc
        self.sems = []
        self.h = ctx.enter_context(nc.sbuf_tensor("h", [P, TT, D], F32))
        self.ident = ctx.enter_context(nc.sbuf_tensor("ident", [P, P], F32))
        self.ps = [ctx.enter_context(nc.psum_tensor(f"bank{i}", [P, 512], F32)) for i in range(8)]

    def sem(self, name):
        self.sems.append(self.nc.alloc_semaphore(name=name))
        return self.sems[-1]

    def end_layer(self):
        self.nc.clear_and_free_semaphores(self.sems)
        self.nc.all_engine_barrier()
        self.sems = []


def constants(c, x):
    nc = c.nc
    x_loaded, ident_made = c.sem("x_loaded"), c.sem("ident_made")
    with nc.Block() as block:
        @block.sync
        def _(sp):
            sp.dma_start(c.h[:], x[0].rearrange("(t p) d -> p t d", p=P)).then_inc(x_loaded, 16)
            sp.wait_ge(x_loaded, 16)

        @block.gpsimd
        def _(pool):
            pool.memset(c.ident[:], 1.0).then_inc(ident_made, 1)
            pool.wait_ge(ident_made, 1)
            pool.affine_select(out=c.ident[:], in_=c.ident[:], compare_op=ALU.is_equal, fill=0.0, base=0,
                               pattern=[[-1, P]], channel_multiplier=1).then_inc(ident_made, 1)


def norm_block(c, name, gain, hi, lo, loads=None):
    nc = c.nc
    S = {s: c.sem(f"{name}_{s}") for s in ("gain", "sq_a", "sq_v", "scale", "root", "scaled_a", "scaled_v", "turned",
                                           "hi")}
    with ExitStack() as st:
        gT = st.enter_context(nc.sbuf_tensor(f"{name}_gT", [P, KD], F32))
        hn = st.enter_context(nc.sbuf_tensor(f"{name}_hn", [P, TT, D], F32))
        ss, ms, std, r, r2 = (st.enter_context(nc.sbuf_tensor(f"{name}_{n}", [P, TT], F32))
                              for n in ("ss", "ms", "std", "r", "r2"))
        block = st.enter_context(nc.Block())

        @block.sync
        def _(sp):
            sp.dma_start(gT[:], gain.rearrange("(k p) -> p k", p=P),
                         allow_slow_non_contiguous=True).then_inc(S["gain"], 16)
            if loads:
                loads(sp)

        NEWTON = 6

        @block.scalar
        def _(act):
            for t in (0, 2):
                act.activation(hn[:, t, :], c.h[:, t, :], ACT.Square, accum_out=ss[:, t:t + 1]).then_inc(S["sq_a"], 1)
            act.wait_ge(S["scale"], 1)
            act.activation(std[:], ms[:], ACT.Sqrt).then_inc(S["root"], 1)
            act.wait_ge(S["scale"], NEWTON)
            for t in (0, 2):
                act.activation(hn[:, t, :], c.h[:, t, :], ACT.Copy, scale=r[:, t:t + 1]).then_inc(S["scaled_a"], 1)
            act.wait_ge(S["gain"], 16)
            for k in range(KD):
                act.wait_ge(S["turned"], k + 1)
                act.activation(hi[:, k, :], c.ps[k][:], ACT.Copy, scale=gT[:, k:k + 1]).then_inc(S["hi"], 1)

        @block.vector
        def _(dve):
            for t in (1, 3):
                dve.tensor_tensor_reduce(hn[:, t, :], c.h[:, t, :], c.h[:, t, :], 1.0, 0.0, ALU.mult, ALU.add,
                                         ss[:, t:t + 1]).then_inc(S["sq_v"], 1)
            dve.wait_ge(S["sq_a"], 2)
            dve.wait_ge(S["sq_v"], 2)
            dve.tensor_scalar(ms[:], ss[:], 1.0 / D, EPS, ALU.mult, ALU.add).then_inc(S["scale"], 1)
            dve.wait_ge(S["root"], 1)
            dve.reciprocal(r[:], std[:]).then_inc(S["scale"], 1)
            dve.wait_ge(S["scale"], 2)
            dve.tensor_tensor(r2[:], r[:], r[:], ALU.mult).then_inc(S["scale"], 1)
            dve.wait_ge(S["scale"], 3)
            dve.scalar_tensor_tensor(r2[:], r2[:], -0.5, ms[:], ALU.mult, ALU.mult).then_inc(S["scale"], 1)
            dve.wait_ge(S["scale"], 4)
            dve.scalar_tensor_tensor(r2[:], r2[:], 1.5, r[:], ALU.add, ALU.mult).then_inc(S["scale"], 1)
            dve.wait_ge(S["scale"], 5)
            dve.tensor_copy(r[:], r2[:]).then_inc(S["scale"], 1)
            dve.wait_ge(S["scale"], NEWTON)
            for t in (1, 3):
                dve.tensor_scalar(hn[:, t, :], c.h[:, t, :], r[:, t:t + 1], None, ALU.mult).then_inc(S["scaled_v"], 1)
            for k in range(KD):
                dve.wait_ge(S["hi"], k + 1)
                dve.scalar_tensor_tensor(lo[:, k, :], c.ps[k][:], gT[:, k:k + 1], hi[:, k, :].bitcast(F32), ALU.mult,
                                         ALU.subtract)

        @block.tensor
        def _(pe):
            pe.wait_ge(S["scaled_a"], 2)
            pe.wait_ge(S["scaled_v"], 2)
            for k in range(KD):
                for t in range(TT):
                    last = pe.transpose(c.ps[k][:, t * P:(t + 1) * P], hn[:, t, k * P:(k + 1) * P], c.ident[:])
                last.then_inc(S["turned"], 1)


SERIES = [1 / 15, 1 / 13, 1 / 11, 1 / 9, 1 / 7, 1 / 5, 1 / 3]


def half_log1p(dve, chain, at, e, d, z, q, p):
    dve.tensor_scalar(d, e, 2.0, None, ALU.add).then_inc(chain, 1)
    dve.wait_ge(chain, at + 1)
    dve.reciprocal(q, d).then_inc(chain, 1)
    dve.wait_ge(chain, at + 2)
    dve.tensor_tensor(z, e, q, ALU.mult).then_inc(chain, 1)
    dve.wait_ge(chain, at + 3)
    dve.tensor_tensor(q, z, z, ALU.mult).then_inc(chain, 1)
    dve.wait_ge(chain, at + 4)
    dve.tensor_scalar(p, q, SERIES[0], None, ALU.mult).then_inc(chain, 1)
    n = at + 5
    for coefficient in SERIES[1:]:
        dve.wait_ge(chain, n)
        dve.scalar_tensor_tensor(p, p, coefficient, q, ALU.add, ALU.mult).then_inc(chain, 1)
        n += 1
    dve.wait_ge(chain, n)
    dve.scalar_tensor_tensor(p, p, 1.0, z, ALU.add, ALU.mult).then_inc(chain, 1)
    dve.wait_ge(chain, n + 1)
    return n + 1


class EvenInputs:

    SLOTS = 4
    SMALL_GATES = 32

    def __init__(self, c, A, st, R):
        def sb(n, shape):
            return st.enter_context(c.nc.sbuf_tensor(f"even_{n}", shape, F32))

        self.w_in = A["even_w_in"][0]
        self.A = A
        self.w = sb("w_in", [P, self.SLOTS, KD, P])
        self.wk, self.wv = sb("wk", [DH, CMP_LEN, DH]), sb("wv", [DH, CMP_LEN, DH])
        self.pos, self.bf = sb("pos", [DH, CMP_LEN]), sb("bf", [NH, 1])
        self.w_loaded = [c.sem(f"even_w_in{i}") for i in range(self.SLOTS)]
        self.bf_loaded, self.cmp_loaded = c.sem("even_bf_loaded"), c.sem("even_cmp_loaded")
        nsa = FOX_QKV + NH
        kv = nsa + NH * DH
        self.gates_at = kv + 6 * P
        self.units = [("small", FOX_QKV, R["gates"][:], 1.0),
                      ("feature", kv, (R["Kc"], 0), 1.0), ("feature", kv + P, (R["Kc"], 2), 1.0)]
        self.units += [("turned", 2 * NH * DH + m * P, R["Vf"][:, :, m * P:(m + 1) * P], 1.0) for m in range(4)]
        self.units += [("turned", kv + (3 + 2 * m) * P, R["Vn"][:, :, m * P:(m + 1) * P], 1.0) for m in range(2)]
        self.units += [("feature", m * P, (R["Qf"], 2 * m), DH ** -0.5) for m in range(4)]
        self.units += [("feature", NH * DH + m * P, (R["Kf"], 2 * m), 1.0) for m in range(4)]
        self.units += [("feature", nsa + m * P, (R["Qn"], 2 * m), DH ** -0.5) for m in range(4)]
        self.units += [("feature", kv + (2 + 2 * m) * P, (R["Kn"], 2 * m), 1.0) for m in range(2)]

    def load_unit(self, sp, n):
        def load(col, width, at=0):
            sp.dma_start(self.w[:, n % self.SLOTS, :, at:at + width],
                         self.w_in[:, col:col + width].rearrange("(k p) n -> p k n", p=P)) \
                .then_inc(self.w_loaded[n % self.SLOTS], 16)

        if n == 0:
            load(FOX_QKV, NH)
            load(self.gates_at, 3 * NH, self.SMALL_GATES)
        else:
            load(self.units[n][1], P)

    def unit_count(self, n):
        return 16 * (n // self.SLOTS + 1 + (n % self.SLOTS == 0))

    def first_loads(self, sp):
        for n in range(self.SLOTS):
            self.load_unit(sp, n)
        sp.dma_start(self.bf[:], self.A["even_b_f"][0].unsqueeze(1)).then_inc(self.bf_loaded, 16)
        sp.dma_start(self.pos[:], self.A["even_cmp_pos"][0].rearrange("l d -> d l"),
                     allow_slow_non_contiguous=True).then_inc(self.cmp_loaded, 16)
        sp.dma_start(self.wk[:], self.A["even_w_cmp_k"][0].rearrange("l d e -> d l e")).then_inc(self.cmp_loaded, 16)
        sp.dma_start(self.wv[:], self.A["even_w_cmp_v"][0].rearrange("l d e -> d l e")).then_inc(self.cmp_loaded, 16)


def even_project(c, W, R, hi, lo):
    nc = c.nc
    S = {s: c.sem(f"proj_{s}") for s in (
        "gap", "w_hi", "w_lo", "unit", "out_a", "out_v", "tmp", "turned", "turned_out", "forget", "chain", "summed",
        "rows", "padded", "shifted", "compressed", "cmp_out")}
    WS = 3
    UB, TB, CB = 4, 4, 6
    units = W.units
    N = len(units)
    CMP_AT, ROWS_AT = 8, 12
    turned = [n for n in range(N) if units[n][0] != "feature"]
    feature_count = [sum(u[0] == "feature" for u in units[:n + 1]) for n in range(N)]
    small = W.SMALL_GATES + 3 * NH
    with ExitStack() as st:
        def sb(n, shape, dt=F32):
            return st.enter_context(nc.sbuf_tensor(f"proj_{n}", shape, dt))

        w_hi, w_lo = sb("w_hi", [P, WS, KD, P], F32R), sb("w_lo", [P, WS, KD, P], F32R)
        tmp = sb("tmp", [P, 2, SEQ])
        Kb = sb("Kb", [DH, 2 * GROUPS, SEQ])
        f, e, z, q, p = (sb(n, [NH, SEQ]) for n in "fezqp")
        block = st.enter_context(nc.Block())

        def width(n):
            return small if units[n][0] == "small" else P

        @block.sync
        def _(sp):
            for n in range(W.SLOTS, N):
                sp.wait_ge(S["w_hi"], n - W.SLOTS + 1)
                sp.wait_ge(S["w_lo"], n - W.SLOTS + 1)
                W.load_unit(sp, n)
                if n == ROWS_AT:
                    sp.wait_ge(S["padded"], 4)
                    sp.wait_ge(S["summed"], 1)
                    for h in range(NH):
                        sp.dma_start(R["Qf"][DH:DH + 1, h, :], e[h:h + 1, :]).then_inc(S["rows"], 16)
                        sp.dma_start(R["Kf"][96:97, h, :], z[h:h + 1, :]).then_inc(S["rows"], 16)
            sp.wait_ge(S["rows"], 16 * 2 * NH)

        @block.tensor
        def _(pe):
            def turn(j):
                m = 3 * NH if j == 0 else P
                pe.wait_ge(S["tmp"], j + 1)
                if j >= 2:
                    pe.wait_ge(S["turned_out"], j - 1)
                for t in range(TT):
                    last = pe.transpose(c.ps[TB + j % 2][:, t * m:(t + 1) * m], tmp[0:m, j % 2, t * P:(t + 1) * P],
                                        c.ident[0:m, 0:m])
                last.then_inc(S["turned"], 1)

            def windows(s, groups, m):
                x = R["Kc"] if m < CMP_STRIDE else Kb
                x = x[:, s:s + groups, :].rearrange("p s (n b) -> p s n b", b=CMP_STRIDE)
                return x[:, :, m // CMP_STRIDE:m // CMP_STRIDE + N_CMP, m % CMP_STRIDE]

            def compress():
                pe.wait_ge(W.cmp_loaded, 48)
                pe.wait_ge(S["shifted"], 4)
                for m in range(CMP_LEN):
                    last = pe.matmul(c.ps[CB][0:DH, 0:GROUPS * N_CMP], W.wk[:, m, :], windows(0, GROUPS, m),
                                     start=(m == 0), stop=(m == CMP_LEN - 1))
                last.then_inc(S["compressed"], 1)
                for g in range(GROUPS):
                    for m in range(CMP_LEN):
                        last = pe.matmul(c.ps[CB + 1][0:N_CMP, g * DH:(g + 1) * DH],
                                         windows(GROUPS + g, 1, m)[:, 0], W.wv[:, m, :],
                                         start=(m == 0), stop=(m == CMP_LEN - 1))
                last.then_inc(S["compressed"], 1)

            for n in range(N):
                pe.wait_ge(S["w_hi"], n + 1)
                pe.wait_ge(S["w_lo"], n + 1)
                m = n - UB
                if m >= 0 and m in turned:
                    pe.wait_ge(S["tmp"], turned.index(m) + 1)
                    if m == 0:
                        pe.wait_ge(S["forget"], 1)
                elif m >= 0:
                    pe.wait_ge(S["out_a"], feature_count[m])
                    pe.wait_ge(S["out_v"], feature_count[m])
                b = c.ps[n % UB]
                for k in range(KD):
                    wh, wl = w_hi[:, n % WS, k, 0:width(n)], w_lo[:, n % WS, k, 0:width(n)]
                    o = b[0:width(n), :]
                    pe.matmul(o, wh, hi[:, k, :], start=(k == 0), stop=False)
                    pe.matmul(o, wh, lo[:, k, :], start=False, stop=False)
                    last = pe.matmul(o, wl, hi[:, k, :], start=False, stop=(k == KD - 1))
                last.then_inc(S["unit"], 1)
                if n - 1 in turned:
                    turn(turned.index(n - 1))
                if n == CMP_AT:
                    compress()

        @block.scalar
        def _(act):
            def split(n):
                if n == 0:
                    act.wait_ge(S["gap"], 1)
                act.wait_ge(W.w_loaded[n % W.SLOTS], W.unit_count(n))
                if n >= WS:
                    act.wait_ge(S["unit"], n - WS + 1)
                act.activation(w_hi[:, n % WS, :, 0:width(n)], W.w[:, n % W.SLOTS, :, 0:width(n)],
                               ACT.Copy).then_inc(S["w_hi"], 1)

            for n in range(WS):
                split(n)
            for n, (kind, _, where, scale) in enumerate(units):
                if n + WS < N:
                    split(n + WS)
                b = c.ps[n % UB]
                act.wait_ge(S["unit"], n + 1)
                if kind == "feature":
                    act.activation(where[0][0:DH, where[1], :], b[0:DH, :], ACT.Copy, scale=scale) \
                        .then_inc(S["out_a"], 1)
                    continue
                j = turned.index(n)
                if j >= 2:
                    act.wait_ge(S["turned"], j - 1)
                if kind == "turned":
                    act.activation(tmp[:, j % 2, :], b[:], ACT.Copy).then_inc(S["tmp"], 1)
                    continue
                act.activation(tmp[0:3 * NH, j % 2, :], b[W.SMALL_GATES:small, :], ACT.Sigmoid).then_inc(S["tmp"], 1)
                act.wait_ge(W.bf_loaded, 16)
                act.activation(f[:], b[0:NH, :], ACT.Identity, bias=W.bf[:, 0:1]).then_inc(S["forget"], 1)
                act.wait_ge(S["forget"], 1)
                act.activation(e[:], f[:], ACT.Abs).then_inc(S["forget"], 1)
                act.wait_ge(S["forget"], 2)
                act.activation(e[:], e[:], ACT.Exp, scale=-1.0).then_inc(S["forget"], 1)

        @block.vector
        def _(dve):
            def running_sum():
                chain = S["chain"]
                dve.wait_ge(S["forget"], 3)
                n = half_log1p(dve, chain, 0, e[:], p[:], z[:], q[:], p[:])
                dve.tensor_scalar(f[:], f[:], 0.0, None, ALU.min)
                dve.memset(q[:], 1.0).then_inc(chain, 1)
                dve.wait_ge(chain, n + 1)
                dve.scalar_tensor_tensor(f[:], p[:], -2.0, f[:], ALU.mult, ALU.add).then_inc(chain, 1)
                dve.wait_ge(chain, n + 2)
                dve.tensor_tensor_scan(e[:], q[:], f[:], 0.0, ALU.mult, ALU.add).then_inc(chain, 1)
                dve.wait_ge(chain, n + 3)
                dve.tensor_scalar(z[:], e[:], -1.0, None, ALU.mult).then_inc(S["summed"], 1)

            def turned_out(j):
                m = 3 * NH if j == 0 else P
                dve.wait_ge(S["turned"], j + 1)
                dve.tensor_copy(units[turned[j]][2],
                                c.ps[TB + j % 2][:, 0:TT * m].rearrange("p (t m) -> p t m", t=TT)) \
                    .then_inc(S["turned_out"], 1)

            for n, (kind, _, where, scale) in enumerate(units):
                if kind == "feature":
                    dve.wait_ge(S["unit"], n + 1)
                    dve.tensor_scalar(where[0][0:DH, where[1] + 1, :], c.ps[n % UB][DH:P, :], scale, None,
                                      ALU.mult).then_inc(S["out_v"], 1)
                if n - 1 in turned:
                    turned_out(turned.index(n - 1))
                if n == 2:
                    running_sum()
            dve.wait_ge(S["compressed"], 2)
            dve.tensor_copy(R["kc"][:], c.ps[CB][0:DH, 0:GROUPS * N_CMP].rearrange("p (g n) -> p g n", g=GROUPS))
            dve.tensor_copy(R["vc"][:], c.ps[CB + 1][0:N_CMP, 0:GROUPS * DH].rearrange("p (g e) -> p g e", g=GROUPS))

        @block.gpsimd
        def _(pool):
            def split(n):
                pool.wait_ge(S["w_hi"], n + 1)
                pool.tensor_tensor(w_lo[:, n % WS, :, 0:width(n)], W.w[:, n % W.SLOTS, :, 0:width(n)],
                                   w_hi[:, n % WS, :, 0:width(n)].bitcast(F32), ALU.subtract).then_inc(S["w_lo"], 1)

            def add_positions(x, s, half):
                def blocks(y):
                    return y[:, s:s + GROUPS, :].rearrange("p s (n b) -> p (s n) b", b=CMP_STRIDE)
                pos = W.pos[:, half * CMP_STRIDE:(half + 1) * CMP_STRIDE]
                pool.tensor_tensor(blocks(x), blocks(R["Kc"]),
                                   bc(pos.unsqueeze(1), [DH, GROUPS * SEQ // CMP_STRIDE, CMP_STRIDE]),
                                   ALU.add).then_inc(S["shifted"], 1)

            pool.memset(W.w[:, 0, :, NH:W.SMALL_GATES], 0.0).then_inc(S["gap"], 1)
            for n in range(N):
                split(n)
                if n == 2:
                    pool.wait_ge(S["w_lo"], n + 1)
                    pads = ((R["Qf"][DH:97], 0.0), (R["Kf"][DH:97], 0.0), (R["Qf"][96:97], 1.0),
                            (R["Kf"][DH:DH + 1], 1.0))
                    for i, (rows, value) in enumerate(pads):
                        pool.memset(rows, value).then_inc(S["padded"], 1)
                        pool.wait_ge(S["padded"], i + 1)
                if n in (4, 5):
                    s = (n - 4) * GROUPS
                    pool.wait_ge(W.cmp_loaded, 48)
                    pool.wait_ge(S["out_a"], n - 3)
                    pool.wait_ge(S["out_v"], n - 3)
                    pool.wait_ge(S["w_lo"], n + 1)
                    add_positions(Kb, s, 1)
                    pool.wait_ge(S["shifted"], 2 * (n - 4) + 1)
                    add_positions(R["Kc"], s, 0)
                    pool.wait_ge(S["shifted"], 2 * (n - 4) + 2)
            pool.wait_ge(S["turned_out"], 1)
            first = R["gates"][:, 0, :].rearrange("p (h b) -> p h b", b=3)[:, :, 0]
            pool.affine_select(out=first, in_=first, compare_op=ALU.is_ge, fill=0.0, base=-(CMP_LEN - 1),
                               pattern=[[0, NH]], channel_multiplier=1)


def even_attend(c, R, oT, w_out, w_loaded, w_dram):
    nc = c.nc
    names = ("tables", "made", "scores", "biased", "exp", "rz", "normed", "turned", "copied", "pv", "out")
    S = {s: c.sem(f"att_{s}") for s in names}
    RING, LONG = 3, 6
    SCORES, TURNED, OUT = (0, 1, 6), (2, 3, 7), 4
    with ExitStack() as st:
        def sb(n, shape):
            return st.enter_context(nc.sbuf_tensor(f"att_{n}", shape, F32))

        bias = sb("bias", [P, NH + 1, SEQ])
        bias_c, dist_c = sb("bias_c", [P, NH, TT, N_CMP]), sb("dist_c", [P, TT, N_CMP])
        dist = sb("dist", [P, SEQ])
        sc = sb("sc", [P, RING, SEQ])
        p = sb("p", [P, LONG, SEQ])
        pT = sb("pT", [P, RING, SEQ])
        low, z, rz = (sb(n, [P, LONG]) for n in ("low", "z", "rz"))
        units = []
        for j in range(2 * NH):
            for i in range(TT):
                width = P * (i + 1)
                cols = slice(i * P, (i + 1) * P)
                if j < NH:
                    v = [R["Vf"][:, s, j * DH:(j + 1) * DH] for s in range(i + 1)]
                    units.append((j, i, width, R["Qf"][:, j, cols], R["Kf"][:, j, 0:width],
                                  bias[:, NH, HALF_ROW - i * P:SEQ], v, None, True, True))
                    continue
                h = j - NH
                g = h // (NH // GROUPS)
                q = R["Qn"][:, h, cols]
                units.append((j, i, N_CMP, q, R["kc"][:, g, :], bias_c[:, h, i, :], [R["vc"][:, g, :]],
                              R["gates"][:, i, 3 * h:3 * h + 1], True, False))
                for b in range(2):
                    v = [R["Vn"][:, s, b * P + g * DH:b * P + (g + 1) * DH] for s in range(i + 1)]
                    units.append((j, i, width, q, R["Kn"][:, 2 * b + g, 0:width], bias[:, h, HALF_ROW - i * P:SEQ], v,
                                  R["gates"][:, i, 3 * h + b + 1:3 * h + b + 2], False, b == 1))
        N = len(units)
        head_end = [max(u for u in range(N) if units[u][0] == j) for j in range(2 * NH)]
        LAG_N, LAG_T, LAG_V = 3, 5, 7
        block = st.enter_context(nc.Block())

        @block.sync
        def _(sp):
            sp.dma_start(w_out[:], w_dram.rearrange("(k p) n -> p k n", p=P)).then_inc(w_loaded, 16)

        @block.tensor
        def _(pe):
            def scores(u):
                _, _, width, q, k, *_ = units[u]
                if u >= RING:
                    pe.wait_ge(S["biased"], u - RING + 1)
                pe.matmul(c.ps[SCORES[u % RING]][:, 0:width], q, k, start=True, stop=True).then_inc(S["scores"], 1)

            def turn(u):
                width = units[u][2]
                pe.wait_ge(S["normed"], u + 1)
                if u >= RING:
                    pe.wait_ge(S["copied"], u - RING + 1)
                for a in range(0, width, P):
                    m = min(P, width - a)
                    last = pe.transpose(c.ps[TURNED[u % RING]][0:m, a:a + P], p[:, u % LONG, a:a + m], c.ident[:])
                last.then_inc(S["turned"], 1)

            def weigh(u):
                j, i, width, *_, values, _, first, final = units[u]
                pe.wait_ge(S["copied"], u + 1)
                if u == 0 or units[u - 1][0] != j:
                    if j >= 2:
                        pe.wait_ge(S["out"], j - 1)
                for s, v in enumerate(values):
                    m = min(P, width - s * P)
                    last = pe.matmul(c.ps[OUT + j % 2][0:DH, i * P:(i + 1) * P], v,
                                     pT[0:m, u % RING, s * P:(s + 1) * P],
                                     start=(first and s == 0), stop=(final and s == len(values) - 1))
                last.then_inc(S["pv"], 1)

            for u in range(N + LAG_V):
                if u < N:
                    scores(u)
                if LAG_T <= u < N + LAG_T:
                    turn(u - LAG_T)
                if u >= LAG_V:
                    weigh(u - LAG_V)

        @block.vector
        def _(dve):
            for u in range(N + LAG_N):
                m = u - LAG_N
                if m >= 0:
                    dve.wait_ge(S["exp"], m + 1)
                    dve.reciprocal(rz[:, m % LONG:m % LONG + 1], z[:, m % LONG:m % LONG + 1]).then_inc(S["rz"], 1)
                if u < N:
                    width, bias = units[u][2], units[u][5]
                    if u == 0 or units[u - 1][0] != units[u][0]:
                        dve.wait_ge(S["made"], max(0, units[u][0] - NH + 1) + 1)
                    dve.wait_ge(S["scores"], u + 1)
                    if u >= RING:
                        dve.wait_ge(S["exp"], u - RING + 1)
                    dve.tensor_tensor_reduce(sc[:, u % RING, 0:width], c.ps[SCORES[u % RING]][:, 0:width], bias, -1.0,
                                             BIG, ALU.add, ALU.min, low[:, u % LONG:u % LONG + 1]) \
                        .then_inc(S["biased"], 1)
                if m >= 0:
                    width, gate = units[m][2], units[m][7]
                    dve.wait_ge(S["rz"], m + 1)
                    o = p[:, m % LONG, 0:width]
                    dve.tensor_scalar(o, o, rz[:, m % LONG:m % LONG + 1], gate, ALU.mult,
                                      ALU.bypass if gate is None else ALU.mult).then_inc(S["normed"], 1)

        @block.scalar
        def _(act):
            done = 0
            for u in range(N + LAG_V + 1):
                if u < N:
                    width = units[u][2]
                    act.wait_ge(S["biased"], u + 1)
                    if u >= LONG:
                        act.wait_ge(S["turned"], u - LONG + 1)
                    act.activation(p[:, u % LONG, 0:width], sc[:, u % RING, 0:width], ACT.Exp,
                                   bias=low[:, u % LONG:u % LONG + 1],
                                   scale=-1.0, accum_out=z[:, u % LONG:u % LONG + 1]).then_inc(S["exp"], 1)
                m = u - LAG_T
                if 0 <= m < N:
                    width = units[m][2]
                    act.wait_ge(S["turned"], m + 1)
                    if m >= RING:
                        act.wait_ge(S["pv"], m - RING + 1)
                    rows = min(P, width)
                    act.activation(pT[0:rows, m % RING, 0:max(width, P)],
                                   c.ps[TURNED[m % RING]][0:rows, 0:max(width, P)], ACT.Copy).then_inc(S["copied"], 1)
                if done < 2 * NH and u - LAG_V - 1 == head_end[done]:
                    act.wait_ge(S["pv"], head_end[done] + 1)
                    r0 = done % 2 * DH
                    act.activation(oT[r0:r0 + DH, done // 2, :], c.ps[OUT + done % 2][0:DH, :],
                                   ACT.Copy).then_inc(S["out"], 1)
                    done += 1

        @block.gpsimd
        def _(pool):
            tables = S["tables"]

            def mask(x, columns, base, pattern):
                return pool.affine_select(out=x, in_=columns, compare_op=ALU.is_ge, fill=NEG, base=base,
                                          pattern=pattern, channel_multiplier=1)

            pool.memset(bias[:, NH, :], 0.0).then_inc(tables, 1)
            pool.wait_ge(tables, 1)
            mask(bias[:, NH, :], bias[:, NH, :], HALF_ROW, [[-1, SEQ]]).then_inc(S["made"], 1)
            pool.iota(dist[:], [[-1, SEQ]], base=HALF_ROW, channel_multiplier=1,
                      allow_small_or_imprecise_dtypes=True)
            pool.iota(dist_c[:], [[P, TT], [-CMP_STRIDE, N_CMP]], base=-(CMP_LEN - 1), channel_multiplier=1,
                      allow_small_or_imprecise_dtypes=True).then_inc(tables, 1)
            pool.wait_ge(tables, 2)
            for h in range(NH):
                slope = 2.0 ** (-8.0 * (h + 1) / NH)
                pool.tensor_scalar(bias[:, h, :], dist[:], -slope, None, ALU.mult)
                pool.tensor_scalar(bias_c[:, h], dist_c[:], -slope, None, ALU.mult).then_inc(tables, 1)
                pool.wait_ge(tables, h + 3)
                mask(bias[:, h, :], bias[:, h, :], HALF_ROW, [[-1, SEQ]])
                mask(bias_c[:, h], bias_c[:, h], -(CMP_LEN - 1), [[P, TT], [-CMP_STRIDE, N_CMP]]) \
                    .then_inc(S["made"], 1)


def project_out(c, name, oT, n_k, parts, loads=None):
    nc = c.nc
    S = {s: c.sem(f"{name}_{s}") for s in ("w_hi", "w_lo", "o_hi", "o_lo", "used", "summed")}
    WS = 3
    part = [max(i for i, (k0, _, _) in enumerate(parts) if k0 <= k) for k in range(n_k)]

    def rows(k):
        k0, w, _ = parts[part[k]]
        return w[:, k - k0, :]

    with ExitStack() as st:
        def sb(n, shape):
            return st.enter_context(nc.sbuf_tensor(f"{name}_{n}", shape, F32R))

        w_hi, w_lo = sb("w_hi", [P, WS, D]), sb("w_lo", [P, WS, D])
        o_hi, o_lo = sb("o_hi", [P, WS, SEQ]), sb("o_lo", [P, WS, SEQ])
        block = st.enter_context(nc.Block())

        @block.sync
        def _(sp):
            if loads:
                loads(sp)

        @block.scalar
        def _(act):
            for k in range(n_k):
                if k == 0 or part[k] != part[k - 1]:
                    act.wait_ge(parts[part[k]][2], 16)
                if k >= WS:
                    act.wait_ge(S["used"], k - WS + 1)
                act.activation(w_hi[:, k % WS, :], rows(k), ACT.Copy).then_inc(S["w_hi"], 1)
                act.activation(o_hi[:, k % WS, :], oT[:, k, :], ACT.Copy).then_inc(S["o_hi"], 1)

        @block.gpsimd
        def _(pool):
            for k in range(n_k):
                pool.wait_ge(S["w_hi"], k + 1)
                pool.tensor_tensor(w_lo[:, k % WS, :], rows(k), w_hi[:, k % WS, :].bitcast(F32),
                                   ALU.subtract).then_inc(S["w_lo"], 1)

        @block.tensor
        def _(pe):
            for k in range(n_k):
                pe.wait_ge(S["w_hi"], k + 1)
                pe.wait_ge(S["w_lo"], k + 1)
                pe.wait_ge(S["o_hi"], k + 1)
                pe.wait_ge(S["o_lo"], k + 1)
                for n in range(2 * TT):
                    tokens, cols = slice(n // 2 * P, (n // 2 + 1) * P), slice(n % 2 * 512, (n % 2 + 1) * 512)
                    oh, ol = o_hi[:, k % WS, tokens], o_lo[:, k % WS, tokens]
                    wh, wl = w_hi[:, k % WS, cols], w_lo[:, k % WS, cols]
                    pe.matmul(c.ps[n][:], oh, wh, start=(k == 0), stop=False)
                    pe.matmul(c.ps[n][:], oh, wl, start=False, stop=False)
                    last = pe.matmul(c.ps[n][:], ol, wh, start=False, stop=(k == n_k - 1))
                    if k == n_k - 1:
                        last.then_inc(S["summed"], 1)
                if k < n_k - 1:
                    last.then_inc(S["used"], 1)

        @block.vector
        def _(dve):
            for k in range(n_k):
                dve.wait_ge(S["o_hi"], k + 1)
                dve.tensor_tensor(o_lo[:, k % WS, :], oT[:, k, :], o_hi[:, k % WS, :].bitcast(F32),
                                  ALU.subtract).then_inc(S["o_lo"], 1)
            for n in range(2 * TT):
                dve.wait_ge(S["summed"], n + 1)
                o = c.h[:, n // 2, n % 2 * 512:(n % 2 + 1) * 512]
                dve.tensor_tensor(o, c.ps[n][:], o, ALU.add)


def even_layer(c, A):
    nc = c.nc
    with ExitStack() as st:
        def sb(n, shape):
            return st.enter_context(nc.sbuf_tensor(f"even_{n}", shape, F32))

        R = dict(
            Qf=sb("Qf", [97, NH, SEQ]), Kf=sb("Kf", [97, NH, SEQ]), Vf=sb("Vf", [P, TT, NH * DH]),
            Qn=sb("Qn", [DH, NH, SEQ]), Kn=sb("Kn", [DH, 2 * GROUPS, SEQ]), Vn=sb("Vn", [P, TT, 2 * P]),
            gates=sb("gates", [P, TT, 3 * NH]), kc=sb("kc", [DH, GROUPS, N_CMP]), vc=sb("vc", [N_CMP, GROUPS, DH]))
        with ExitStack() as st2:
            R["Kc"] = st2.enter_context(nc.sbuf_tensor("even_Kc", [DH, 2 * GROUPS, SEQ], F32))
            hi = st2.enter_context(nc.sbuf_tensor("even_hn_hi", [P, KD, SEQ], F32R))
            lo = st2.enter_context(nc.sbuf_tensor("even_hn_lo", [P, KD, SEQ], F32R))
            W = EvenInputs(c, A, st2, R)
            norm_block(c, "even_norm", A["even_norm_g"][0], hi, lo, W.first_loads)
            even_project(c, W, R, hi, lo)
        w_loaded = c.sem("even_w_out_loaded")
        oT, w_out = sb("oT", [P, KD, SEQ]), sb("w_out", [P, KD, D])
        even_attend(c, R, oT, w_out, w_loaded, A["even_w_out"][0])
        project_out(c, "even_out", oT, KD, [(0, w_out, w_loaded)])


class RecurrentWeights:

    SLOTS = 4
    UNITS = 2 * NR

    def __init__(self, c, A, st):
        def sb(n, shape):
            return st.enter_context(c.nc.sbuf_tensor(f"lru_{n}", shape, F32))

        self.A = A
        self.w = sb("w_in", [P, self.SLOTS, KD, P])
        self.cw = sb("cw", [P, CONV_W, NR])
        self.cb, self.ba, self.bi, self.lam = (sb(n, [P, NR]) for n in ("cb", "ba", "bi", "lam"))
        self.wa, self.wi = sb("wa", [P, NR, P]), sb("wi", [P, NR, P])
        self.w_loaded = [c.sem(f"lru_w_in{i}") for i in range(self.SLOTS)]
        self.small_loaded, self.gates_loaded = c.sem("lru_small"), c.sem("lru_gates")
        self.SMALL = 16 * (CONV_W + 4)

    def load_unit(self, sp, n):
        col = D_RNN + n * P if n < NR else (n - NR) * P
        sp.dma_start(self.w[:, n % self.SLOTS],
                     self.A["odd_w_in"][0, :, col:col + P].rearrange("(k p) n -> p k n", p=P)) \
            .then_inc(self.w_loaded[n % self.SLOTS], 16)

    def first_loads(self, sp):
        A, loaded, small = self.A, self.small_loaded, dict(allow_slow_non_contiguous=True)
        for n in range(2):
            self.load_unit(sp, n)
        sp.dma_start(self.lam[:], A["odd_lam"][0].rearrange("(n p) -> p n", p=P), **small).then_inc(loaded, 16)
        sp.dma_start(self.cb[:], A["odd_conv_b"][0].rearrange("(n p) -> p n", p=P), **small).then_inc(loaded, 16)
        for j in range(CONV_W):
            sp.dma_start(self.cw[:, j, :], A["odd_conv_w"][0, j].rearrange("(n p) -> p n", p=P), **small) \
                .then_inc(loaded, 16)
        sp.dma_start(self.ba[:], A["odd_b_ra"][0].rearrange("(n p) -> p n", p=P), **small).then_inc(loaded, 16)
        sp.dma_start(self.bi[:], A["odd_b_ri"][0].rearrange("(n p) -> p n", p=P), **small).then_inc(loaded, 16)
        for n in range(2, self.SLOTS):
            self.load_unit(sp, n)
        sp.dma_start(self.wa[:], A["odd_w_ra"][0].rearrange("n c e -> c n e")).then_inc(self.gates_loaded, 16)
        sp.dma_start(self.wi[:], A["odd_w_ri"][0].rearrange("n c e -> c n e")).then_inc(self.gates_loaded, 16)


def odd_mix(c, W, hi, lo, gate, w_first, w_first_dram, w_first_loaded):
    nc = c.nc
    S = {s: c.sem(f"lru_{s}") for s in (
        "w_hi", "w_lo", "unit", "xr", "gelu", "chain", "exps", "soft", "conv", "y", "product", "ri", "tanh", "ix",
        "decay", "root", "rix", "u", "scan")}
    WS = 3
    UB, PB = 4, 4
    LAG = 3
    with ExitStack() as st:
        def sb(n, shape, dt=F32):
            return st.enter_context(nc.sbuf_tensor(f"lru_{n}", shape, dt))

        w_hi, w_lo = sb("w_hi", [P, WS, KD, P], F32R), sb("w_lo", [P, WS, KD, P], F32R)
        e, d, z, q, pp, soft, neg = (sb(n, [P, NR]) for n in ("e", "d", "z", "q", "p", "soft", "neg"))
        xr = sb("xr", [P, 2, CONV_W - 1 + SEQ])
        y = sb("y", [P, 2, SEQ])
        r, i_ = sb("r", [P, 2, SEQ]), sb("i", [P, 2, SEQ])
        s_ = sb("s", [P, NR, SEQ])
        ix = sb("ix", [P, NR, SEQ])
        a = gate
        u = sb("u", [P, 2, SEQ])
        block = st.enter_context(nc.Block())

        @block.sync
        def _(sp):
            for n in range(W.SLOTS, W.UNITS):
                sp.wait_ge(S["w_hi"], n - W.SLOTS + 1)
                sp.wait_ge(S["w_lo"], n - W.SLOTS + 1)
                W.load_unit(sp, n)
            sp.dma_start(w_first[:], w_first_dram).then_inc(w_first_loaded, 16)

        @block.tensor
        def _(pe):
            def products(n):
                pe.wait_ge(S["y"], n + 1)
                if n >= 2:
                    pe.wait_ge(S["ri"], 2 * n - 2)
                for g, wg in enumerate((W.wa, W.wi)):
                    pe.matmul(c.ps[PB + 2 * (n % 2) + g][:], wg[:, n, :], y[:, n % 2, :], start=True,
                              stop=True).then_inc(S["product"], 1)

            for n in range(W.UNITS):
                pe.wait_ge(S["w_hi"], n + 1)
                pe.wait_ge(S["w_lo"], n + 1)
                if n >= UB:
                    if n - UB < NR:
                        pe.wait_ge(S["xr"], n - UB + 1)
                    else:
                        pe.wait_ge(S["gelu"], n - UB - NR + 1)
                b = c.ps[n % UB]
                for k in range(KD):
                    wh, wl = w_hi[:, n % WS, k, :], w_lo[:, n % WS, k, :]
                    pe.matmul(b[:], wh, hi[:, k, :], start=(k == 0), stop=False)
                    pe.matmul(b[:], wh, lo[:, k, :], start=False, stop=False)
                    last = pe.matmul(b[:], wl, hi[:, k, :], start=False, stop=(k == KD - 1))
                last.then_inc(S["unit"], 1)
                if n == 1:
                    pe.wait_ge(W.gates_loaded, 32)
                if 1 <= n <= NR:
                    products(n - 1)

        @block.scalar
        def _(act):
            def split(n):
                act.wait_ge(W.w_loaded[n % W.SLOTS], 16 * (n // W.SLOTS + 1))
                if n >= WS:
                    act.wait_ge(S["unit"], n - WS + 1)
                act.activation(w_hi[:, n % WS], W.w[:, n % W.SLOTS], ACT.Copy).then_inc(S["w_hi"], 1)

            def gates(n):
                act.wait_ge(S["product"], 2 * n + 1)
                act.activation(r[:, n % 2, :], c.ps[PB + 2 * (n % 2)][:], ACT.Sigmoid, bias=W.ba[:, n:n + 1]) \
                    .then_inc(S["ri"], 1)
                act.wait_ge(S["product"], 2 * n + 2)
                if n >= 2:
                    act.wait_ge(S["ix"], n - 1)
                act.activation(i_[:, n % 2, :], c.ps[PB + 2 * (n % 2) + 1][:], ACT.Sigmoid, bias=W.bi[:, n:n + 1]) \
                    .then_inc(S["ri"], 1)
                act.wait_ge(S["ri"], 2 * n + 1)
                if n == 0:
                    act.wait_ge(S["soft"], 1)
                act.activation(s_[:, n, :], r[:, n % 2, :], ACT.Tanh, scale=soft[:, n:n + 1]).then_inc(S["tanh"], 1)
                act.activation(a[:, n, :], r[:, n % 2, :], ACT.Exp, scale=neg[:, n:n + 1]).then_inc(S["decay"], 1)

            split(0)
            act.wait_ge(W.small_loaded, W.SMALL)
            act.activation(e[:], W.lam[:], ACT.Abs).then_inc(S["exps"], 1)
            act.wait_ge(S["exps"], 1)
            act.activation(e[:], e[:], ACT.Exp, scale=-1.0).then_inc(S["exps"], 1)
            for n in range(1, WS):
                split(n)
            for n in range(NR + 1):
                split(n + WS)
                if n >= 1:
                    gates(n - 1)
            for n in range(NR):
                act.wait_ge(S["tanh"], n + 1)
                act.activation(s_[:, n, :], s_[:, n, :], ACT.Sqrt).then_inc(S["root"], 1)
            for n in range(NR):
                if NR + 1 + n + WS < W.UNITS:
                    split(NR + 1 + n + WS)
                act.wait_ge(S["unit"], NR + n + 1)
                act.wait_ge(S["scan"], n + 1)
                act.activation(gate[:, n, :], c.ps[(NR + n) % UB][:], ACT.Gelu).then_inc(S["gelu"], 1)

        @block.gpsimd
        def _(pool):
            def split(n):
                pool.wait_ge(S["w_hi"], n + 1)
                pool.tensor_tensor(w_lo[:, n % WS], W.w[:, n % W.SLOTS], w_hi[:, n % WS].bitcast(F32),
                                   ALU.subtract).then_inc(S["w_lo"], 1)

            for n in range(WS):
                split(n)
            for n in range(NR + 1):
                split(n + WS)
                if n >= 1:
                    pool.wait_ge(S["ri"], 2 * n)
                    pool.tensor_tensor(ix[:, n - 1, :], i_[:, (n - 1) % 2, :], y[:, (n - 1) % 2, :],
                                       ALU.mult).then_inc(S["ix"], 1)
            for n in range(NR):
                pool.wait_ge(S["ix"], n + 1)
                pool.wait_ge(S["root"], n + 1)
                pool.tensor_tensor(ix[:, n, :], ix[:, n, :], s_[:, n, :], ALU.mult).then_inc(S["rix"], 1)
                if NR + 1 + n + WS < W.UNITS:
                    split(NR + 1 + n + WS)

        @block.vector
        def _(dve):
            dve.memset(xr[:, :, 0:CONV_W - 1], 0.0)
            dve.wait_ge(W.small_loaded, W.SMALL)
            dve.wait_ge(S["exps"], 2)
            at = half_log1p(dve, S["chain"], 0, e[:], d[:], z[:], q[:], pp[:])
            dve.tensor_scalar(d[:], W.lam[:], -4.0, 0.0, ALU.mult, ALU.max).then_inc(S["chain"], 1)
            dve.wait_ge(S["chain"], at + 1)
            dve.scalar_tensor_tensor(soft[:], pp[:], 8.0, d[:], ALU.mult, ALU.add).then_inc(S["chain"], 1)
            dve.wait_ge(S["chain"], at + 2)
            dve.tensor_scalar(neg[:], soft[:], -2.0, None, ALU.mult).then_inc(S["soft"], 1)
            for n in range(NR):
                x, yn = xr[:, n % 2], y[:, n % 2, :]
                dve.wait_ge(S["unit"], n + 1)
                if n >= 2:
                    dve.wait_ge(S["y"], n - 1)
                dve.tensor_copy(x[:, CONV_W - 1:], c.ps[n % UB][:]).then_inc(S["xr"], 1)
                dve.wait_ge(S["xr"], n + 1)
                if n >= 2:
                    dve.wait_ge(S["ix"], n - 1)
                    dve.wait_ge(S["product"], 2 * n - 2)
                dve.tensor_scalar(yn, x[:, 0:SEQ], W.cw[:, 0, n:n + 1], W.cb[:, n:n + 1], ALU.mult,
                                  ALU.add).then_inc(S["conv"], 1)
                for j in range(1, CONV_W):
                    dve.wait_ge(S["conv"], (CONV_W - 1) * n + j)
                    last = dve.scalar_tensor_tensor(yn, x[:, j:j + SEQ], W.cw[:, j, n:n + 1], yn, ALU.mult, ALU.add)
                    last.then_inc(S["conv"] if j < CONV_W - 1 else S["y"], 1)

            for n in range(NR + LAG):
                if n < NR:
                    if n >= 2:
                        dve.wait_ge(S["scan"], n - 1)
                    dve.wait_ge(S["decay"], n + 1)
                    dve.wait_ge(S["rix"], n + 1)
                    dve.scalar_tensor_tensor(u[:, n % 2, :], a[:, n, :], 1.0, ix[:, n, :], ALU.add,
                                             ALU.mult).then_inc(S["u"], 1)
                    dve.wait_ge(S["u"], n + 1)
                    dve.tensor_tensor_scan(ix[:, n, :], a[:, n, :], u[:, n % 2, :], 0.0, ALU.mult,
                                           ALU.add).then_inc(S["scan"], 1)
                if n >= LAG:
                    m = n - LAG
                    dve.wait_ge(S["gelu"], m + 1)
                    dve.wait_ge(S["scan"], m + 1)
                    dve.tensor_tensor(gate[:, m, :], gate[:, m, :], ix[:, m, :], ALU.mult)


def odd_layer(c, A):
    nc = c.nc
    FIRST, PIECE = 4, 2
    w_dram = A["odd_w_out"][0].rearrange("(k p) n -> p k n", p=P)
    with ExitStack() as st:
        gate = st.enter_context(nc.sbuf_tensor("odd_gate", [P, NR, SEQ], F32))
        w_first = st.enter_context(nc.sbuf_tensor("odd_w_first", [P, FIRST, D], F32))
        pieces = range(FIRST, NR, PIECE)
        loaded = [c.sem(f"odd_w_out{i}") for i in range(1 + len(pieces))]
        with ExitStack() as st2:
            hi = st2.enter_context(nc.sbuf_tensor("odd_hn_hi", [P, KD, SEQ], F32R))
            lo = st2.enter_context(nc.sbuf_tensor("odd_hn_lo", [P, KD, SEQ], F32R))
            W = RecurrentWeights(c, A, st2)
            norm_block(c, "odd_norm", A["odd_norm_g"][0], hi, lo, W.first_loads)
            odd_mix(c, W, hi, lo, gate, w_first, w_dram[:, 0:FIRST], loaded[0])
        w_rest = st.enter_context(nc.sbuf_tensor("odd_w_rest", [P, NR - FIRST, D], F32))
        parts = [(0, w_first, loaded[0])]
        parts += [(k, w_rest[:, k - FIRST:k - FIRST + PIECE], loaded[1 + i]) for i, k in enumerate(pieces)]

        def rest(sp):
            for k, rows, done in parts[1:]:
                sp.dma_start(rows, w_dram[:, k:k + PIECE]).then_inc(done, 16)

        project_out(c, "odd_out", gate, NR, parts, rest)


WIDE = 4
NARROW = 4
CAND = WIDE * TOPK + (TOPK - WIDE) * NARROW


def expert_rows(tab):
    return tab.rearrange("(i j) d -> i j d", i=P)


class Experts:

    def __init__(self, c, name, st, u_tab, v_tab):
        self.uv, self.vv = expert_rows(u_tab), expert_rows(v_tab)
        self.u = st.enter_context(c.nc.sbuf_tensor(f"{name}_u", [P, 2, 2, D], F32))
        self.ahead = st.enter_context(c.nc.sbuf_tensor(f"{name}_ahead", [P, AHEAD, SEQ], F32))
        self.sems = {s: c.sem(f"{name}_{s}") for s in ("turned", "u_hi", "u_lo", "act", "gelu")}
        self.u_loaded = [c.sem(f"{name}_u{r}") for r in range(2)]
        self.v_loaded = [c.sem(f"{name}_v{r}") for r in range(2)]

    def make_v(self, c, name, st):
        self.v = st.enter_context(c.nc.sbuf_tensor(f"{name}_v", [P, 2, GRP, 512], F32))

    def load_u(self, sp, s, r):
        sp.dma_start(self.u[:, r], self.uv[:, bass.ds(s * 2, 2), :]).then_inc(self.u_loaded[r], 16)

    def load_v(self, sp, i, r):
        sp.dma_start(self.v[:, r], self.vv[:, bass.ds(i * GRP, GRP), r * 512:(r + 1) * 512]) \
            .then_inc(self.v_loaded[r], 16)


class PickInputs:

    SLOTS = 4

    def __init__(self, c, name, st, w_q, sub_keys, tables):
        self.w_q, self.sub_keys, self.tables = w_q, sub_keys, tables
        self.w = st.enter_context(c.nc.sbuf_tensor(f"{name}_w_q", [P, self.SLOTS, KD, P], F32))
        self.keys = st.enter_context(c.nc.sbuf_tensor(f"{name}_keys", [P, HC, P], F32))
        self.w_loaded = [c.sem(f"{name}_w_q{i}") for i in range(self.SLOTS)]
        self.keys_loaded = c.sem(f"{name}_keys_loaded")

    def load_w(self, sp, n):
        sp.dma_start(self.w[:, n % self.SLOTS], self.w_q[:, n * P:(n + 1) * P].rearrange("(k p) n -> p k n", p=P)) \
            .then_inc(self.w_loaded[n % self.SLOTS], 16)

    def first_loads(self, sp):
        self.load_w(sp, 0)
        sp.dma_start(self.keys[:], self.sub_keys.rearrange("h c k d -> k (h c) d")).then_inc(self.keys_loaded, 16)
        for n in range(1, self.SLOTS):
            self.load_w(sp, n)
        for r in range(2):
            self.tables.load_u(sp, r, r)


def peer_pick(c, name, hi, lo, W, tables, picks, gates, gate_low, iota):
    nc = c.nc
    S = {s: c.sem(f"{name}_{s}") for s in (
        "w_hi", "w_lo", "keysT", "keysT_out", "q", "q_out", "sc", "sc_out", "chain", "place",
        "float", "onehot", "half", "indexed", "exp", "turn")}
    WS = 3

    HALF_STEPS = ("max", "strike", "max2", "index2")
    HEAD_STEPS = ("cand", "bmax", "bstrike", "bmax2", "bindex2", "shift", "wide", "row", "column", "eq")
    steps = []
    for n in range(HC + 2):
        mine = [(s, n) for s in HALF_STEPS] if n < HC else []
        h = n // 2 - 1
        before = [(s, h) for s in (HEAD_STEPS[5:] if n % 2 else HEAD_STEPS[:5])] if h >= 0 else []
        for i in range(5):
            steps += mine[i:i + 1] + before[i:i + 1]
        if n % 2 and h >= 1:
            steps.append(("gather", h - 1))
    steps += [("sub", 0), ("sum", 0), ("recip", 0), ("weigh", 0), ("gather", PH - 1)]
    done = {s: i + 1 for i, s in enumerate(steps)}
    TF = 4
    SPLIT_AT = [5 * (HC - 4) + 2 + 4 * j for j in range(AHEAD - 1)]
    FLOATS_AT = (1, 2, 4, 5)
    EXP_AT = AHEAD - 1
    RESULTS_AT = AHEAD - 2

    with ExitStack() as st:
        def sb(n, shape, dt=F32):
            return st.enter_context(nc.sbuf_tensor(f"{name}_{n}", shape, dt))

        w, keys = W.w, W.keys
        w_hi, w_lo = sb("w_hi", [P, WS, KD, P], F32R), sb("w_lo", [P, WS, KD, P], F32R)
        keysT = sb("keysT", [P, HC, P])
        qT = sb("qT", [P, 2, SEQ])
        sc = sb("sc", [P, TT, 4, P])
        left = sb("left", [P, TT, P])
        top_v = sb("top_v", [P, HC, TT, TOPK])
        top_i = sb("top_i", [P, HC, TT, TOPK], U32)
        top_f = sb("top_f", [P, TF, 2, TT, TOPK], F16)
        cand = sb("cand", [P, TT, CAND])
        rest = sb("rest", [P, TT, CAND])
        best = sb("best", [P, TT, PH, TOPK])
        best_i = sb("best_i", [P, TT, PH, TOPK], U32)
        sh = sb("sh", [P, 2, TT, TOPK], U32)
        shf = sb("shf", [P, 3, TT, TOPK])
        ab = sb("ab", [P, 2, TT, TOPK], F16)
        eq = sb("eq", [P, 2, 2, TT, TOPK, TOPK], F16)
        iota16 = sb("iota16", [P, TOPK, TOPK], F16)
        i12 = sb("i12", [P, 2, TT, PH, TOPK])
        e = sb("e", [P, TT, PH, TOPK])
        z = sb("z", [P, TT, PH])
        rz = sb("rz", [P, TT, PH])
        gT = sb("gT", [P, SEQ])
        T = tables.sems
        TURN, ACTB, LAST = 0, 2, 4
        block = st.enter_context(nc.Block())

        @block.sync
        def _(sp):
            for n in range(W.SLOTS, HC):
                sp.wait_ge(S["w_hi"], n - W.SLOTS + 1)
                sp.wait_ge(S["w_lo"], n - W.SLOTS + 1)
                W.load_w(sp, n)
            for s in range(2, AHEAD // 2):
                sp.wait_ge(T["turned"], 4 * s - 4)
                tables.load_u(sp, s, s % 2)

        @block.tensor
        def _(pe):
            def turn_keys(g):
                pe.wait_ge(W.keys_loaded, 16)
                for j in range(4):
                    last = pe.transpose(c.ps[g][:, j * P:(j + 1) * P], keys[:, 4 * g + j, :], c.ident[:])
                last.then_inc(S["keysT"], 1)

            def scores(n):
                pe.wait_ge(S["q_out"], n + 1)
                pe.wait_ge(S["keysT_out"], n // 4 + 1)
                if n >= 2:
                    pe.wait_ge(S["sc_out"], n - 1)
                for t in range(TT):
                    last = pe.matmul(c.ps[6 + n % 2][:, t * P:(t + 1) * P], qT[:, n % 2, t * P:(t + 1) * P],
                                     keysT[:, n, :], start=True, stop=True)
                last.then_inc(S["sc"], 1)

            turn_keys(0)
            for n in range(HC):
                pe.wait_ge(S["w_hi"], n + 1)
                pe.wait_ge(S["w_lo"], n + 1)
                if n >= 2:
                    pe.wait_ge(S["q_out"], n - 1)
                b = c.ps[4 + n % 2]
                for k in range(KD):
                    wh, wl = w_hi[:, n % WS, k, :], w_lo[:, n % WS, k, :]
                    pe.matmul(b[:], wh, hi[:, k, :], start=(k == 0), stop=False)
                    pe.matmul(b[:], wh, lo[:, k, :], start=False, stop=False)
                    last = pe.matmul(b[:], wl, hi[:, k, :], start=False, stop=(k == KD - 1))
                last.then_inc(S["q"], 1)
                if 1 <= n < 4:
                    turn_keys(n)
                if n >= 3:
                    scores(n - 1)
                if n < 2 or n == HC - 1:
                    scores(n)
            def turn_u(j):
                if j % 2 == 0:
                    pe.wait_ge(tables.u_loaded[j // 2 % 2], 16 * (j // 4 + 1))
                if j >= 1:
                    pe.wait_ge(T["u_lo"], 2 * j)
                for b in range(2):
                    for k in range(4):
                        last = pe.transpose(c.ps[TURN + b][:, k * P:(k + 1) * P],
                                            tables.u[:, j // 2 % 2, j % 2, (4 * b + k) * P:(4 * b + k + 1) * P],
                                            c.ident[:])
                    last.then_inc(T["turned"], 1)

            def activations(j):
                pe.wait_ge(T["u_hi"], 2 * j + 2)
                pe.wait_ge(T["u_lo"], 2 * j + 2)
                if j >= 2:
                    pe.wait_ge(T["gelu"], j - 1)
                o = c.ps[ACTB + j % 2]
                if j + 1 < AHEAD:
                    turn_u(j + 1)
                for k in range(KD):
                    uh, ul = w_hi[:, (HC + j) % WS, k, :], w_lo[:, (HC + j) % WS, k, :]
                    pe.matmul(o[:], uh, hi[:, k, :], start=(k == 0), stop=False)
                    pe.matmul(o[:], uh, lo[:, k, :], start=False, stop=False)
                    last = pe.matmul(o[:], ul, hi[:, k, :], start=False, stop=(k == KD - 1))
                last.then_inc(T["act"], 1)

            def results(s, src, step):
                pe.wait_ge(S["chain"], done[step])
                if s == 2:
                    pe.wait_ge(S["sc_out"], HC)
                for t in range(TT):
                    last = pe.transpose(c.ps[LAST + s][:, t * P:(t + 1) * P], src[:, t].rearrange("p h k -> p (h k)"),
                                        c.ident[:])
                last.then_inc(S["turn"], 1)

            pe.wait_ge(S["keysT_out"], 4)
            pe.wait_ge(S["q_out"], HC)
            turn_u(0)
            for j in range(AHEAD):
                activations(j)
                if j == RESULTS_AT:
                    results(0, e, ("weigh", 0))
                    for s in range(2):
                        results(1 + s, i12[:, s], ("gather", PH - 1))

        @block.scalar
        def _(act):
            def split(n):
                act.wait_ge(W.w_loaded[n % W.SLOTS], 16 * (n // W.SLOTS + 1))
                if n >= WS:
                    act.wait_ge(S["q"], n - WS + 1)
                act.activation(w_hi[:, n % WS], w[:, n % W.SLOTS], ACT.Copy).then_inc(S["w_hi"], 1)

            def floats(n):
                act.wait_ge(S["chain"], done["index2", n])
                if n >= 2 * TF:
                    act.wait_ge(S["onehot"], 2 * (n // 2 - TF + 1))
                act.activation(top_f[:, n // 2 % TF, n % 2], top_i[:, n], ACT.Copy).then_inc(S["float"], 1)

            def split_u(j):
                m = HC + j
                if m - WS < HC:
                    act.wait_ge(S["q"], m - WS + 1)
                else:
                    act.wait_ge(T["act"], j - WS + 1)
                for b in range(2):
                    act.wait_ge(T["turned"], 2 * j + b + 1)
                    act.activation(w_hi[:, m % WS, 4 * b:4 * b + 4, :].rearrange("p k i -> p (k i)"),
                                   c.ps[TURN + b][:], ACT.Copy).then_inc(T["u_hi"], 1)

            def gelu(j):
                act.wait_ge(T["act"], j + 1)
                act.activation(tables.ahead[:, j, :], c.ps[ACTB + j % 2][:], ACT.Gelu).then_inc(T["gelu"], 1)

            split(0)
            split(1)
            for n in range(HC + 1):
                if n + 2 < HC:
                    split(n + 2)
                if n < HC:
                    act.wait_ge(S["q"], n + 1)
                    if n >= 2:
                        act.wait_ge(S["sc"], n - 1)
                    act.activation(qT[:, n % 2, :], c.ps[4 + n % 2][:], ACT.Copy).then_inc(S["q_out"], 1)
                if n < 4:
                    act.wait_ge(S["keysT"], n + 1)
                    act.activation(keysT[:, 4 * n:4 * n + 4, :], c.ps[n][:].rearrange("p (j k) -> p j k", j=4),
                                   ACT.Copy).then_inc(S["keysT_out"], 1)
                if n < 2 or 3 <= n <= HC:
                    m = n if n < 2 else n - 1
                    act.wait_ge(S["sc"], m + 1)
                    if m >= 4:
                        act.wait_ge(S["chain"], done["max2", m - 4])
                    act.activation(sc[:, :, m % 4, :], c.ps[6 + m % 2][:].rearrange("p (t k) -> p t k", t=TT),
                                   ACT.Copy).then_inc(S["sc_out"], 1)
                if 4 <= n < HC:
                    floats(n - 4)
            for j in range(AHEAD):
                split_u(j)
                if j == EXP_AT:
                    act.wait_ge(S["chain"], done["sub", 0])
                    act.activation(e[:], e[:], ACT.Exp).then_inc(S["exp"], 1)
                if j >= 1:
                    gelu(j - 1)
                if j in FLOATS_AT:
                    floats(HC - 4 + FLOATS_AT.index(j))
            act.wait_ge(S["turn"], 3)
            act.activation(picks[1][:], c.ps[LAST + 2][:], ACT.Copy)
            gelu(AHEAD - 1)

        @block.gpsimd
        def _(pool):

            def split(n):
                pool.wait_ge(S["w_hi"], n + 1)
                pool.tensor_tensor(w_lo[:, n % WS], w[:, n % W.SLOTS], w_hi[:, n % WS].bitcast(F32),
                                   ALU.subtract).then_inc(S["w_lo"], 1)

            def index(h):
                pool.wait_ge(S["chain"], done["eq", h])
                pool.wait_ge(S["float"], 2 * h + 2)
                for s in range(2):
                    x = eq[:, h % 2, s]
                    pool.tensor_tensor(x, x, bc(top_f[:, h % TF, s].unsqueeze(3), [P, TT, TOPK, TOPK]),
                                       ALU.mult).then_inc(S["onehot"], 1)
                for s in range(2):
                    x = eq[:, h % 2, s]
                    pool.wait_ge(S["onehot"], 2 * h + s + 1)
                    pool.tensor_tensor(x[:, :, 0:8], x[:, :, 0:8], x[:, :, 8:16], ALU.add).then_inc(S["half"], 1)
                for s in range(2):
                    x = eq[:, h % 2, s]
                    pool.wait_ge(S["half"], 2 * h + s + 1)
                    pool.tensor_tensor(x[:, :, 0:4], x[:, :, 0:4], x[:, :, 4:8], ALU.add).then_inc(S["indexed"], 1)

            for n in range(HC):
                split(n)
                if n == 2:
                    pool.iota(iota16[:], [[1, TOPK], [0, TOPK]], base=0, channel_multiplier=0,
                              allow_small_or_imprecise_dtypes=True).then_inc(S["place"], 1)
                    pool.iota(iota[:], [[1, NK], [0, BATCH]], base=0, channel_multiplier=0,
                              allow_small_or_imprecise_dtypes=True)
                if n % 2 == 0 and n >= 8:
                    index(n // 2 - 4)
            for h in range(PH - 4, PH):
                index(h)

        @block.vector
        def _(dve):
            chain = S["chain"]

            def gather(h):
                dve.wait_ge(S["indexed"], 2 * h + 2)
                for s in range(2):
                    last = dve.tensor_reduce(i12[:, s, :, h, :],
                                             eq[:, h % 2, s, :, 0:4, :].rearrange("p t m k -> p t k m"), X, ALU.add)
                last.then_inc(chain, 1)

            def half_max(n):
                dve.wait_ge(S["sc_out"], n + 1)
                for t in range(TT):
                    last = dve.max(top_v[:, n, t, 0:8], sc[:, t, n % 4, :])
                last.then_inc(chain, 1)

            def half_strike(n):
                dve.wait_ge(chain, done["max", n])
                if n >= 1:
                    dve.wait_ge(chain, done["index2", n - 1])
                for t in range(TT):
                    last = dve.match_replace(left[:, t, :], top_v[:, n, t, 0:8], sc[:, t, n % 4, :], -BIG)
                last.then_inc(chain, 1)

            def half_max2(n):
                dve.wait_ge(chain, done["strike", n])
                for t in range(TT):
                    dve.max(top_v[:, n, t, 8:16], left[:, t, :])
                    last = dve.max_index(top_i[:, n, t, 0:8], top_v[:, n, t, 0:8], sc[:, t, n % 4, :])
                last.then_inc(chain, 1)

            def half_index2(n):
                dve.wait_ge(chain, done["max2", n])
                for t in range(TT):
                    last = dve.max_index(top_i[:, n, t, 8:16], top_v[:, n, t, 8:16], left[:, t, :])
                last.then_inc(chain, 1)

            def sums(h):
                v0, v1 = top_v[:, 2 * h], top_v[:, 2 * h + 1]
                wide_sums = WIDE * TOPK
                dve.wait_ge(chain, done["max2", 2 * h + 1])
                dve.tensor_tensor(cand[:, :, 0:wide_sums].rearrange("p t (a b) -> p t a b", a=WIDE),
                                  bc(v0[:, :, 0:WIDE].unsqueeze(3), [P, TT, WIDE, TOPK]),
                                  bc(v1.unsqueeze(2), [P, TT, WIDE, TOPK]), ALU.add)
                dve.tensor_tensor(cand[:, :, wide_sums:CAND].rearrange("p t (a b) -> p t a b", b=NARROW),
                                  bc(v0[:, :, WIDE:TOPK].unsqueeze(3), [P, TT, TOPK - WIDE, NARROW]),
                                  bc(v1[:, :, 0:NARROW].unsqueeze(2), [P, TT, TOPK - WIDE, NARROW]),
                                  ALU.add).then_inc(chain, 1)

            def sums_max(h):
                dve.wait_ge(chain, done["cand", h])
                for t in range(TT):
                    last = dve.max(best[:, t, h, 0:8], cand[:, t, :])
                last.then_inc(chain, 1)

            def sums_strike(h):
                dve.wait_ge(chain, done["bmax", h])
                for t in range(TT):
                    last = dve.match_replace(rest[:, t, :], best[:, t, h, 0:8], cand[:, t, :], -BIG)
                last.then_inc(chain, 1)

            def sums_max2(h):
                dve.wait_ge(chain, done["bstrike", h])
                for t in range(TT):
                    dve.max(best[:, t, h, 8:16], rest[:, t, :])
                    last = dve.max_index(best_i[:, t, h, 0:8], best[:, t, h, 0:8], cand[:, t, :])
                last.then_inc(chain, 1)

            def sums_index2(h):
                dve.wait_ge(chain, done["bmax2", h])
                for t in range(TT):
                    last = dve.max_index(best_i[:, t, h, 8:16], best[:, t, h, 8:16], rest[:, t, :])
                last.then_inc(chain, 1)

            def shift(h):
                place = best_i[:, :, h, :]
                dve.wait_ge(chain, done["bindex2", h])
                dve.tensor_scalar(sh[:, 0], place, 4, None, ALU.logical_shift_right)
                dve.tensor_scalar(sh[:, 1], place, 2, None, ALU.logical_shift_right).then_inc(chain, 1)

            def wide(h):
                dve.wait_ge(chain, done["shift", h])
                dve.tensor_scalar(shf[:, 0], sh[:, 0], float(WIDE), None, ALU.min)
                dve.tensor_scalar(shf[:, 1], sh[:, 1], float(WIDE * TOPK // NARROW), 0.0, ALU.subtract,
                                  ALU.max).then_inc(chain, 1)

            def row(h):
                dve.wait_ge(chain, done["wide", h])
                dve.tensor_tensor(ab[:, 0], shf[:, 0], shf[:, 1], ALU.add)
                dve.scalar_tensor_tensor(shf[:, 2], shf[:, 0], float(TOPK // NARROW), shf[:, 1], ALU.mult,
                                         ALU.add).then_inc(chain, 1)

            def column(h):
                dve.wait_ge(chain, done["row", h])
                dve.scalar_tensor_tensor(ab[:, 1], shf[:, 2], -float(NARROW), best_i[:, :, h, :], ALU.mult,
                                         ALU.add).then_inc(chain, 1)

            def onehots(h):
                dve.wait_ge(chain, done["column", h])
                if h == 0:
                    dve.wait_ge(S["place"], 1)
                if h >= 2:
                    dve.wait_ge(chain, done["gather", h - 2])
                for s in range(2):
                    last = dve.tensor_tensor(eq[:, h % 2, s], bc(ab[:, s].unsqueeze(2), [P, TT, TOPK, TOPK]),
                                             bc(iota16[:].unsqueeze(1), [P, TT, TOPK, TOPK]), ALU.is_equal)
                last.then_inc(chain, 1)

            def split_u(j):
                m = HC + j
                for b in range(2):
                    dve.wait_ge(T["u_hi"], 2 * j + b + 1)
                    part = slice(4 * b, 4 * b + 4)
                    dve.tensor_tensor(w_lo[:, m % WS, part, :].rearrange("p k i -> p (k i)"), c.ps[TURN + b][:],
                                      w_hi[:, m % WS, part, :].rearrange("p k i -> p (k i)").bitcast(F32),
                                      ALU.subtract).then_inc(T["u_lo"], 1)

            half_parts = (half_max, half_strike, half_max2, half_index2)
            head_parts = (sums, sums_max, sums_strike, sums_max2, sums_index2, shift, wide, row, column, onehots)
            for n in range(HC + 2):
                h = n // 2 - 1
                for i in range(5):
                    if n < HC and i < 4:
                        half_parts[i](n)
                    if h >= 0:
                        head_parts[5 * (n % 2) + i](h)
                    if 5 * n + i in SPLIT_AT:
                        split_u(SPLIT_AT.index(5 * n + i))
                if n % 2 and h >= 1:
                    gather(h - 1)
            b3, e3 = best[:].rearrange("p t h k -> p (t h) k"), e[:].rearrange("p t h k -> p (t h) k")
            z2, rz2 = z[:].rearrange("p t h -> p (t h)"), rz[:].rearrange("p t h -> p (t h)")
            dve.tensor_tensor(e3, b3, bc(b3[:, :, 0:1], [P, TT * PH, TOPK]), ALU.subtract).then_inc(chain, 1)
            split_u(AHEAD - 1)
            dve.wait_ge(S["exp"], 1)
            dve.tensor_reduce(z2, e3, X, ALU.add).then_inc(chain, 1)
            dve.wait_ge(chain, done["sum", 0])
            dve.reciprocal(rz2, z2).then_inc(chain, 1)
            dve.wait_ge(chain, done["recip", 0])
            dve.scalar_tensor_tensor(e3, e3, GSCALE, bc(rz2.unsqueeze(2), [P, TT * PH, TOPK]), ALU.mult,
                                     ALU.mult).then_inc(chain, 1)
            gather(PH - 1)
            dve.wait_ge(S["turn"], 1)
            dve.tensor_copy(gT[:], c.ps[LAST][:]).then_inc(chain, 1)
            dve.wait_ge(chain, len(steps) + 1)
            dve.tensor_copy(gates[0][:], gT[:]).then_inc(chain, 1)
            dve.wait_ge(chain, len(steps) + 2)
            dve.tensor_tensor(gate_low[:], gT[:], gates[0][:], ALU.subtract).then_inc(chain, 1)
            dve.wait_ge(chain, len(steps) + 3)
            dve.tensor_copy(gates[1][:], gate_low[:])
            dve.wait_ge(S["turn"], 2)
            dve.tensor_copy(picks[0][:], c.ps[LAST + 1][:])


STAGE = 64
STAGES = SEQ // STAGE



def peer_gates(c, name, picks, gates, gate_low, iota, G, tables, stored, last_stored):
    nc = c.nc
    S = {s: c.sem(f"{name}_{s}") for s in ("picked", "made", "low", "low_a", "summed", "staged")}
    PER = 4
    QB = BATCH // PER
    TURNS = 8 // QB
    LOOPS = SEQ // BATCH // TURNS
    with ExitStack() as st:
        def sb(n, shape, dt=F32):
            return st.enter_context(nc.sbuf_tensor(f"{name}_{n}", shape, dt))

        stage = sb("stage", [P, 2, NK, STAGE])
        A = sb("A", [P, TURNS, NK, BATCH], F16)
        E = sb("E", [P, TURNS, NK, BATCH], F16)
        B1 = sb("B1", [P, TURNS, NK, BATCH], F16)
        B2 = sb("B2", [P, TURNS, NK, BATCH], F16)
        block = st.enter_context(nc.Block())
        shape = [P, NK, BATCH]

        def columns(x, b):
            return bc(x[:, bass.ds(b * BATCH, BATCH)].unsqueeze(1), shape)

        @block.vector
        def _(dve):
            def batch(i, r, again):
                b = TURNS * i + r
                if again:
                    dve.wait_ge(S["summed"], (b - TURNS + 1) * QB)
                dve.tensor_tensor(E[:, r], iota[:], columns(picks[1], b), ALU.is_equal).then_inc(S["picked"], 1)
                dve.tensor_tensor(A[:, r], iota[:], columns(picks[0], b), ALU.is_equal)
                dve.wait_ge(S["picked"], b + 1)
                dve.tensor_tensor(B1[:, r], E[:, r], columns(gates[0], b), ALU.mult).then_inc(S["made"], 1)

            for r in range(TURNS):
                batch(0, r, False)
            with dve.Fori(1, LOOPS) as i:
                for r in range(TURNS):
                    batch(i, r, True)

        @block.gpsimd
        def _(pool):
            with pool.Fori(0, LOOPS) as i:
                for r in range(1, TURNS):
                    b = TURNS * i + r
                    pool.wait_ge(S["picked"], b + 1)
                    pool.tensor_tensor(B2[:, r], E[:, r], columns(gates[1], b), ALU.mult).then_inc(S["low"], 1)

        @block.tensor
        def _(pe):
            def batch(i, r, again):
                b = TURNS * i + r
                pe.wait_ge(S["made"], b + 1)
                if r == 0:
                    pe.wait_ge(S["low_a"], i + 1)
                else:
                    pe.wait_ge(S["low"], (TURNS - 1) * i + r)
                for q in range(QB):
                    if again:
                        pe.wait_ge(S["staged"], b * QB + q - 7)
                    for j in range(PER):
                        t = q * PER + j
                        o = c.ps[r * QB + q][:, j * NK:(j + 1) * NK]
                        pe.matmul(o, A[:, r, :, t], B1[:, r, :, t], start=True, stop=False)
                        last = pe.matmul(o, A[:, r, :, t], B2[:, r, :, t], start=False, stop=True)
                    last.then_inc(S["summed"], 1)

            for r in range(TURNS):
                batch(0, r, False)
            with pe.Fori(1, LOOPS) as i:
                for r in range(TURNS):
                    batch(i, r, True)

        @block.scalar
        def _(act):
            def low(i):
                act.wait_ge(S["picked"], TURNS * i + 1)
                for t in range(BATCH):
                    last = act.activation(B2[:, 0, :, t], E[:, 0, :, t], ACT.Copy,
                                          scale=gate_low[:, bass.ds(i * (TURNS * BATCH) + t, 1)])
                last.then_inc(S["low_a"], 1)

            low(0)
            for s in range(STAGES):
                if s >= 2:
                    act.wait_ge(stored[s % 2], 16 * (s // 2))
                for i in range(STAGE // PER // 8):
                    for q in range(8):
                        if q == 2 and not (s == STAGES - 1 and i == STAGE // PER // 8 - 1):
                            low(s * (STAGE // PER // 8) + i + 1)
                        act.wait_ge(S["summed"], s * (STAGE // PER) + 8 * i + q + 1)
                        act.activation(stage[:, s % 2, :, (8 * i + q) * PER:(8 * i + q + 1) * PER],
                                       c.ps[q][:].rearrange("p (t k) -> p k t", t=PER), ACT.Copy,
                                       scale=1.0 / GSCALE).then_inc(S["staged"], 1)

        @block.sync
        def _(sp):
            for r in range(2):
                tables.load_v(sp, 0, r)
                tables.load_u(sp, AHEAD // 2 + r, r)
            for s in range(STAGES - 1):
                sp.wait_ge(S["staged"], (s + 1) * (STAGE // PER))
                sp.dma_start(G[:, s], stage[:, s % 2]).then_inc(stored[s % 2], 16)
            sp.wait_ge(S["staged"], STAGES * (STAGE // PER))
            for i in range(2):
                half = slice(i * NK // 2, (i + 1) * NK // 2)
                sp.dma_start(G[:, STAGES - 1, half], stage[:, 1, half]).then_inc(last_stored[i], 16)
            sp.wait_ge(stored[0], 16 * (STAGES // 2))


def peer_dense(c, name, hi, lo, G, tables, last_stored):
    nc = c.nc
    S = dict(tables.sems)
    S |= {s: c.sem(f"{name}_{s}") for s in (
        "g0", "g1", "w", "w_hi", "w_lo", "v_hi",
        "v_lo", "out", "added")}
    NS = NK
    TURN, ACTB, OUTB = 0, 2, 4
    with ExitStack() as st:
        def sb(n, shape, dt=F32):
            return st.enter_context(nc.sbuf_tensor(f"{name}_{n}", shape, dt))

        u, v = tables.u, tables.v
        g = sb("g", [P, 2, STAGES, 2, STAGE])
        a = sb("a", [P, 2, SEQ])
        w = sb("w", [P, 2, SEQ])
        u_hi, u_lo = sb("u_hi", [P, 2, KD, P], F32R), sb("u_lo", [P, 2, KD, P], F32R)
        w_hi = sb("w_hi", [P, 2, GRP, SEQ], F32R)
        v_lo = sb("v_lo", [P, 2, GRP, 512], F32R)
        w_lo = sb("w_lo", [P, 2, GRP, SEQ], F32R)
        v_hi = sb("v_hi", [P, 2, GRP, 512], F32R)
        block = st.enter_context(nc.Block())

        LOOPS = NS // 8

        def before(i, r, n):
            return isinstance(i, int) and 8 * i + r < n

        def after(i, r, by=1):
            return (i, r + by) if r + by < 8 else (i + 1, r + by - 8)

        @block.sync
        def _(sp):
            def loads(i, r, free, with_u):
                s = 2 * i + r
                if with_u:
                    sp.wait_ge(S["turned"], 4 * s - 4)
                    tables.load_u(sp, s, r)
                if free:
                    sp.wait_ge(S["w"], 2 * s - 2)
                sp.dma_start(g[:, r], G[:, :, bass.ds(s * 2, 2), :]).then_inc(S[f"g{r}"], 16)
                if free:
                    sp.wait_ge(S["v_hi"], 2 * s - 2)
                    sp.wait_ge(S["v_lo"], 2 * s - 2)
                    tables.load_v(sp, i, r)

            sp.wait_ge(last_stored[0], 16)
            for i in range(3):
                for r in range(2):
                    loads(i, r, i > 0, False)
            sp.wait_ge(last_stored[1], 16)
            with sp.Fori(3, NS // GRP) as i:
                for r in range(2):
                    loads(i, r, True, True)

        @block.tensor
        def _(pe):
            def turn(i, r):
                if r % 2 == 0:
                    pe.wait_ge(tables.u_loaded[r // 2 % 2], 16 * (2 * i + r // 4 + 1))
                for b in range(2):
                    for k in range(4):
                        last = pe.transpose(c.ps[TURN + b][:, k * P:(k + 1) * P],
                                            u[:, r // 2 % 2, r % 2, (4 * b + k) * P:(4 * b + k + 1) * P], c.ident[:])
                    last.then_inc(S["turned"], 1)

            def activations(i, r):
                if not before(i, r, 2):
                    pe.wait_ge(S["gelu"], 8 * i + r - 1)
                o = c.ps[ACTB + r % 2]
                for k in range(KD):
                    uh, ul = u_hi[:, r % 2, k, :], u_lo[:, r % 2, k, :]
                    pe.matmul(o[:], uh, hi[:, k, :], start=(k == 0), stop=False)
                    pe.matmul(o[:], uh, lo[:, k, :], start=False, stop=False)
                    last = pe.matmul(o[:], ul, hi[:, k, :], start=False, stop=(k == KD - 1))
                last.then_inc(S["act"], 1)

            def outputs(i, r):
                n = 8 * i + r
                q2, grp2 = r // 2 % 2, (r // 4 + 1) % 2
                if r % 4 == 0:
                    pe.wait_ge(S["w_hi"], n)
                    pe.wait_ge(S["w_lo"], n)
                if r % 2 == 0:
                    pe.wait_ge(S["v_hi"], n - 2)
                    pe.wait_ge(S["v_lo"], n - 2)
                for m in range(2):
                    t = 2 * (r % 2) + m
                    b = c.ps[OUTB + t]
                    if not before(i, r, GRP + 2):
                        pe.wait_ge(S["added"], 2 * n + m - 2 * GRP - 3)
                    for j in range(GRP):
                        wh, wl = w_hi[:, grp2, j, t * P:(t + 1) * P], w_lo[:, grp2, j, t * P:(t + 1) * P]
                        pe.matmul(b[:], wh, v_hi[:, q2, j, :], start=(j == 0), stop=False)
                        pe.matmul(b[:], wh, v_lo[:, q2, j, :], start=False, stop=False)
                        last = pe.matmul(b[:], wl, v_hi[:, q2, j, :], start=False, stop=(j == GRP - 1))
                    last.then_inc(S["out"], 1)

            def first_half(i, r, turn_next=True):
                pe.wait_ge(S["u_hi"], 2 * (8 * i + r) + 2)
                pe.wait_ge(S["u_lo"], 2 * (8 * i + r) + 2)
                if turn_next:
                    turn(*after(i, r))
                activations(i, r)

            def step(i, r, turn_next=True):
                first_half(i, r, turn_next)
                outputs(i, r)

            turn(1, 0)
            for r in range(2):
                first_half(1, r)
            for r in range(GRP, AHEAD):
                outputs(0, r)
            for r in range(2):
                outputs(1, r)
            for r in range(2, 8):
                step(1, r)
            with pe.Fori(2, LOOPS - 1) as i:
                for r in range(8):
                    step(i, r)
            for r in range(8):
                step(LOOPS - 1, r, turn_next=(r < 7))
            for r in range(GRP):
                outputs(LOOPS, r)

        @block.scalar
        def _(act):
            def split_u(i, r):
                n = 8 * i + r
                if not before(i, r, 2):
                    act.wait_ge(S["act"], n - 1)
                for b in range(2):
                    act.wait_ge(S["turned"], 2 * n + b + 1)
                    act.activation(u_hi[:, r % 2, 4 * b:4 * b + 4, :].rearrange("p k i -> p (k i)"),
                                   c.ps[TURN + b][:], ACT.Copy).then_inc(S["u_hi"], 1)

            def split_v(i, r):
                s2 = r // 2 % 2
                if r % 2 == 0:
                    act.wait_ge(tables.v_loaded[s2], 16 * (2 * i + r // 4 + 1))
                    if not before(i, r, 4):
                        act.wait_ge(S["out"], 2 * (8 * i + r) - 4)
                j = 2 * (r % 2)
                act.activation(v_hi[:, s2, j:j + 2, :], v[:, s2, j:j + 2, :], ACT.Copy).then_inc(S["v_hi"], 1)

            def step(i, r, split_next=True):
                n = 8 * i + r
                if split_next:
                    split_u(*after(i, r))
                if not before(i, r, 2):
                    split_v(i, r - 2) if r >= 2 else split_v(i - 1, r + 6)
                if not before(i, r, AHEAD):
                    act.wait_ge(S["act"], n + 1)
                    act.wait_ge(S["w"], n - 1)
                    act.activation(a[:, r % 2, :], c.ps[ACTB + r % 2][:], ACT.Gelu).then_inc(S["gelu"], 1)
                act.wait_ge(S["w"], n + 1)
                if r % 4 == 0 and not before(i, r, 8):
                    act.wait_ge(S["out"], 2 * n - 8)
                act.activation(w_hi[:, r // 4, r % 4, :], w[:, r % 2, :], ACT.Copy).then_inc(S["w_hi"], 1)

            for r in range(2):
                split_u(1, r)
            for r in range(AHEAD):
                step(0, r, split_next=False)
            for r in range(8):
                step(1, r, split_next=(r > 0))
            with act.Fori(2, LOOPS - 1) as i:
                for r in range(8):
                    step(i, r)
            for r in range(8):
                step(LOOPS - 1, r, split_next=(r < 7))
            for r in range(6, 8):
                split_v(LOOPS - 1, r)

        @block.gpsimd
        def _(pool):
            pool.wait_ge(last_stored[1], 16)
            with pool.Fori(0, LOOPS) as i:
                for r in range(8):
                    s2, j = r // 2 % 2, 2 * (r % 2)
                    pool.wait_ge(S["v_hi"], 8 * i + r + 1)
                    pool.tensor_tensor(v_lo[:, s2, j:j + 2, :], v[:, s2, j:j + 2, :],
                                       v_hi[:, s2, j:j + 2, :].bitcast(F32), ALU.subtract).then_inc(S["v_lo"], 1)

        @block.vector
        def _(dve):
            def split_u(i, r):
                for b in range(2):
                    dve.wait_ge(S["u_hi"], 2 * (8 * i + r) + b + 1)
                    part = slice(4 * b, 4 * b + 4)
                    dve.tensor_tensor(u_lo[:, r % 2, part, :].rearrange("p k i -> p (k i)"), c.ps[TURN + b][:],
                                      u_hi[:, r % 2, part, :].rearrange("p k i -> p (k i)").bitcast(F32),
                                      ALU.subtract).then_inc(S["u_lo"], 1)

            def weigh(i, r):
                n = 8 * i + r
                dve.wait_ge(S["gelu"], n + 1)
                if r % 2 == 0:
                    dve.wait_ge(S[f"g{r // 2 % 2}"], 16 * (2 * i + r // 4 + 1))
                if not before(i, r, 2):
                    dve.wait_ge(S["w_lo"], n - 1)
                x = tables.ahead[:, r, :] if before(i, r, AHEAD) else a[:, r % 2, :]
                dve.tensor_tensor(w[:, r % 2, :].rearrange("p (s t) -> p s t", s=STAGES),
                                  x.rearrange("p (s t) -> p s t", s=STAGES),
                                  g[:, r // 2 % 2, :, r % 2, :], ALU.mult).then_inc(S["w"], 1)
                dve.wait_ge(S["w_hi"], n + 1)
                dve.tensor_tensor(w_lo[:, r // 4, r % 4, :], w[:, r % 2, :],
                                  w_hi[:, r // 4, r % 4, :].bitcast(F32), ALU.subtract).then_inc(S["w_lo"], 1)

            def add_out(i, r):
                n = 8 * i + r
                for m in range(2):
                    t = 2 * (r % 2) + m
                    dve.wait_ge(S["out"], 2 * n + m - 2 * GRP + 1)
                    if not before(i, r, 2 * GRP):
                        dve.wait_ge(S["added"], 2 * n + m - 2 * GRP - 7)
                    o = c.h[:, t, r // 2 % 2 * 512:(r // 2 % 2 + 1) * 512]
                    dve.tensor_tensor(o, c.ps[OUTB + t][:], o, ALU.add).then_inc(S["added"], 1)

            def step(i, r, split_next=True):
                if split_next:
                    split_u(*after(i, r))
                weigh(i, r)
                if not before(i, r, GRP):
                    add_out(i, r)

            for r in range(2):
                split_u(1, r)
            for r in range(AHEAD):
                step(0, r, split_next=False)
            for r in range(8):
                step(1, r, split_next=(r > 0))
            with dve.Fori(2, LOOPS - 1) as i:
                for r in range(8):
                    step(i, r)
            for r in range(8):
                step(LOOPS - 1, r, split_next=(r < 7))
            for r in range(GRP):
                add_out(LOOPS, r)


def final_norm(c, gain, out):
    nc = c.nc
    gain_loaded, squares, scale, normed, stored = (
        c.sem(f"final_{s}") for s in ("gain", "squares", "scale", "normed", "stored"))
    with ExitStack() as st:
        g = st.enter_context(nc.sbuf_tensor("final_gain", [P, D], F32))
        o = st.enter_context(nc.sbuf_tensor("final_o", [P, TT, D], F32))
        ss = st.enter_context(nc.sbuf_tensor("final_ss", [P, TT], F32))
        ms = st.enter_context(nc.sbuf_tensor("final_ms", [P, TT], F32))
        std = st.enter_context(nc.sbuf_tensor("final_std", [P, TT], F32))
        r = st.enter_context(nc.sbuf_tensor("final_r", [P, TT], F32))
        block = st.enter_context(nc.Block())

        @block.sync
        def _(sp):
            sp.dma_start(g[:], gain.partition_broadcast(P)).then_inc(gain_loaded, 16)
            for t in range(TT):
                sp.wait_ge(normed, t + 1)
                sp.dma_start(out[0, t * P:(t + 1) * P, :], o[:, t, :]).then_inc(stored, 16)
            sp.wait_ge(stored, 16 * TT)

        @block.scalar
        def _(act):
            for t in range(TT):
                act.activation(o[:, t, :], c.h[:, t, :], ACT.Square, accum_out=ss[:, t:t + 1]).then_inc(squares, 1)
            act.wait_ge(scale, 1)
            act.activation(std[:], ms[:], ACT.Sqrt).then_inc(squares, 1)

        @block.vector
        def _(dve):
            dve.wait_ge(squares, TT)
            dve.tensor_scalar(ms[:], ss[:], 1.0 / D, EPS, ALU.mult, ALU.add).then_inc(scale, 1)
            dve.wait_ge(squares, TT + 1)
            dve.reciprocal(r[:], std[:]).then_inc(scale, 1)
            dve.wait_ge(scale, 2)
            dve.wait_ge(gain_loaded, 16)
            for t in range(TT):
                dve.scalar_tensor_tensor(o[:, t, :], c.h[:, t, :], r[:, t:t + 1], g[:], ALU.mult,
                                         ALU.mult).then_inc(normed, 1)


def peer(c, name, gain, w_q, sub_keys, u_tab, v_tab, G):
    nc = c.nc
    with ExitStack() as st:
        def sb(n, shape, dt=F32):
            return st.enter_context(nc.sbuf_tensor(f"{name}_{n}", shape, dt))
        hi, lo = sb("hn_hi", [P, KD, SEQ], F32R), sb("hn_lo", [P, KD, SEQ], F32R)
        with ExitStack() as st2:
            picks = [st2.enter_context(nc.sbuf_tensor(f"{name}_picks{i}", [P, SEQ], F16)) for i in range(2)]
            gates = [st2.enter_context(nc.sbuf_tensor(f"{name}_gates{i}", [P, SEQ], F16)) for i in range(2)]
            gate_low = st2.enter_context(nc.sbuf_tensor(f"{name}_gate_low", [P, SEQ], F32))
            iota = st2.enter_context(nc.sbuf_tensor(f"{name}_iota", [P, NK, BATCH], F16))
            tables = Experts(c, name, st2, u_tab, v_tab)
            with ExitStack() as st3:
                W = PickInputs(c, name, st3, w_q, sub_keys, tables)
                norm_block(c, f"{name}_norm", gain, hi, lo, W.first_loads)
                peer_pick(c, f"{name}_pick", hi, lo, W, tables, picks, gates, gate_low, iota)
            tables.make_v(c, name, st2)
            stored = [c.sem(f"{name}_stored{i}") for i in range(2)]
            last_stored = [c.sem(f"{name}_last_stored{i}") for i in range(2)]
            peer_gates(c, f"{name}_gate", picks, gates, gate_low, iota, G, tables, stored, last_stored)
            peer_dense(c, f"{name}_dense", hi, lo, G, tables, last_stored)


def trunk(nc, A, out, stages=("even", "peer0", "odd", "peer1", "final")):
    ctx = ExitStack()
    with ctx:
        c = Core(nc, ctx)
        G = nc.dram_tensor("gate_matrix", (P, STAGES, NK, STAGE), F32).ap()
        constants(c, A["x"])
        for s in stages:
            if s == "even":
                even_layer(c, A)
            if s == "odd":
                odd_layer(c, A)
            if s[:4] == "peer":
                i = int(s[4])
                peer(c, s, A["ffn_norm_g"][i], A["peer_w_q"][i], A["peer_sub_keys"][i], A["peer_u"][i],
                     A["peer_v"][i], G)
            if s == "final":
                final_norm(c, A["final_g"], out)
            c.end_layer()


_INS = ["x", "even_norm_g", "even_w_in", "even_b_f", "even_cmp_pos", "even_w_cmp_k", "even_w_cmp_v", "even_w_out",
        "odd_norm_g", "odd_w_in", "odd_conv_w", "odd_conv_b", "odd_w_ra", "odd_b_ra", "odd_w_ri", "odd_b_ri",
        "odd_lam", "odd_w_out", "ffn_norm_g", "peer_w_q", "peer_sub_keys", "peer_u", "peer_v", "final_g"]


def kernel(**inputs):
    import numpy as _np
    import concourse.bacc as _bacc
    from concourse import mybir as _mybir
    from concourse.bass_utils import run_bass_kernel_spmd as _run

    nc = _bacc.Bacc("TRN2", target_bir_lowering=False, num_devices=1)
    arrays, args = {}, {}
    for name in _INS:
        a = _np.ascontiguousarray(inputs[name])
        arrays[f"in_{name}_dram"] = a
        args[name] = nc.dram_tensor(f"in_{name}_dram", a.shape, _mybir.dt.from_np(a.dtype), kind="ExternalInput").ap()
    out = nc.dram_tensor("out_0_dram", (1, SEQ, D), F32, kind="ExternalOutput").ap()
    trunk(nc, args, out)
    r = _run(nc, [arrays], core_ids=[0])
    return r.results[0]["out_0_dram"]
```
